# Optimizing a Trainium2 kernel written in Bass

```python
import math
import jax
import jax.numpy as jnp
from jax import lax
import numpy as np

D_MODEL = 1024
BATCH = 1
SEQ = 1024
DEPTH = 2
DEC_BATCH = 8
DEC_SEQ = 1
PAST_LEN = 2048
PAGE_SIZE = 128

N_MEM = 256
MEM_HEADS = 4
MEM_HD = D_MODEL // MEM_HEADS
FOX_HEADS = 8
FOX_HD = 64
FOX_WIDTH = FOX_HEADS * FOX_HD
Q_BLOCK = 128
POOL_WINDOWS = (2, 4, 8, 16)
POOL_GROUPS = len(POOL_WINDOWS)
POOL_WIDTH = D_MODEL // 2
POOL_GC = POOL_WIDTH // POOL_GROUPS
POOL_BUF = max(POOL_WINDOWS) - 1
SSM_HEADS = 16
SSM_HD = 64
SSM_INNER = SSM_HEADS * SSM_HD
SSM_GROUPS = 2
SSM_STATE = 128
CONV_W = 4
SSM_CHUNK = 128
CONV_CH = SSM_INNER + 2 * SSM_GROUPS * SSM_STATE
GMLP_WIDTH = D_MODEL // 2
GMLP_GROUPS = 4
GMLP_GC = GMLP_WIDTH // GMLP_GROUPS
GMLP_CHUNK = 128
D_FF = -(-8 * D_MODEL // (3 * 256)) * 256
ALPHA = (2 * DEPTH) ** 0.25
BETA = (8 * DEPTH) ** -0.25
LN_EPS = 1e-5
N_AB = (DEPTH + 1) // 2
N_CD = DEPTH // 2
AB_IN = 3 * FOX_WIDTH + FOX_HEADS + POOL_WIDTH
AB_OUT = FOX_WIDTH + POOL_WIDTH
CD_IN = SSM_INNER + CONV_CH + SSM_HEADS + 2 * GMLP_WIDTH
CD_OUT = SSM_INNER + GMLP_WIDTH

kernel_name = 'hybrid_fox_pool_ssd_gmlp_step'

def _ln(x, g, b):
    xf = x.astype(jnp.float32)
    mu = jnp.mean(xf, axis=-1, keepdims=True)
    var = jnp.mean(jnp.square(xf - mu), axis=-1, keepdims=True)
    return ((xf - mu) * lax.rsqrt(var + LN_EPS) * g.astype(jnp.float32) + b.astype(jnp.float32)).astype(x.dtype)

def _rmsnorm(x, w):
    xf = x.astype(jnp.float32)
    return xf * lax.rsqrt(jnp.mean(jnp.square(xf), axis=-1, keepdims=True) + LN_EPS) * w.astype(jnp.float32)

def _post(x, sub, g, b):
    return _ln(ALPHA * x + sub, g, b)

def _swiglu(x, wg, wu, wd):
    return (jax.nn.silu(x @ wg) * (x @ wu)) @ wd

def _mem_kv(mem, wk, wv):
    b, m, _ = mem.shape
    return (mem @ wk).reshape(b, m, MEM_HEADS, MEM_HD), (mem @ wv).reshape(b, m, MEM_HEADS, MEM_HD)

def _cross_attn(x, mk, mv, wq, wo):
    b, l, _ = x.shape
    q = (x @ wq).reshape(b, l, MEM_HEADS, MEM_HD)
    s = jnp.einsum('bqhd,bkhd->bhqk', q, mk).astype(jnp.float32) * (MEM_HD ** -0.5)
    p = jax.nn.softmax(s, axis=-1).astype(mv.dtype)
    o = jnp.einsum('bhqk,bkhd->bqhd', p, mv).reshape(b, l, MEM_HEADS * MEM_HD)
    return o @ wo

def _ab_project(x, w_in, b_forget):
    b, l, _ = x.shape
    proj = x @ w_in
    q, k, v, fl, u = jnp.split(proj, [FOX_WIDTH, 2 * FOX_WIDTH, 3 * FOX_WIDTH, 3 * FOX_WIDTH + FOX_HEADS], axis=-1)
    logf = jax.nn.log_sigmoid(fl.astype(jnp.float32) + b_forget.astype(jnp.float32))
    shp = (b, l, FOX_HEADS, FOX_HD)
    return q.reshape(shp), k.reshape(shp), v.reshape(shp), logf, u

def _fox_prompt(q, k, v, logf):
    b, s, h, d = q.shape
    nb = s // Q_BLOCK
    c = jnp.cumsum(logf.astype(jnp.float32), axis=1).transpose(0, 2, 1)
    qb = q.reshape(b, nb, Q_BLOCK, h, d).transpose(1, 0, 2, 3, 4)
    cb = c.reshape(b, h, nb, Q_BLOCK).transpose(2, 0, 1, 3)
    kpos = jnp.arange(s)
    scale = FOX_HD ** -0.5

    def block(args):
        i, qi, ci = args
        sc = jnp.einsum('bqhd,bkhd->bhqk', qi, k).astype(jnp.float32) * scale
        sc = sc + ci[..., :, None] - c[:, :, None, :]
        qpos = i * Q_BLOCK + jnp.arange(Q_BLOCK)
        sc = jnp.where(kpos[None, :] <= qpos[:, None], sc, -jnp.inf)
        p = jax.nn.softmax(sc, axis=-1).astype(v.dtype)
        return jnp.einsum('bhqk,bkhd->bqhd', p, v)

    out = lax.map(block, (jnp.arange(nb), qb, cb))
    return out.transpose(1, 0, 2, 3, 4).reshape(b, s, h * d)

def _fox_sample(q, k_new, v_new, logf_new, k_pool, v_pool, lf_pool, page_table):
    b, l, h, d = q.shape
    past = page_table.shape[1] * k_pool.shape[1]
    k_all = jnp.concatenate([k_pool[page_table].reshape(b, past, h, d).astype(k_new.dtype), k_new], axis=1)
    v_all = jnp.concatenate([v_pool[page_table].reshape(b, past, h, d).astype(v_new.dtype), v_new], axis=1)
    lf_all = jnp.concatenate([lf_pool[page_table].reshape(b, past, h).astype(jnp.float32),
                              logf_new.astype(jnp.float32)], axis=1)
    c = jnp.cumsum(lf_all, axis=1).transpose(0, 2, 1)
    sc = jnp.einsum('bqhd,bkhd->bhqk', q, k_all).astype(jnp.float32) * (FOX_HD ** -0.5)
    sc = sc + c[:, :, past:, None] - c[:, :, None, :]
    qpos = past + jnp.arange(l)
    kpos = jnp.arange(past + l)
    sc = jnp.where(kpos[None, :] <= qpos[:, None], sc, -jnp.inf)
    p = jax.nn.softmax(sc, axis=-1).astype(v_all.dtype)
    return jnp.einsum('bhqk,bkhd->bqhd', p, v_all).reshape(b, l, h * d)

def _pool_mixer(u, prefix, start, w_pool, pool_scale):
    b, l, ch = u.shape
    ext = jnp.concatenate([prefix.astype(u.dtype), u], axis=1)
    cs = jnp.cumsum(ext.astype(jnp.float32), axis=1)
    cs = jnp.concatenate([jnp.zeros((b, 1, ch), jnp.float32), cs], axis=1)
    hi = cs[:, POOL_BUF + 1:]
    pos = start + jnp.arange(l)
    uf = u.astype(jnp.float32)
    outs = []
    for g, w in enumerate(POOL_WINDOWS):
        sl = slice(g * POOL_GC, (g + 1) * POOL_GC)
        lo = cs[:, POOL_BUF + 1 - w:POOL_BUF + 1 - w + l, sl]
        cnt = jnp.minimum(pos + 1, w).astype(jnp.float32)[None, :, None]
        outs.append((hi[..., sl] - lo) / cnt - uf[..., sl])
    dlt = jnp.stack(outs, axis=2).astype(u.dtype)
    y = jnp.einsum('blgc,gce->blge', dlt, w_pool).reshape(b, l, ch) * pool_scale
    return y, ext[:, -POOL_BUF:]

def _causal_conv(xbc, prefix, w, bias):
    ext = jnp.concatenate([prefix.astype(xbc.dtype), xbc], axis=1)
    y = lax.conv_general_dilated(ext, w[:, None, :].astype(ext.dtype), (1,), 'VALID',
                                 dimension_numbers=('NWC', 'WIO', 'NWC'),
                                 feature_group_count=ext.shape[-1])
    return y + bias, ext[:, -(CONV_W - 1):]

def _ssd(xdt, da, bm, cm, h0):
    b, l, nh, hp = xdt.shape
    ng, ns = bm.shape[2], bm.shape[3]
    nr = nh // ng
    lc = min(SSM_CHUNK, l)
    nc = -(-l // lc)
    pad = nc * lc - l
    f32 = jnp.float32
    if pad:
        def padf(a):
            return jnp.pad(a, [(0, 0), (0, pad)] + [(0, 0)] * (a.ndim - 2))
        xdt, da, bm, cm = padf(xdt), padf(da), padf(bm), padf(cm)
    xc = xdt.astype(f32).reshape(b, nc, lc, ng, nr, hp)
    ac = da.astype(f32).reshape(b, nc, lc, ng, nr)
    bc = bm.astype(f32).reshape(b, nc, lc, ng, ns)
    cc = cm.astype(f32).reshape(b, nc, lc, ng, ns)
    acs = jnp.cumsum(ac, axis=2)
    causal = jnp.tril(jnp.ones((lc, lc), bool))[None, None, :, :, None, None]
    seg = jnp.exp(jnp.where(causal, acs[:, :, :, None] - acs[:, :, None, :], -jnp.inf))
    cb = jnp.einsum('bctgn,bcsgn->bctsg', cc, bc)
    y_diag = jnp.einsum('bctsg,bctsgr,bcsgrp->bctgrp', cb, seg, xc)
    decay_to_end = jnp.exp(acs[:, :, -1:] - acs)
    chunk_states = jnp.einsum('bclgn,bclgr,bclgrp->bcgrpn', bc, decay_to_end, xc)
    chunk_decay = jnp.exp(acs[:, :, -1])

    def step(h, inp):
        s_c, a_c = inp
        return h * a_c[..., None, None] + s_c, h

    h_last, h_prev = lax.scan(step, h0.astype(f32).reshape(b, ng, nr, hp, ns),
                              (jnp.moveaxis(chunk_states, 1, 0), jnp.moveaxis(chunk_decay, 1, 0)))
    h_prev = jnp.moveaxis(h_prev, 0, 1)
    y_off = jnp.einsum('bclgn,bcgrpn,bclgr->bclgrp', cc, h_prev, jnp.exp(acs))
    y = (y_diag + y_off).reshape(b, nc * lc, nh, hp)[:, :l]
    return y, h_last.reshape(b, nh, hp, ns)

def _cd_mixer(x, conv_prefix, h0, w_in, conv_w, conv_b, dt_bias, a_log, d_skip, norm_w,
              ln_g, ln_b, w_sp, b_sp, w_out):
    b, l, _ = x.shape
    proj = x @ w_in
    o1 = SSM_INNER
    o2 = o1 + CONV_CH
    o3 = o2 + SSM_HEADS
    o4 = o3 + GMLP_WIDTH
    z, xbc, dt_raw, gu, gv = jnp.split(proj, [o1, o2, o3, o4], axis=-1)
    xbc, conv_state = _causal_conv(xbc, conv_prefix, conv_w, conv_b)
    xbc = jax.nn.silu(xbc)
    xs, bm, cm = jnp.split(xbc, [SSM_INNER, SSM_INNER + SSM_GROUPS * SSM_STATE], axis=-1)
    xs = xs.reshape(b, l, SSM_HEADS, SSM_HD)
    bm = bm.reshape(b, l, SSM_GROUPS, SSM_STATE)
    cm = cm.reshape(b, l, SSM_GROUPS, SSM_STATE)
    dt = jax.nn.softplus(dt_raw.astype(jnp.float32) + dt_bias.astype(jnp.float32))
    da = dt * (-jnp.exp(a_log.astype(jnp.float32)))
    y, h_last = _ssd(xs.astype(jnp.float32) * dt[..., None], da, bm, cm, h0)
    y = y + d_skip.astype(jnp.float32)[:, None] * xs.astype(jnp.float32)
    y = _rmsnorm(y.reshape(b, l, SSM_INNER) * jax.nn.silu(z.astype(jnp.float32)), norm_w).astype(x.dtype)
    u = jax.nn.gelu(gu)
    v = _ln(jax.nn.gelu(gv), ln_g, ln_b)
    lc = min(GMLP_CHUNK, l)
    nch = l // lc
    wm = w_sp[:, :lc, :lc] * jnp.tril(jnp.ones((lc, lc), w_sp.dtype))
    vc = v.reshape(b, nch, lc, GMLP_GROUPS, GMLP_GC)
    sg = jnp.einsum('gts,bnsgc->bntgc', wm, vc) + b_sp[:, :lc].T[None, None, :, :, None]
    yd = (u * sg.reshape(b, l, GMLP_WIDTH)).astype(x.dtype)
    out = jnp.concatenate([y, yd], axis=-1) @ w_out
    return out, conv_state, h_last, v

def setup_inputs(seed: int = 0) -> dict:
    key = jax.random.key(seed)
    keys = jax.random.split(key, 64)
    counter = [0]

    def nk():
        counter[0] += 1
        return keys[counter[0] - 1]

    f32 = jnp.float32
    n_pages = PAST_LEN // PAGE_SIZE
    n_used = DEC_BATCH * n_pages
    n_phys = n_used + (n_used + 3) // 4

    def w(shape, fan_in, gain=1.0):
        return jax.random.normal(nk(), shape, f32) * (gain * fan_in ** -0.5)

    def gain(shape):
        return 1.0 + 0.02 * jax.random.normal(nk(), shape, f32)

    def small(shape, s=0.02):
        return s * jax.random.normal(nk(), shape, f32)

    inp = {}
    inp['x_prompt'] = jax.random.normal(nk(), (BATCH, SEQ, D_MODEL), f32)
    inp['x_sample'] = jax.random.normal(nk(), (DEC_BATCH, DEC_SEQ, D_MODEL), f32)
    inp['cache_fox_k'] = jax.random.normal(nk(), (N_AB, n_phys, PAGE_SIZE, FOX_HEADS, FOX_HD), f32)
    inp['cache_fox_v'] = jax.random.normal(nk(), (N_AB, n_phys, PAGE_SIZE, FOX_HEADS, FOX_HD), f32)
    inp['cache_fox_logf'] = jax.nn.log_sigmoid(
        jax.random.normal(nk(), (N_AB, n_phys, PAGE_SIZE, FOX_HEADS), f32) + 4.0)
    inp['state_pool'] = jax.random.normal(nk(), (N_AB, DEC_BATCH, POOL_BUF, POOL_WIDTH), f32)
    inp['state_conv'] = jax.random.normal(nk(), (N_CD, DEC_BATCH, CONV_W - 1, CONV_CH), f32)
    inp['state_ssm'] = 0.1 * jax.random.normal(nk(), (N_CD, DEC_BATCH, SSM_HEADS, SSM_HD, SSM_STATE), f32)
    inp['cache_mem_k'] = jax.random.normal(nk(), (DEPTH, DEC_BATCH, N_MEM, MEM_HEADS, MEM_HD), f32)
    inp['cache_mem_v'] = jax.random.normal(nk(), (DEPTH, DEC_BATCH, N_MEM, MEM_HEADS, MEM_HD), f32)
    inp['page_table'] = jax.random.permutation(nk(), n_phys)[:n_used].reshape(DEC_BATCH, n_pages).astype(jnp.int32)
    inp['mem_prompt'] = jax.random.normal(nk(), (BATCH, N_MEM, D_MODEL), f32)
    inp['w_in_ab'] = w((N_AB, D_MODEL, AB_IN), D_MODEL)
    inp['b_forget'] = jax.random.uniform(nk(), (N_AB, FOX_HEADS), f32, 1.0, 6.0)
    inp['w_pool'] = w((N_AB, POOL_GROUPS, POOL_GC, POOL_GC), POOL_GC)
    inp['pool_scale'] = 1.0 + 0.1 * jax.random.normal(nk(), (N_AB, POOL_WIDTH), f32)
    inp['w_out_ab'] = w((N_AB, AB_OUT, D_MODEL), AB_OUT, BETA)
    inp['w_in_cd'] = w((N_CD, D_MODEL, CD_IN), D_MODEL)
    inp['conv_w'] = w((N_CD, CONV_W, CONV_CH), CONV_W)
    inp['conv_b'] = small((N_CD, CONV_CH))
    dt0 = jnp.exp(jax.random.uniform(nk(), (N_CD, SSM_HEADS), f32, math.log(1e-3), math.log(1e-1)))
    inp['dt_bias'] = dt0 + jnp.log(-jnp.expm1(-dt0))
    inp['a_log'] = jnp.log(jax.random.uniform(nk(), (N_CD, SSM_HEADS), f32, 1.0, 16.0))
    inp['d_skip'] = 1.0 + 0.1 * jax.random.normal(nk(), (N_CD, SSM_HEADS), f32)
    inp['ssm_norm_w'] = gain((N_CD, SSM_INNER))
    inp['gmlp_ln_g'] = gain((N_CD, GMLP_WIDTH))
    inp['gmlp_ln_b'] = small((N_CD, GMLP_WIDTH))
    inp['w_spatial'] = w((N_CD, GMLP_GROUPS, GMLP_CHUNK, GMLP_CHUNK), GMLP_CHUNK)
    inp['b_spatial'] = 1.0 + 0.1 * jax.random.normal(nk(), (N_CD, GMLP_GROUPS, GMLP_CHUNK), f32)
    inp['w_out_cd'] = w((N_CD, CD_OUT, D_MODEL), CD_OUT, BETA)
    inp['ln_mix_g'] = gain((DEPTH, D_MODEL))
    inp['ln_mix_b'] = small((DEPTH, D_MODEL))
    inp['w_xq'] = w((DEPTH, D_MODEL, D_MODEL), D_MODEL)
    inp['w_xk'] = w((DEPTH, D_MODEL, D_MODEL), D_MODEL)
    inp['w_xv'] = w((DEPTH, D_MODEL, D_MODEL), D_MODEL)
    inp['w_xo'] = w((DEPTH, D_MODEL, D_MODEL), D_MODEL, BETA)
    inp['ln_x_g'] = gain((DEPTH, D_MODEL))
    inp['ln_x_b'] = small((DEPTH, D_MODEL))
    inp['w_gate'] = w((DEPTH, D_MODEL, D_FF), D_MODEL)
    inp['w_up'] = w((DEPTH, D_MODEL, D_FF), D_MODEL)
    inp['w_down'] = w((DEPTH, D_FF, D_MODEL), D_FF, BETA)
    inp['ln_ff_g'] = gain((DEPTH, D_MODEL))
    inp['ln_ff_b'] = small((DEPTH, D_MODEL))
    return inp

def reference(x_prompt, x_sample, cache_fox_k, cache_fox_v, cache_fox_logf, state_pool, state_conv,
              state_ssm, cache_mem_k, cache_mem_v, page_table, mem_prompt,
              w_in_ab, b_forget, w_pool, pool_scale, w_out_ab,
              w_in_cd, conv_w, conv_b, dt_bias, a_log, d_skip, ssm_norm_w, gmlp_ln_g, gmlp_ln_b,
              w_spatial, b_spatial, w_out_cd,
              ln_mix_g, ln_mix_b, w_xq, w_xk, w_xv, w_xo, ln_x_g, ln_x_b,
              w_gate, w_up, w_down, ln_ff_g, ln_ff_b):
    yp, ys = x_prompt, x_sample
    bp = x_prompt.shape[0]
    fkp, fvp, flp, fks, fvs, fls = [], [], [], [], [], []
    pps, pss = [], []
    cps, css, hps, hss, gvs = [], [], [], [], []
    mkp, mvp = [], []
    for i in range(DEPTH):
        j = i // 2
        if i % 2 == 0:
            q, k, v, lf, u = _ab_project(yp, w_in_ab[j], b_forget[j])
            att = _fox_prompt(q, k, v, lf)
            pool, pst = _pool_mixer(u, jnp.zeros((bp, POOL_BUF, POOL_WIDTH), u.dtype), 0, w_pool[j], pool_scale[j])
            mix_p = jnp.concatenate([att, pool.astype(att.dtype)], axis=-1) @ w_out_ab[j]
            fkp.append(k)
            fvp.append(v)
            flp.append(lf)
            pps.append(pst)
            q, k, v, lf, u = _ab_project(ys, w_in_ab[j], b_forget[j])
            att = _fox_sample(q, k, v, lf, cache_fox_k[j], cache_fox_v[j], cache_fox_logf[j], page_table)
            pool, pst = _pool_mixer(u, state_pool[j], PAST_LEN, w_pool[j], pool_scale[j])
            mix_s = jnp.concatenate([att, pool.astype(att.dtype)], axis=-1) @ w_out_ab[j]
            fks.append(k)
            fvs.append(v)
            fls.append(lf)
            pss.append(pst)
        else:
            mix_p, cst, hst, _ = _cd_mixer(
                yp, jnp.zeros((bp, CONV_W - 1, CONV_CH), yp.dtype),
                jnp.zeros((bp, SSM_HEADS, SSM_HD, SSM_STATE), jnp.float32),
                w_in_cd[j], conv_w[j], conv_b[j], dt_bias[j], a_log[j], d_skip[j], ssm_norm_w[j],
                gmlp_ln_g[j], gmlp_ln_b[j], w_spatial[j], b_spatial[j], w_out_cd[j])
            cps.append(cst)
            hps.append(hst)
            mix_s, cst, hst, gv = _cd_mixer(
                ys, state_conv[j], state_ssm[j],
                w_in_cd[j], conv_w[j], conv_b[j], dt_bias[j], a_log[j], d_skip[j], ssm_norm_w[j],
                gmlp_ln_g[j], gmlp_ln_b[j], w_spatial[j], b_spatial[j], w_out_cd[j])
            css.append(cst)
            hss.append(hst)
            gvs.append(gv)
        yp = _post(yp, mix_p, ln_mix_g[i], ln_mix_b[i])
        ys = _post(ys, mix_s, ln_mix_g[i], ln_mix_b[i])
        mk, mv = _mem_kv(mem_prompt, w_xk[i], w_xv[i])
        mkp.append(mk)
        mvp.append(mv)
        yp = _post(yp, _cross_attn(yp, mk, mv, w_xq[i], w_xo[i]), ln_x_g[i], ln_x_b[i])
        ys = _post(ys, _cross_attn(ys, cache_mem_k[i], cache_mem_v[i], w_xq[i], w_xo[i]), ln_x_g[i], ln_x_b[i])
        yp = _post(yp, _swiglu(yp, w_gate[i], w_up[i], w_down[i]), ln_ff_g[i], ln_ff_b[i])
        ys = _post(ys, _swiglu(ys, w_gate[i], w_up[i], w_down[i]), ln_ff_g[i], ln_ff_b[i])
    return (yp, ys,
            jnp.stack(fkp), jnp.stack(fvp), jnp.stack(flp),
            jnp.stack(fks), jnp.stack(fvs), jnp.stack(fls),
            jnp.stack(pps), jnp.stack(pss),
            jnp.stack(cps), jnp.stack(css),
            jnp.stack(hps), jnp.stack(hss),
            jnp.stack(gvs),
            jnp.stack(mkp), jnp.stack(mvp))


_drawn_inputs = setup_inputs


def setup_inputs(seed=0):
    import zlib

    import numpy as np

    out = dict(_drawn_inputs(seed))
    spreads = {}
    factors = {'cache_fox_logf': 8.0, 'ssm_norm_w': 8.0, 'gmlp_ln_b': 2.786, 'b_spatial': 4.644}
    for name, (base, spread) in spreads.items():
        noise = np.random.default_rng([zlib.crc32(name.encode()), seed]).standard_normal(out[name].shape)
        drawn = base * np.exp(spread * noise) if base else spread * noise
        out[name] = jnp.asarray(drawn.astype(out[name].dtype))
    for name, factor in factors.items():
        out[name] = (out[name] * factor).astype(out[name].dtype)
    return out
```

```python
from contextlib import ExitStack

import concourse.bass as bass
from concourse import mybir

F32 = mybir.dt.float32
F32R = mybir.dt.float32r
I32 = mybir.dt.int32
ALU = mybir.AluOpType
ACT = mybir.ActivationFunctionType
AX = mybir.AxisListType
RMAX = bass.bass_isa.ReduceOp.max
RADD = bass.bass_isa.ReduceOp.add
ds = bass.ds

P = 128
D = 1024
DC = D // P
SEQ = 1024
NT = SEQ // P
DECB = 8
TOK = SEQ + DECB
NB = 3
TB = TOK // NB
DEPTH = 2
ALPHA = (2 * DEPTH) ** 0.25
LN_EPS = 1e-5
BIG = 1e30
FH, FD = 8, 64
FW = FH * FD
PAGE, NPG = 128, 16
NPHYS = 160
WINDOWS = (2, 4, 8, 16)
PBUF = 15
NMEM, MH, MD = 256, 4, 256
SH, SD, SN, SG = 16, 64, 128, 2
SI = SH * SD
CCH = SI + 2 * SG * SN
CONVW = 4
GW = 512
FFC = 22
FF = FFC * P
FF_GROUPS = (8, 8, 6)


def hybrid_step(nc, A, O):
    with ExitStack() as ctx:
        sems = {}

        def sem(name):
            if name not in sems:
                sems[name] = ctx.enter_context(nc.semaphore(name))
            return sems[name]

        def sb(name, shape, dt=F32, at=None):
            return (at or ctx).enter_context(nc.sbuf_tensor(name, shape, dt))

        def scratch(name, shape):
            return nc.dram_tensor(name, shape, F32, kind="Internal").ap()

        x = sb("x", [P, DC, TOK])
        raw_w = sb("raw_w", [P, 2, DC, P])
        spl_w = sb("spl_w", [P, 2, 2, DC, P], F32R)
        ident = sb("ident", [P, P])
        ones = sb("ones", [P, P])
        causal = sb("causal", [P, P])
        later = sb("later", [P, P])
        future = sb("future", [P, P])
        cols = sb("cols", [P, 192])
        eps = sb("eps", [P, 1])
        tiny = sb("tiny", [P, 64])
        tmax = sb("tmax", [P, 4])
        nmax = sb("nmax", [P, 8])
        rsum = sb("rsum", [P, 8])
        rinv = sb("rinv", [P, 8])
        st_sum = sb("st_sum", [P, 4, DECB])
        page_idx = sb("page_idx", [1, DECB * NPG], I32)
        lf_new = sb("lf_new", [P, DECB * FH])
        sc_new = sb("sc_new", [1, DECB * FH])
        s_red = sb("s_red", [P, 4, DECB * FH])
        smx = sb("smx", [P, DECB, 2, MH])
        sel_b = sb("sel_b", [MH * DECB, DECB])
        smr = sb("smr", [P, 4, DECB, MH])
        dskip = sb("dskip", [P, DC])
        s_new = sb("s_new", [P, 4, DECB])
        s_sum = sb("s_sum", [P, 4, DECB])
        inv_cnt = sb("inv_cnt", [P, 4, 16])
        w_small = sb("w_small", [P, DC, SH])

        xs_area = ExitStack()
        xs = sb("xs", [P, 2, DC, TOK], F32R, xs_area)

        rest = ExitStack()
        proj = sb("proj", [P, 16, TOK], F32, rest)
        kst = sb("kst", [P, 2, FW], F32, rest)
        w_pl = sb("w_pl", [P, 4, P], F32, rest)
        lf_pg = sb("lf_pg", [P, DECB, NPG, FH], F32, rest)
        ulast = sb("ulast", [PBUF, FW], F32, rest)
        own = sb("own", [FH, FW], F32, rest)
        rest.close()
        rest = ExitStack()
        xin = sb("xin", [P, 2, D], F32, rest)
        prow = sb("prow", [P, 2, P], F32, rest)
        rest.close()
        rest = ExitStack()
        sum_x = sb("sum_x", [P, TOK], F32, rest)
        sum_sq = sb("sum_sq", [P, TOK], F32, rest)
        sq = sb("sq", [P, TOK], F32, rest)
        ln_rest = ExitStack()
        hs = sb("hs", [P, 2, DC, TOK], F32R, ln_rest)
        ln_rest.close()
        ln_rest = ExitStack()
        qx = sb("qx", [P, DC, TOK], F32, ln_rest)
        mem_s = sb("mem_s", [P, 2, DC, NMEM], F32R, ln_rest)
        mkT = sb("mkT", [P, DC, NMEM], F32, ln_rest)
        mem_n = sb("mem_n", [P, 2, D], F32, ln_rest)
        ln_rest.close()
        rest.close()

        xs_area.close()
        xs_area = ExitStack()
        cb = sb("cb", [P, 2, SEQ], F32, xs_area)
        cbd = sb("cbd", [P, 2, NT, P], F32, xs_area)
        prob = sb("prob", [P, 3, SEQ], F32, xs_area)
        pT = sb("pT", [P, 2, NT, P], F32, xs_area)
        kp_area = ExitStack()
        kpage = sb("kpage", [P, 4, 2, FW], F32, kp_area)
        kp_area.close()
        s_nat = sb("s_nat", [DECB, 4, FW], F32, xs_area)
        s_qk = sb("s_qk", [P, 4, FW], F32, xs_area)
        qb = sb("qb", [P, 2, FW], F32, xs_area)
        sc_area = ExitStack()
        sc = sb("sc", [P, DECB, FH, NPG + 1], F32, sc_area)
        sc_area.close()
        sc_area = ExitStack()
        win = sb("win", [P, 2, TOK], F32, sc_area)
        sc_area.close()
        xs_area.close()
        xs_area = ExitStack()
        rows = sb("rows", [FH, 5, TOK], F32, xs_area)
        lf_nat = sb("lf_nat", [P, NT + 1, FH], F32, xs_area)
        xs_area.close()
        xs_area = ExitStack()
        mkv = sb("mkv", [P, 4, 2, D], F32, xs_area)
        qbx = sb("qbx", [P, 2, D], F32, xs_area)
        probx = sb("probx", [P, 2, D], F32, xs_area)
        pTx = sb("pTx", [P, 2, 2 * MH, P], F32, xs_area)
        qn_area = ExitStack()
        qn = sb("qn", [DECB, D], F32, qn_area)
        qn_area.close()
        own_x = sb("own_x", [MH * DECB, MH, MD], F32, xs_area)
        smz = sb("smz", [P, DECB, 2, MH, DECB], F32, xs_area)
        xs_area.close()

        rest = ExitStack()
        sb("beside_xs", [P, 2, DC, TOK], F32R, rest)
        xbc = sb("xbc", [P, 12, TOK], F32, rest)
        acc = sb("acc", [P, 2, TOK], F32, rest)
        work = sb("work", [P, 4, 1024], F32, rest)
        tail = sb("tail", [P, 12, CONVW - 1 + DECB], F32, rest)
        convT = sb("convT", [P, 12, DECB, CONVW - 1], F32, rest)
        dtn = sb("dtn", [P, 2, NT, SH], F32, rest)
        ends = sb("ends", [P, SH, NT], F32, rest)
        sdt = sb("sdt", [P, 2, DC, DECB], F32, rest)
        dec_end = sb("dec_end", [P, NT, SH], F32, rest)
        dec_chunk = sb("dec_chunk", [P, SH, NT], F32, rest)
        ys = sb("ys", [P, DC, DECB], F32, rest)
        rest.close()
        rest = ExitStack()
        sb("beside_xs_too", [P, 2, DC, TOK], F32R, rest)
        sb("under_yd", [P, DC, TOK], F32, rest)
        yd_s = sb("yd_s", [P, 2, 4, TOK], F32R, rest)
        rest.close()
        b_nat = work[:, 0:2].rearrange("p a (i n) -> p (a i) n", n=2 * SN)
        cbT = work[:, 2:4].rearrange("p g (i n) -> p g i n", n=P)
        xs_area = ExitStack()
        xdt = sb("xdt", [P, NT, SI], F32, xs_area)
        hprev = sb("hprev", [P, NT, SI], F32, xs_area)
        xs_area.close()
        xs_area = ExitStack()
        rows16 = sb("rows16", [SH, 6, TOK], F32, xs_area)
        ctail = sb("ctail", [CONVW - 1 + DECB, CCH], F32, xs_area)
        xs_area.close()
        xs_area = ExitStack()
        gv = sb("gv", [P, 4, TOK], F32, xs_area)
        gu = sb("gu", [P, 4, TOK], F32, xs_area)
        sst = sb("sst", [P, DECB, DC, SN], F32, xs_area)
        xs_area.close()

        ps = ctx.enter_context(nc.psum_tensor("ps", [P, 8, 512], F32))
        ps_set = [ps[:, 0:3, 0:TB], ps[:, 3:6, 0:TB]]

        lf_flat = lf_pg[:].rearrange("p b g h -> p (b g h)")
        suf = kst[:].rearrange("p a n -> p (a n)")

        STEPS = {
            "pe": ("colsT_ready", "gate_logits", "stateT_ready", "ulastT_ready", "s_natT_ready", "lfT_ready", "s_values_ready", "convT_turned", "dt_logits", "tailT_ready", "s_bcT_ready", "dtT_ready", "lastT_ready", "wmT_turned", "v_rowT"),
            "act": ("gate_ln", "ulast_ready", "s_nat_ready", "sc_exp", "convT_ready", "dt_row", "dt_ln", "ctail_ready", "s_bc_ready", "dtn_ready", "last_ready", "g_mean_sq", "g_std", "v_row_ready", "rms_rstd"),
            "dve": ("inv_cnt_ready", "sel_b_ready", "logf_ready", "c_ready", "new_scores", "sc_cleared", "s_max_ready", "sc_shifted", "s_sum_ready", "sc_ready", "acs_ready",
                    "dec_diff", "g_var", "wmT_ready", "xdt_s"),
            "pool": ("own_ready", "s_max_all", "s_sum_all"),
        }
        pe_steps, act_steps, dve_steps, pool_steps = (sem(f"{e}_steps") for e in ("pe", "act", "dve", "pool"))
        marked = {e: 0 for e in STEPS}

        def step(name):
            return next(names.index(name) + 1 for names in STEPS.values() if name in names)

        def mark(name):
            e = next(e for e, names in STEPS.items() if name in names)
            marked[e] += 1
            assert marked[e] == step(name), (name, marked[e])
            return 1

        w_loaded = [sem("w_loaded0"), sem("w_loaded1")]
        hi_ready, lo_ready, tile_done = sem("hi_ready"), sem("lo_ready"), sem("tile_done")
        set_free = [sem("set0_free"), sem("set1_free")]

        def kview(w, rows=None):
            w = w if rows is None else w[rows[0]:rows[1], :]
            return w.rearrange("(k p) n -> p k n", p=P)

        def loop(eng, n, body):
            if n == 1:
                body(0)
            else:
                with eng.Fori(0, n) as i:
                    body(i)

        def load_pair(sp, g, src0, src1, nk=DC, first=False):
            for s, src in enumerate((src0, src1)):
                if not first:
                    sp.wait_ge(hi_ready, 2 * g - 1 + s)
                    sp.wait_ge(lo_ready, 2 * g - 1 + s)
                sp.dma_start(raw_w[:, s, 0:nk, :], src).then_inc(w_loaded[s], 16)

        def split_hi(act, s, g, first=False):
            act.wait_ge(w_loaded[s], 16 * (g + 1))
            if not first:
                act.wait_ge(tile_done, 2 * g - 1 + s)
            act.copy(spl_w[:, s, 0], raw_w[:, s]).then_inc(hi_ready, 1)

        def split_lo(dve, s, g):
            dve.wait_ge(hi_ready, 2 * g + s + 1)
            dve.tensor_tensor(spl_w[:, s, 1], raw_w[:, s], spl_w[:, s, 0].bitcast(F32),
                              ALU.subtract).then_inc(lo_ready, 1)

        def product_tile(pe, s, g, act_in, nk=DC, n=NB, width=TB, first=False, split=None):
            pe.wait_ge(lo_ready, 2 * g + s + 1)
            if not first:
                pe.wait_ge(set_free[s], g)
            for k in range(nk):
                if split:
                    pe.wait_ge(split[0], split[1] + k + 1)
                for step, (a, b) in enumerate(((0, 0), (0, 1), (1, 0))):
                    for t in range(n):
                        mm = pe.matmul(ps[:, 3 * s + t, 0:width], spl_w[:, s, a, k],
                                       act_in[:, b, k, width * t:width * (t + 1)],
                                       start=(k == 0 and step == 0), stop=(k == nk - 1 and step == 2))
            mm.then_inc(tile_done, 1)

        sizes = [("ab_q", 2), ("ab_kv", 4), ("ab_u", 2), ("ab_out", 4)]
        for L in range(DEPTH):
            if L == 1:
                sizes += [("cd_z", 4), ("cd_gu", 2), ("cd_xbc", 6), ("cd_gv", 2),
                          ("cd_out_y", 4), ("cd_out_d", 4)]
            sizes += [(f"mem{L}", 8), (f"xq{L}", 4), (f"xo{L}", 4)]
            for q, c in enumerate(FF_GROUPS):
                sizes += [(f"gu{L}_{q}", c), (f"down{L}_{q}", 4)]
        G0, G1, at = {}, {}, 0
        for name, n in sizes:
            G0[name] = at
            at += n
            G1[name] = at
        N_PAIRS = at

        COL = {"ln_mix_g": 0, "ln_mix_b": 16, "ln_x_g": 32, "ln_x_b": 48, "ln_ff_g": 64,
               "ln_ff_b": 80, "pool_scale": 96, "conv_b": 100, "ssm_norm_w": 112,
               "gmlp_ln_g": 120, "gmlp_ln_b": 124, "conv_w": 128}

        def col(name, c):
            return cols[:, COL[name] + c:COL[name] + c + 1]

        q_d = scratch("q_d", [DECB, FW])
        ks_d = scratch("ks_d", [DECB, FH])
        c_d = scratch("c_d", [FH, SEQ])

        chains = {}

        def chain(eng, name):
            name = name.split("_")[0] + "_chain"
            s, n = sem(name), chains.setdefault(name, [0])

            def then(ins):
                n[0] += 1
                ins.then_inc(s, 1)
                eng.wait_ge(s, n[0])
            return then

        tiles = [(i * P, P) for i in range(NT)] + [(SEQ, DECB)]

        def sp_setup(sp):
            for n, name in enumerate(("ln_mix_g", "ln_mix_b", "ln_x_g", "ln_x_b", "ln_ff_g", "ln_ff_b",
                                      "pool_scale", "conv_b", "ssm_norm_w", "gmlp_ln_g", "gmlp_ln_b")):
                src = A[name].rearrange("a (c p) -> (a c) p", p=P)
                sp.dma_start(prow[COL[name]:COL[name] + src.shape[0], 0, :], src).then_inc(sem("rows_in"), 16)
            sp.dma_start(prow[0:48, 1, :], A["conv_w"].rearrange("a j (c p) -> (a j c) p", p=P)).then_inc(sem("rows_in"), 16)
            for n, (t0, m) in enumerate(tiles):
                if n >= 2:
                    sp.wait_ge(sem("xT_ready"), n - 1)
                src = A["x_prompt"][0, t0:t0 + m, :] if n < NT else A["x_sample"][:, 0, :]
                sp.dma_start(xin[0:m, n % 2, :], src).then_inc(sem(f"xin_loaded{n % 2}"), 16)
            load_pair(sp, 0, win_ab[:, :, 0:P], win_ab[:, :, P:2 * P], first=True)
            sp.dma_start(page_idx[:], A["page_table"].rearrange("b g -> (b g)").unsqueeze(0)).then_inc(sem("pages_in"), 16)
            sp.dma_start(w_small[:, :, 0:FH], win_ab[:, :, 3 * FW:3 * FW + FH]).then_inc(sem("w_small_in"), 16)
            sp.dma_start(tiny[0:FH, 0:1], A["b_forget"].rearrange("a h -> h a")).then_inc(sem("w_small_in"), 16)
            sp.dma_start(tiny[0:SH, 1:2], A["dt_bias"].rearrange("a h -> h a")).then_inc(sem("w_small_in"), 16)
            sp.dma_start(tiny[0:SH, 2:3], A["a_log"].rearrange("a h -> h a")).then_inc(sem("w_small_in"), 16)

        def pool_setup(pool):
            then = chain(pool, "pool_setup")
            then(pool.memset(ident[:], 0.0))
            then(pool.memset(future[:], 0.0))
            then(pool.memset(ones[:], 1.0))
            pool.sem_inc(sem("sum_x_ready"), 1)
            pool.sem_inc(sem("sq_used"), 1)
            pool.sem_inc(sem("spilled0"), 16)
            pool.sem_inc(sem("spilled1"), 16)
            pool.sem_inc(sem("ff_hi"), 1)
            pool.sem_inc(sem("ff_lo"), 1)
            pool.sem_inc(sem("mem_rows"), 2)
            pool.sem_inc(sem("mem_rowsT"), 2)
            pool.memset(eps[:], LN_EPS).then_inc(sem("const_ready"), 1)
            pool.affine_select(out=ident[:], in_=ident[:], compare_op=ALU.not_equal, fill=1.0, base=0,
                               pattern=[[-1, P]], channel_multiplier=1).then_inc(sem("const_ready"), 1)
            pool.affine_select(out=future[:], in_=future[:], compare_op=ALU.is_ge, fill=BIG, base=0,
                               pattern=[[-1, P]], channel_multiplier=1).then_inc(sem("const_ready"), 1)
            pool.affine_select(out=later[:], in_=ones[:], compare_op=ALU.is_gt, fill=0.0, base=0,
                               pattern=[[-1, P]], channel_multiplier=1).then_inc(sem("const_ready"), 1)
            pool.affine_select(out=causal[:], in_=ones[:], compare_op=ALU.is_ge, fill=0.0, base=0,
                               pattern=[[1, P]], channel_multiplier=-1).then_inc(sem("const_ready"), 1)
            then(pool.iota(inv_cnt[:], pattern=[[0, 4], [1, 16]], base=1, channel_multiplier=0,
                           allow_small_or_imprecise_dtypes=True))
            for g, w in enumerate(WINDOWS):
                pool.tensor_scalar(inv_cnt[:, g], inv_cnt[:, g], float(w), None, ALU.min).then_inc(sem("const_ready"), 1)

        N_CONST = 9

        def pe_setup(pe):
            pe.wait_ge(sem("const_ready"), N_CONST)
            pe.wait_ge(sem("rows_in"), 16 * 12)
            pe.transpose(ps[:, 0, 0:P], prow[:, 0, :], ident[:])
            pe.transpose(ps[:, 0, P:P + 48], prow[0:48, 1, :], ident[0:48, 0:48]).then_inc(pe_steps, mark("colsT_ready"))
            for n, (t0, m) in enumerate(tiles):
                pe.wait_ge(sem(f"xin_loaded{n % 2}"), 16 * (n // 2 + 1))
                if n >= 2:
                    pe.wait_ge(sem("xT_copied"), n - 1)
                for c in range(DC):
                    mm = pe.transpose(ps[:, 2 + 2 * (n % 2) + c // 4, m * (c % 4):m * (c % 4 + 1)],
                                      xin[0:m, n % 2, P * c:P * (c + 1)], ident[0:m, 0:m])
                mm.then_inc(sem("xT_ready"), 1)

        def act_setup(act):
            act.wait_ge(pe_steps, step("colsT_ready"))
            act.copy(cols[:, 0:176], ps[:, 0, 0:176]).then_inc(sem("cols_ready"), 1)
            for n, (t0, m) in enumerate(tiles):
                act.wait_ge(sem("xT_ready"), n + 1)
                b = 2 + 2 * (n % 2)
                act.copy(x[:, :, t0:t0 + m].rearrange("p (a c) t -> p a c t", a=2),
                         ps[:, b:b + 2, 0:4 * m].rearrange("p a (c t) -> p a c t", c=4)).then_inc(sem("xT_copied"), 1)
            split_hi(act, 0, 0, first=True)
            act.wait_ge(sem("xT_copied"), NT + 1)
            for k in range(DC):
                act.copy(xs[:, 0, k], x[:, k]).then_inc(sem("xs_hi"), 1)

        def dve_setup(dve):
            dve.wait_ge(sem("const_ready"), N_CONST)
            dve.reciprocal(inv_cnt[:], inv_cnt[:]).then_inc(dve_steps, mark("inv_cnt_ready"))
            n = MH * DECB
            dve.tensor_reduce(sel_b[:], ident[0:n, 0:n].rearrange("p (h b) -> p b h", h=MH), AX.X, ALU.add
                              ).then_inc(dve_steps, mark("sel_b_ready"))
            split_lo(dve, 0, 0)
            for k in range(DC):
                split_act_lo(dve, k, x[:, k], k + 1)

        def split_act_lo(dve, k, src, n_hi):
            dve.wait_ge(sem("xs_hi"), n_hi)
            dve.tensor_tensor(xs[:, 1, k], src, xs[:, 0, k].bitcast(F32), ALU.subtract).then_inc(sem("xs_lo"), 1)

        def sp_stream(sp, name, src, nk=DC, skip=0):
            g0, n = G0[name], G1[name] - G0[name]
            if skip < n:
                loop(sp, n - skip, lambda i: load_pair(sp, g0 + skip + i, *src(i + skip), nk=nk))

        def pe_stream(pe, name, act_in, nk=DC, n=NB, width=TB, split=None):
            g0, cnt = G0[name], G1[name] - G0[name]
            if split:
                for s in range(2):
                    product_tile(pe, s, g0, act_in, nk, n, width, first=(g0 == 0), split=split if s == 0 else None)
                g0, cnt = g0 + 1, cnt - 1
            def body(i):
                for s in range(2):
                    product_tile(pe, s, g0 + i, act_in, nk, n, width)
            loop(pe, cnt, body)

        def act_stream(act, name, evac=None):
            g0, cnt = G0[name], G1[name] - G0[name]
            def body(i, last=False, first=False):
                g = g0 + i
                split_hi(act, 1, g, first=first)
                if evac:
                    act.wait_ge(tile_done, 2 * g + 1)
                    settle(act)
                    evac(0, i, g)
                if not last:
                    split_hi(act, 0, g + 1)
                if evac:
                    act.wait_ge(tile_done, 2 * g + 2)
                    settle(act)
                    evac(1, i, g)
            if g0 == 0:
                body(0, first=True)
                loop(act, cnt - 1, lambda i: body(i + 1))
            elif G1[name] == N_PAIRS:
                loop(act, cnt - 1, body)
                body(cnt - 1, last=True)
            else:
                loop(act, cnt, body)

        def dve_stream(dve, name, evac=None):
            g0, cnt = G0[name], G1[name] - G0[name]
            def body(i, last=False):
                g = g0 + i
                split_lo(dve, 1, g)
                if evac:
                    evac(0, i, g)
                if not last:
                    split_lo(dve, 0, g + 1)
                if evac:
                    evac(1, i, g)
            if G1[name] == N_PAIRS:
                loop(dve, cnt - 1, body)
                body(cnt - 1, last=True)
            else:
                loop(dve, cnt, body)

        def settle(act, n=0):
            act.wait_ge(sem(("cols_ready", "xT_copied", "const_ready", "rows_in", "xin_loaded0", "w_small_in")[n]), 1)

        def chunk(t, c):
            return t[:, ds(c, 1), :].rearrange("p a n -> p (a n)")

        def blocks(ap):
            return ap.rearrange("p (b n) -> p b n", b=NB)

        win_ab = kview(A["w_in_ab"][0])
        AB_COL = {"ab_q": 0, "ab_kv": FW, "ab_u": 3 * FW + FH}

        def sp_ab_in(sp):
            for name in ("ab_q", "ab_kv", "ab_u"):
                c0 = AB_COL[name]
                sp_stream(sp, name, lambda i, c0=c0: (win_ab[:, :, ds(c0 + 256 * i, P)],
                                                      win_ab[:, :, ds(c0 + P + 256 * i, P)]),
                          skip=(name == "ab_q"))

        def pe_ab_in(pe):
            for name in ("ab_q", "ab_kv", "ab_u"):
                pe_stream(pe, name, xs, split=(sem("xs_lo"), 0) if name == "ab_q" else None)

        def act_ab_in(act):
            for name, c0, scale in (("ab_q", 0, FD ** -0.5), ("ab_kv", 4, 1.0), ("ab_u", 12, 1.0)):
                def evac(s, i, g, c0=c0, scale=scale):
                    act.activation(blocks(chunk(proj, c0 + 2 * i + s)), ps_set[s], ACT.Copy,
                                   scale=scale).then_inc(set_free[s], 1)
                act_stream(act, name, evac)

        def dve_ab_in(dve):
            for name in ("ab_q", "ab_kv", "ab_u"):
                dve_stream(dve, name)

        def pe_gates(pe):
            pe.wait_ge(sem("w_small_in"), 64)
            pe.wait_ge(set_free[0], G1["ab_u"])
            for k in range(DC):
                for t in range(NB):
                    mm = pe.matmul(ps[0:FH, t, 0:TB], w_small[:, k, 0:FH], x[:, k, TB * t:TB * (t + 1)],
                                   start=(k == 0), stop=(k == DC - 1))
            mm.then_inc(pe_steps, mark("gate_logits"))

        def act_gates(act):
            then = chain(act, "act_gate_chain")
            act.wait_ge(pe_steps, step("gate_logits"))
            act.wait_ge(tile_done, 2 * G1["ab_u"])
            then(act.activation(blocks(rows[:, 0, :]), ps[0:FH, 0:NB, 0:TB], ACT.Identity, bias=tiny[0:FH, 0:1]))
            then(act.activation(rows[:, 1, :], rows[:, 0, :], ACT.Abs))
            then(act.activation(rows[:, 1, :], rows[:, 1, :], ACT.Exp, scale=-1.0))
            act.activation(rows[:, 2, :], rows[:, 1, :], ACT.Ln, bias=1.0).then_inc(act_steps, mark("gate_ln"))

        def log1p_fix(dve, then, e, ln, u, d):
            then(dve.tensor_scalar(u, e, 1.0, None, ALU.add))
            then(dve.scalar_tensor_tensor(out=d, in0=u, scalar=-1.0, in1=e, op0=ALU.add, op1=ALU.subtract))
            then(dve.reciprocal(u, u))
            then(dve.tensor_tensor(d, d, u, ALU.mult))
            then(dve.tensor_tensor(ln, ln, d, ALU.subtract))

        def dve_gates(dve):
            then = chain(dve, "dve_gate_chain")
            dve.wait_ge(act_steps, step("gate_ln"))
            log1p_fix(dve, then, rows[:, 1, :], rows[:, 2, :], rows[:, 3, :], rows[:, 4, :])
            then(dve.scalar_tensor_tensor(out=rows[:, 0, :], in0=rows[:, 0, :], scalar=0.0, in1=rows[:, 2, :],
                                          op0=ALU.min, op1=ALU.subtract))
            dve.memset(rows[:, 1, :], 1.0).then_inc(dve_steps, mark("logf_ready"))
            dve.wait_ge(dve_steps, step("logf_ready"))
            dve.tensor_tensor_scan(rows[:, 3, 0:SEQ], rows[:, 1, 0:SEQ], rows[:, 0, 0:SEQ], 0.0,
                                   ALU.mult, ALU.add).then_inc(dve_steps, mark("c_ready"))

        def pe_gate_rows(pe):
            pe.wait_ge(dve_steps, step("logf_ready"))
            for n, (t0, m) in enumerate(tiles):
                mm = pe.transpose(ps[0:m, 0, FH * n:FH * (n + 1)], rows[:, 0, t0:t0 + m], ident[0:FH, 0:FH])
            mm.then_inc(pe_steps, mark("lfT_ready"))

        def act_gate_rows(act):
            act.wait_ge(pe_steps, step("lfT_ready"))
            act.copy(lf_nat[:, 0:NT], ps[:, 0, 0:FH * NT].rearrange("p (n h) -> p n h", h=FH)).then_inc(sem("lf_nat_ready"), 1)
            act.copy(lf_nat[0:DECB, NT], ps[0:DECB, 0, FH * NT:FH * (NT + 1)]).then_inc(sem("lf_nat_ready"), 1)
            act.wait_ge(sem("lf_nat_ready"), 2)
            act.dma_start(O["fox_logf_prompt"][0, 0].rearrange("(n p) h -> p n h", p=P), lf_nat[:, 0:NT]).then_inc(sem("lf_stored"), 16)
            act.dma_start(O["fox_logf_sample"][0, :, 0, :], lf_nat[0:DECB, NT]).then_inc(sem("lf_stored"), 16)
            act.wait_ge(dve_steps, step("c_ready"))
            act.dma_start(c_d, rows[:, 3, 0:SEQ]).then_inc(sem("lf_stored"), 16)

        def sp_naturals(sp):
            sp.dma_start(w_pl[:], A["w_pool"][0].rearrange("g c e -> c g e")).then_inc(sem("w_pool_in"), 16)
            sp.dma_start(kst[0:DECB * PBUF, 0, :],
                         A["state_pool"][0].rearrange("b t c -> (b t) c")).then_inc(sem("w_pool_in"), 16)
            sp.dma_start(O["pool_state_sample"][0, :, 0:PBUF - 1, :], A["state_pool"][0, :, 1:PBUF, :]).then_inc(sem("stored"), 16)

        def pe_naturals(pe):
            pe.wait_ge(sem("w_pool_in"), 32)
            pe.wait_ge(set_free[1], G1["ab_u"])
            n_state = DECB * PBUF
            for g in range(4):
                mm = pe.transpose(ps[:, 7, n_state * g:n_state * (g + 1)], kst[0:n_state, 0, P * g:P * (g + 1)],
                                  ident[0:n_state, 0:n_state])
            mm.then_inc(pe_steps, mark("stateT_ready"))
            for n in range(2 * NT):
                if n >= 4:
                    pe.wait_ge(sem("k_copied" if n % 2 == 0 else "v_copied"), n // 2 - 1)
                for c in range(4):
                    mm = pe.transpose(ps[:, 3 + n % 4, P * c:P * (c + 1)],
                                      proj[:, 4 + 4 * (n % 2) + c, P * (n // 2):P * (n // 2 + 1)], ident[:])
                mm.then_inc(sem("natT_ready"), 1)
            pe.wait_ge(sem("state_taken"), 1)
            for c in range(4):
                mm = pe.transpose(ps[0:PBUF, 7, P * c:P * (c + 1)], proj[:, 12 + c, SEQ - PBUF:SEQ], ident[:])
            mm.then_inc(pe_steps, mark("ulastT_ready"))
            pe.wait_ge(sem("k_copied"), NT)
            pe.wait_ge(sem("v_copied"), NT)
            for c in range(16):
                mm = pe.transpose(ps[0:DECB, 3 + c // 4, P * (c % 4):P * (c % 4 + 1)], proj[:, c, SEQ:TOK], ident[:])
            mm.then_inc(pe_steps, mark("s_natT_ready"))

        def act_naturals(act):
            for i in range(NT):
                act.wait_ge(sem("natT_ready"), 2 * i + 1)
                if i >= 2:
                    act.wait_ge(sem(f"rows_stored{i % 2}"), 16 * (i // 2))
                elif i == 0:
                    act.wait_ge(pe_steps, step("stateT_ready"))
                act.copy(kst[:, i % 2], ps[:, 3 + (2 * i) % 4, :]).then_inc(sem("k_copied"), 1)
                act.wait_ge(sem("k_copied"), i + 1)
                act.dma_start(O["fox_k_prompt"][0, 0, P * i:P * (i + 1)].rearrange("t h d -> t (h d)"),
                              kst[:, i % 2]).then_inc(sem(f"rows_stored{i % 2}"), 16)
                act.wait_ge(sem("v_copied"), i + 1)
                act.dma_start(O["fox_v_prompt"][0, 0, P * i:P * (i + 1)].rearrange("t h d -> t (h d)").rearrange("t (c n) -> t c n", c=4),
                              proj[:, 8:12, P * i:P * (i + 1)]).then_inc(sem("stored"), 16)
            act.wait_ge(pe_steps, step("ulastT_ready"))
            act.copy(ulast[:], ps[0:PBUF, 7, :]).then_inc(act_steps, mark("ulast_ready"))
            act.wait_ge(act_steps, step("ulast_ready"))
            act.dma_start(O["pool_state_prompt"][0, 0], ulast[:]).then_inc(sem("stored"), 16)
            act.wait_ge(pe_steps, step("s_natT_ready"))
            act.copy(s_nat[:], ps[0:DECB, 3:7, :]).then_inc(act_steps, mark("s_nat_ready"))
            act.wait_ge(act_steps, step("s_nat_ready"))
            act.dma_start(q_d, s_nat[:, 0]).then_inc(sem("q_stored"), 16)
            act.dma_start(O["fox_k_sample"][0, :, 0].rearrange("b h d -> b (h d)"), s_nat[:, 1]).then_inc(sem("stored"), 16)
            act.dma_start(O["fox_v_sample"][0, :, 0].rearrange("b h d -> b (h d)"), s_nat[:, 2]).then_inc(sem("stored"), 16)
            act.dma_start(O["pool_state_sample"][0, :, PBUF - 1, :], s_nat[:, 3]).then_inc(sem("stored"), 16)

        def dve_naturals(dve):
            for i in range(NT):
                dve.wait_ge(sem("natT_ready"), 2 * i + 2)
                dve.tensor_copy(proj[:, 8:12, P * i:P * (i + 1)],
                                ps[:, 3 + (2 * i + 1) % 4, :].rearrange("p (c n) -> p c n", c=4)).then_inc(sem("v_copied"), 1)

        def dve_new_scores(dve):
            then = chain(dve, "dve_new_chain")
            dve.wait_ge(act_steps, step("s_nat_ready"))
            then(dve.tensor_tensor(s_qk[0:DECB, 0], s_nat[:, 0], s_nat[:, 1], ALU.mult))
            dve.tensor_reduce(tiny[0:DECB, 8:8 + FH], s_qk[0:DECB, 0].rearrange("b (h d) -> b h d", h=FH),
                              AX.X, ALU.add).then_inc(dve_steps, mark("new_scores"))

        def dve_state_sums(dve):
            dve.wait_ge(pe_steps, step("stateT_ready"))
            st = ps[:, 7, 0:4 * DECB * PBUF].rearrange("p (g b t) -> p g b t", g=4, t=PBUF)
            for g, w in enumerate(WINDOWS):
                dve.tensor_reduce(st_sum[:, g], st[:, g, :, PBUF - (w - 1):PBUF], AX.X,
                                  ALU.add).then_inc(sem("state_taken"), 1)

        def dve_pool(dve):
            then = chain(dve, "dve_pool_chain")
            dve.wait_ge(dve_steps, step("inv_cnt_ready"))
            dve.wait_ge(sem("state_taken"), 4)
            dve.wait_ge(set_free[1], G1["ab_u"])
            dve.wait_ge(set_free[0], G1["ab_u"])
            dve.wait_ge(tile_done, 2 * G1["ab_u"])
            for g, w in enumerate(WINDOWS):
                u, us = proj[:, 12 + g, 0:SEQ], proj[:, 12 + g, SEQ:TOK]
                if g >= 1:
                    dve.wait_ge(sem("pool_products"), g)
                src, span, slot = u, 1, 0
                while span < w:
                    dst = win[:, slot, 0:SEQ]
                    then(dve.tensor_copy(dst[:, 0:span], src[:, 0:span]))
                    then(dve.tensor_tensor(dst[:, span:SEQ], src[:, span:SEQ], src[:, 0:SEQ - span], ALU.add))
                    src, span, slot = dst, 2 * span, 1 - slot
                then(dve.tensor_tensor(src[:, 0:16], src[:, 0:16], inv_cnt[:, g], ALU.mult))
                then(dve.tensor_scalar(src[:, 16:SEQ], src[:, 16:SEQ], 1.0 / w, None, ALU.mult))
                then(dve.tensor_tensor(src, src, u, ALU.subtract))
                out_s = win[:, g % 2, SEQ:TOK]
                then(dve.tensor_tensor(out_s, st_sum[:, g], us, ALU.add))
                dve.scalar_tensor_tensor(out=out_s, in0=out_s, scalar=1.0 / w, in1=us,
                                         op0=ALU.mult, op1=ALU.subtract).then_inc(sem("pool_ready"), 1)

        def pe_pool(pe):
            pe.wait_ge(sem("lf_nat_ready"), 2)
            pe.wait_ge(act_steps, step("s_nat_ready"))
            for g in range(4):
                pe.wait_ge(sem("pool_ready"), g + 1)
                if g >= 2:
                    pe.wait_ge(sem("pool_copied"), g - 1)
                for t in range(NB):
                    mm = pe.matmul(ps_set[g % 2][:, t], w_pl[:, g], win[:, g % 2, TB * t:TB * (t + 1)],
                                   start=True, stop=True)
                mm.then_inc(sem("pool_products"), 1)

        def act_pool(act):
            for g in range(4):
                act.wait_ge(sem("pool_products"), g + 1)
                act.activation(blocks(proj[:, 12 + g]), ps_set[g % 2], ACT.Copy,
                               scale=col("pool_scale", g)).then_inc(sem("pool_copied"), 1)

        N_ATT = FH * NT
        score_ps = [ps[:, 0:2, :].rearrange("p a n -> p (a n)"), ps[:, 2:4, :].rearrange("p a n -> p (a n)")]
        pT_ps = ps[:, 4:6, :].rearrange("p a (b n) -> p (a b) n", n=P)

        def head_rows(h):
            return slice(FD * (h % 2), FD * (h % 2 + 1))

        def act_load_c(act, h):
            if h >= 2:
                act.wait_ge(sem("scores_shifted"), NT * (h - 1))
                act.wait_ge(sem("masked"), h - 1)
            act.dma_start(cb[:, h % 2], c_d[h:h + 1, :].to_broadcast([P, SEQ])).then_inc(sem(f"row_loaded{h % 2}"), 16)

        def pool_mask(pool, h):
            pool.wait_ge(sem(f"row_loaded{h % 2}"), 16 * (h // 2 + 1))
            if h >= 2:
                pool.wait_ge(sem("scores_shifted"), NT * (h - 1))
            pool.tensor_tensor(cbd[:, h % 2], cb[:, h % 2].rearrange("p (i n) -> p i n", n=P),
                               future[:].unsqueeze(1).to_broadcast([P, NT, P]), ALU.add).then_inc(sem("masked"), 1)

        def pe_scores(pe, n):
            h, i = divmod(n, NT)
            if n >= 2:
                pe.wait_ge(sem("scores_shifted"), n - 1)
            r = head_rows(h)
            for k0 in range(0, P * (i + 1), 512):
                k1 = min(k0 + 512, P * (i + 1))
                mm = pe.matmul(score_ps[n % 2][:, k0:k1], proj[r, h // 2, P * i:P * (i + 1)],
                               proj[r, 4 + h // 2, k0:k1], start=True, stop=True)
            mm.then_inc(sem("scores_ready"), 1)

        def dve_shift(dve, n):
            h, i = divmod(n, NT)
            dve.wait_ge(sem("scores_ready"), n + 1)
            if i == 0:
                dve.wait_ge(sem("masked"), h + 1)
            if n >= 3:
                dve.wait_ge(sem("pT_ready"), n - 2)
            if n >= 2:
                dve.wait_ge(sem("nmax_ready"), n - 1)
                dve.wait_ge(sem("exp_done"), n - 1)
            k, t0 = P * i, 2 * (n % 2)
            if i:
                dve.tensor_tensor_reduce(prob[:, n % 3, 0:k], score_ps[n % 2][:, 0:k], cb[:, h % 2, 0:k], 1.0, -BIG,
                                         ALU.subtract, ALU.max, tmax[:, t0:t0 + 1])
            dve.tensor_tensor_reduce(prob[:, n % 3, k:k + P], score_ps[n % 2][:, k:k + P], cbd[:, h % 2, i], 1.0, -BIG,
                                     ALU.subtract, ALU.max, tmax[:, t0 + 1:t0 + 2]).then_inc(sem("scores_shifted"), 1)
            dve.wait_ge(sem("scores_shifted"), n + 1)
            dve.tensor_reduce(nmax[:, n % 2:n % 2 + 1], tmax[:, t0 + (0 if i else 1):t0 + 2], AX.X, ALU.max,
                              negate=True).then_inc(sem("nmax_ready"), 1)

        def act_exp(act, n):
            k = P * (n % NT + 1)
            act.wait_ge(sem("nmax_ready"), n + 1)
            if n >= 2:
                act.wait_ge(sem("prob_ready"), n - 1)
            act.activation(prob[:, n % 3, 0:k], prob[:, n % 3, 0:k], ACT.Exp, bias=nmax[:, n % 2:n % 2 + 1],
                           accum_out=rsum[:, n % 2:n % 2 + 1]).then_inc(sem("exp_done"), 1)

        def dve_normalize(dve, n):
            k = P * (n % NT + 1)
            dve.wait_ge(sem("exp_done"), n + 1)
            chain(dve, "dve_")(dve.reciprocal(rinv[:, n % 2:n % 2 + 1], rsum[:, n % 2:n % 2 + 1]))
            dve.tensor_scalar(prob[:, n % 3, 0:k], prob[:, n % 3, 0:k], rinv[:, n % 2:n % 2 + 1], None,
                              ALU.mult).then_inc(sem("prob_ready"), 1)

        def pe_turn(pe, n):
            pe.wait_ge(sem("prob_ready"), n + 1)
            if n:
                pe.wait_ge(sem("pT_copied"), n)
            for j in range(n % NT + 1):
                mm = pe.transpose(pT_ps[:, j], prob[:, n % 3, P * j:P * (j + 1)], ident[:])
            mm.then_inc(sem("pT_ready"), 1)

        def act_turn(act, n):
            j = n % NT + 1
            act.wait_ge(sem("pT_ready"), n + 1)
            if n >= 2:
                act.wait_ge(sem("out_ready"), n - 1)
            act.copy(pT[:, n % 2, 0:j], pT_ps[:, 0:j]).then_inc(sem("pT_copied"), 1)

        def pe_values(pe, n):
            h, i = divmod(n, NT)
            pe.wait_ge(sem("pT_copied"), n + 1)
            if n:
                pe.wait_ge(sem("out_copied"), n)
            for j in range(i + 1):
                v0 = P * j + FD * (h % 2)
                mm = pe.matmul(ps[head_rows(h), 6, 0:P], proj[:, 8 + h // 2, v0:v0 + FD],
                               pT[:, n % 2, j], start=(j == 0), stop=(j == i))
            mm.then_inc(sem("out_ready"), 1)

        def act_out(act, n):
            h, i = divmod(n, NT)
            act.wait_ge(sem("out_ready"), n + 1)
            act.copy(proj[head_rows(h), h // 2, P * i:P * (i + 1)],
                     ps[head_rows(h), 6, 0:P]).then_inc(sem("out_copied"), 1)

        page_loaded = [sem(f"page_loaded{slot}") for slot in range(4)]
        pages_used = sem("pages_used")
        N_STEP = DECB * NPG // 2

        def sp_pages(sp):
            sp.wait_ge(sem("pages_in"), 16)
            sp.wait_ge(sem("q_stored"), 32)
            sp.wait_ge(sem("stored"), 16 * 13)
            sp.wait_ge(sem("lf_stored"), 48)
            sp.dma_start(lf_new[:], O["fox_logf_sample"].rearrange("a b t h -> a (b t h)").to_broadcast([P, DECB * FH])).then_inc(sem("new_in"), 16)
            sp.dma_start(sc_new[:], ks_d.rearrange("b h -> (b h)").unsqueeze(0)).then_inc(sem("new_in"), 16)

            def page(j):
                return sp.value_load(page_idx[0:1, ds(j, 1)], min_val=0, max_val=NPHYS - 1)

            def fill(slot, u, j, cache):
                sp.wait_ge(pages_used, u + 1)
                for e in range(2):
                    sp.dma_start(kpage[:, slot, e], cache[0, ds(page(j + e), 1)].rearrange("a t h d -> (a t) (h d)")
                                 ).then_inc(page_loaded[slot], 16)

            def keys(b2):
                for r in range(2):
                    u0 = (2 * b2 + r) * (NPG // 2)
                    sp.wait_ge(pages_used, u0 + 1)
                    sp.dma_start(qb[:, r], q_d[ds(2 * b2 + r, 1), :].to_broadcast([P, FW])).then_inc(sem(f"q_row_loaded{r}"), 16)
                    for v in range(NPG // 2):
                        fill(v % 4, u0 + v, 2 * (u0 + v), A["cache_fox_k"])
            loop(sp, DECB // 2, keys)

            def values(m):
                for slot in range(4):
                    fill(slot, N_STEP + 4 * m + slot, 2 * (4 * m + slot), A["cache_fox_v"])
            loop(sp, N_STEP // 4, values)

        def pool_keys(pool, u):
            b, slot = u // (NPG // 2), u % 4
            pool.wait_ge(page_loaded[slot], 32 * (u // 4 + 1))
            pool.wait_ge(sem(f"q_row_loaded{b % 2}"), 16 * (b // 2 + 1))
            pool.tensor_tensor(kpage[:, slot], kpage[:, slot], qb[:, b % 2].unsqueeze(1).to_broadcast([P, 2, FW]),
                               ALU.mult).then_inc(sem("keys_multiplied"), 1)

        def dve_keys(dve, u):
            b, g, slot = u // (NPG // 2), 2 * (u % (NPG // 2)), u % 4
            dve.wait_ge(sem("keys_multiplied"), u + 1)
            dve.tensor_reduce(sc[:, b, :, g:g + 2].rearrange("p h g -> p g h"),
                              kpage[:, slot].rearrange("p g (h d) -> p g h d", h=FH), AX.X,
                              ALU.add).then_inc(pages_used, 1)

        def pe_suffix(pe, q):
            pe.wait_ge(sem("lf_loaded"), 16 * DECB * NPG)
            if q:
                pe.wait_ge(sem("suffix_copied"), 2 * q)
            src = lf_flat[:, 256 * q:256 * (q + 1)]
            pe.matmul(ps[:, 7, 0:256], later[:], src, start=True, stop=True)
            pe.matmul(ps[:, 7, 256:512], ones[:], src, start=True, stop=True).then_inc(sem("suffix_ready"), 1)

        def dve_suffix(dve, q):
            dve.wait_ge(sem("suffix_ready"), q + 1)
            if q == 0:
                for r in range(2):
                    dve.wait_ge(sem(f"rows_stored{r}"), 16 * NT // 2)
            dve.tensor_copy(suf[:, 256 * q:256 * (q + 1)], ps[:, 7, 0:256]).then_inc(sem("suffix_copied"), 1)
            dve.tensor_copy(lf_flat[:, 256 * q:256 * (q + 1)], ps[:, 7, 256:512]).then_inc(sem("suffix_copied"), 1)

        def dve_later_pages(dve):
            then = chain(dve, "dve_pages_chain")
            dve.wait_ge(sem("suffix_copied"), 8)
            dve.wait_ge(sem("new_in"), 32)
            for g in range(NPG - 2, -1, -1):
                then(dve.tensor_tensor(lf_pg[:, :, g], lf_pg[:, :, g], lf_pg[:, :, g + 1], ALU.add))
            sv = suf.rearrange("p (b g h) -> p b g h", b=DECB, h=FH)
            then(dve.tensor_tensor(sv[:, :, 0:NPG - 1], sv[:, :, 0:NPG - 1], lf_pg[:, :, 1:NPG], ALU.add))
            then(dve.tensor_tensor(sv, sv, lf_new[:].rearrange("p (b h) -> p b h", b=DECB).unsqueeze(2)
                                   .to_broadcast([P, DECB, NPG, FH]), ALU.add))

        def dve_sample_softmax(dve):
            then = chain(dve, "dve_softmax_chain")
            dve.wait_ge(pages_used, N_STEP + 4)
            bh = "p (b h) -> p b h"
            past = sc[:, :, :, 0:NPG]
            sv = suf.rearrange("p (b g h) -> p b h g", b=DECB, h=FH)
            then(dve.tensor_tensor(past, past, sv, ALU.add))
            then(dve.tensor_copy(sc[0:1, :, :, NPG], sc_new[:].rearrange(bh, b=DECB)))
            dve.tensor_reduce(s_red[:, 0].rearrange(bh, b=DECB), sc[:], AX.X, ALU.max).then_inc(dve_steps, mark("s_max_ready"))
            dve.wait_ge(pool_steps, step("s_max_all"))
            dve.tensor_tensor(sc[:], sc[:], s_red[:, 1].rearrange(bh, b=DECB).unsqueeze(3)
                              .to_broadcast([P, DECB, FH, NPG + 1]), ALU.subtract).then_inc(dve_steps, mark("sc_shifted"))
            dve.wait_ge(act_steps, step("sc_exp"))
            dve.tensor_reduce(s_red[:, 2].rearrange(bh, b=DECB), sc[:], AX.X, ALU.add).then_inc(dve_steps, mark("s_sum_ready"))
            dve.wait_ge(pool_steps, step("s_sum_all"))
            then(dve.reciprocal(s_red[:, 3], s_red[:, 3]))
            dve.tensor_tensor(sc[:], sc[:], s_red[:, 3].rearrange(bh, b=DECB).unsqueeze(3)
                              .to_broadcast([P, DECB, FH, NPG + 1]), ALU.mult).then_inc(dve_steps, mark("sc_ready"))

        def pool_sample_softmax(pool):
            pool.wait_ge(dve_steps, step("s_max_ready"))
            pool.partition_all_reduce(s_red[:, 1], s_red[:, 0], P, RMAX).then_inc(pool_steps, mark("s_max_all"))
            pool.wait_ge(dve_steps, step("s_sum_ready"))
            pool.partition_all_reduce(s_red[:, 3], s_red[:, 2], P, RADD).then_inc(pool_steps, mark("s_sum_all"))

        def act_sample_softmax(act):
            act.wait_ge(dve_steps, step("sc_shifted"))
            act.activation(sc[:], sc[:], ACT.Exp).then_inc(act_steps, mark("sc_exp"))

        def pe_sample_values(pe, u):
            b, slot = u // (NPG // 2), u % 4
            pe.wait_ge(page_loaded[slot], 32 * ((N_STEP + u) // 4 + 1))
            if u == 0:
                pe.wait_ge(dve_steps, step("sc_ready"))
                pe.wait_ge(sem("suffix_copied"), 8)
            if u % (NPG // 2) == 0 and b:
                pe.wait_ge(sem("s_own_step"), 2 * b)
            for e in range(2):
                g = 2 * (u % (NPG // 2)) + e
                mm = pe.matmul(ps[0:FH, 7, :], sc[:, b, :, g], kpage[:, slot, e], start=(g == 0), stop=(g == NPG - 1))
            mm.then_inc(pages_used, 1)

        def dve_sample_own(dve, b):
            if b == 0:
                dve.wait_ge(pool_steps, step("own_ready"))
            dve.wait_ge(pages_used, N_STEP + 4 + (NPG // 2) * (b + 1))
            if b >= 2:
                dve.wait_ge(sem("s_columns"), b - 1)
            dve.tensor_tensor(qb[0:FH, b % 2], ps[0:FH, 7, :], own[:], ALU.mult).then_inc(sem("s_own_step"), 1)

        def pe_sample_columns(pe, b):
            pe.wait_ge(sem("s_own_step"), 2 * b + 1)
            for c in range(4):
                mm = pe.matmul(ps[:, 7, c:c + 1], qb[0:FH, b % 2, P * c:P * (c + 1)], ones[0:FH, 0:1], start=True, stop=True)
            mm.then_inc(sem("s_columns"), 1)

        def dve_sample_columns(dve, b):
            dve.wait_ge(sem("s_columns"), b + 1)
            dve.tensor_copy(s_sum[:, :, b], ps[:, 7, 0:4]).then_inc(sem("s_own_step"), 1)

        def pe_sample_new(pe):
            pe.wait_ge(sem("s_own_step"), 2 * DECB)
            pe.matmul(ps[:, 7, 128:192], ones[0:1, :], sc[0:1, :, :, NPG].rearrange("p b h -> p b h"),
                      start=True, stop=True).then_inc(pe_steps, mark("s_values_ready"))

        def dve_sample_out(dve):
            dve.wait_ge(pe_steps, step("s_values_ready"))
            p_new = ps[:, 7, 128:192].rearrange("p (b c r) -> p r c b", b=DECB, r=2)
            for r in range(2):
                rs = slice(FD * r, FD * (r + 1))
                ins = dve.tensor_tensor(s_new[rs], proj[rs, 8:12, SEQ:TOK], p_new[rs, r], ALU.mult)
            chain(dve, "dve_")(ins)
            for r in range(2):
                rs = slice(FD * r, FD * (r + 1))
                dve.tensor_tensor(proj[rs, 0:4, SEQ:TOK], s_new[rs], s_sum[rs], ALU.add).then_inc(sem("s_att_ready"), 1)

        def sp_attention(sp):
            sp_pages(sp)

        def pool_gates(pool):
            pool.wait_ge(sem("pages_in"), 16)

            def gates(j):
                page = pool.value_load(page_idx[0:1, ds(j, 1)], min_val=0, max_val=NPHYS - 1)
                pool.dma_start(lf_flat[:, ds(FH * j, FH)], A["cache_fox_logf"][0, ds(page, 1)].rearrange("a t h -> (a t) h")
                               ).then_inc(sem("lf_loaded"), 16)
            loop(pool, DECB * NPG, gates)

        def pool_attention(pool):
            pool.sem_inc(pages_used, 4)
            then = chain(pool, "pool_")
            then(pool.memset(own[:], 1.0))
            then(pool.affine_select(out=own[:], in_=own[:], compare_op=ALU.is_ge, fill=0.0, base=0,
                                    pattern=[[1, FW]], channel_multiplier=-FD))
            pool.affine_select(out=own[:], in_=own[:], compare_op=ALU.is_ge, fill=0.0, base=FD - 1,
                               pattern=[[-1, FW]], channel_multiplier=FD).then_inc(pool_steps, mark("own_ready"))
            pool.wait_ge(dve_steps, step("new_scores"))
            pool_mask(pool, 0)
            for n in range(N_ATT):
                if n % NT == 4 and n // NT + 1 < FH:
                    pool_mask(pool, n // NT + 1)
                if n < 32:
                    pool_keys(pool, 2 * n)
                    pool_keys(pool, 2 * n + 1)
                if n == 33:
                    pool_sample_softmax(pool)

        def pe_attention(pe):
            pe.wait_ge(sem("lf_nat_ready"), 2)
            pe.wait_ge(act_steps, step("s_nat_ready"))
            pe.wait_ge(sem("v_copied"), NT)
            pe.wait_ge(act_steps, step("ulast_ready"))
            pe.wait_ge(sem("pool_copied"), 4)
            pe_scores(pe, 0)
            for n in range(N_ATT + 2):
                if n + 1 < N_ATT:
                    pe_scores(pe, n + 1)
                if 1 <= n <= N_ATT:
                    pe_turn(pe, n - 1)
                if n >= 2:
                    pe_values(pe, n - 2)
                if 8 <= n < 12:
                    pe_suffix(pe, n - 8)
                if n > 34 and (n - 34) % (NPG // 4) == 0:
                    pe_sample_columns(pe, (n - 34) // (NPG // 4) - 1)
                if n >= 34:
                    pe_sample_values(pe, 2 * (n - 34))
                    pe_sample_values(pe, 2 * (n - 34) + 1)
            pe_sample_columns(pe, DECB - 1)
            pe_sample_new(pe)

        def act_attention(act):
            act.wait_ge(sem("lf_stored"), 48)
            act.wait_ge(sem("pool_copied"), 4)
            act_load_c(act, 0)
            act_load_c(act, 1)
            for n in range(N_ATT + 2):
                if n < N_ATT:
                    act_exp(act, n)
                    if n % NT == NT - 1 and n // NT + 2 < FH:
                        act_load_c(act, n // NT + 2)
                if 1 <= n <= N_ATT:
                    act_turn(act, n - 1)
                if n >= 2:
                    act_out(act, n - 2)
                if n == 32:
                    act_sample_softmax(act)
            for k in range(DC):
                if k == 0:
                    act.wait_ge(sem("s_att_ready"), 2)
                    act.wait_ge(sem("out_copied"), N_ATT)
                act.copy(xs[:, 0, k], proj[:, AB_CHUNKS[k]]).then_inc(sem("xs_hi"), 1)

        AB_CHUNKS = (0, 1, 2, 3, 12, 13, 14, 15)

        def dve_attention(dve):
            dve.wait_ge(sem("pool_copied"), 4)
            dve.memset(sc[:, :, :, NPG], -BIG).then_inc(dve_steps, mark("sc_cleared"))
            dve.wait_ge(dve_steps, step("sc_cleared"))
            for n in range(N_ATT + 1):
                if n < N_ATT:
                    dve_shift(dve, n)
                if n:
                    dve_normalize(dve, n - 1)
                if n < 32:
                    dve_keys(dve, 2 * n)
                    dve_keys(dve, 2 * n + 1)
                if 9 <= n < 13:
                    dve_suffix(dve, n - 9)
                if n == 13:
                    dve_later_pages(dve)
                if n == 32:
                    dve_sample_softmax(dve)
                if n > 34 and (n - 34) % (NPG // 4) == 0:
                    dve_sample_own(dve, (n - 34) // (NPG // 4) - 1)
                    dve_sample_columns(dve, (n - 34) // (NPG // 4) - 1)
            dve_sample_own(dve, DECB - 1)
            dve_sample_columns(dve, DECB - 1)
            dve_sample_out(dve)
            for k in range(DC):
                split_act_lo(dve, k, proj[:, AB_CHUNKS[k]], DC + k + 1)

        def dve_residual(first, alpha):
            def evac(s, i, g):
                dve = nc.vector
                dve.wait_ge(tile_done, 2 * g + s + 1)
                xm = blocks(chunk(x, 2 * i + s))
                if alpha:
                    ins = dve.scalar_tensor_tensor(out=xm, in0=xm, scalar=ALPHA, in1=ps_set[s], op0=ALU.mult, op1=ALU.add)
                else:
                    ins = dve.tensor_tensor(xm, xm, ps_set[s], ALU.add)
                ins.then_inc(set_free[s], 1)
            return evac

        def act_square(ln):
            def evac(s, i, g):
                act = nc.scalar
                act.wait_ge(set_free[s], g + 1)
                act.wait_ge(sem("sq_used"), DC * ln + 2 * i + s + 1)
                settle(act)
                act.activation(sq[:], chunk(x, 2 * i + s), ACT.Square).then_inc(sem("sq_ready"), 1)
            return evac

        def pool_sums(pool, name, ln):
            g0, cnt = G0[name], G1[name] - G0[name]
            if ln:
                pool.wait_ge(sem("ln_scaled"), DC * ln)
                pool.wait_ge(sem("ln_shifted"), DC * ln)
            if ln in (2, 5):
                pool.wait_ge(sem("ff_hi"), FFC * (ln // 3 + 1) + 1)
                pool.wait_ge(sem("ff_lo"), FFC * (ln // 3 + 1) + 1)
            if ln in (0, 3):
                pool.wait_ge(sem("xs_lo"), XS_LO_MIXER[ln // 3])
            then = chain(pool, f"pool_ln{ln}")
            then(pool.memset(sum_x[:], 0.0))
            then(pool.memset(sum_sq[:], 0.0))

            def body(i):
                for s in range(2):
                    m = DC * ln + 2 * i + s
                    pool.wait_ge(set_free[s], g0 + i + 1)
                    pool.wait_ge(sem("sum_x_ready"), m + 1)
                    pool.tensor_tensor(sum_x[:], sum_x[:], chunk(x, 2 * i + s), ALU.add).then_inc(sem("sum_x_ready"), 1)
                    pool.wait_ge(sem("sq_ready"), m + 1)
                    pool.wait_ge(sem("sq_used"), m + 1)
                    pool.tensor_tensor(sum_sq[:], sum_sq[:], sq[:], ALU.add).then_inc(sem("sq_used"), 1)
            loop(pool, cnt, body)

        def pe_norm(pe, ln, g_end):
            pe.wait_ge(sem("sum_x_ready"), DC * (ln + 1) + 1)
            pe.wait_ge(set_free[0], g_end)
            pe.wait_ge(set_free[1], g_end)
            for t in range(NB):
                pe.matmul(ps_set[0][:, t], ones[:], sum_x[:, TB * t:TB * (t + 1)], start=True, stop=True)
            pe.wait_ge(sem("sq_used"), DC * (ln + 1) + 1)
            for t in range(NB):
                mm = pe.matmul(ps_set[1][:, t], ones[:], sum_sq[:, TB * t:TB * (t + 1)], start=True, stop=True)
            mm.then_inc(sem("ln_sums"), 1)

        def act_norm_stats(act, ln):
            act.wait_ge(sem("ln_sums"), ln + 1)
            act.activation(blocks(sq[:]), ps_set[0], ACT.Square, scale=1.0 / D).then_inc(sem("ln_act_step"), 1)
            act.wait_ge(sem("ln_dve_step"), 2 * ln + 1)
            chain(act, "act_")(act.activation(sum_sq[:], sum_sq[:], ACT.Ln, bias=eps[:, 0:1]))
            act.activation(sum_sq[:], sum_sq[:], ACT.Exp, scale=-0.5).then_inc(sem("ln_act_step"), 1)

        def dve_norm_stats(dve, ln):
            dve.wait_ge(sem("ln_act_step"), 2 * ln + 1)
            dve.scalar_tensor_tensor(out=blocks(sum_sq[:]), in0=ps_set[1], scalar=1.0 / D, in1=blocks(sq[:]),
                                     op0=ALU.mult, op1=ALU.subtract).then_inc(sem("ln_dve_step"), 1)
            dve.wait_ge(sem("ln_act_step"), 2 * ln + 2)
            dve.scalar_tensor_tensor(out=blocks(sum_x[:]), in0=ps_set[0], scalar=-1.0 / D, in1=blocks(sum_sq[:]),
                                     op0=ALU.mult, op1=ALU.mult).then_inc(sem("ln_dve_step"), 1)

        def dve_norm_scale(dve, ln, k):
            xk = chunk(x, k)
            dve.tensor_tensor(xk, xk, sum_sq[:], ALU.mult).then_inc(sem("ln_scaled"), 1)

        def pool_norm_shift(pool, ln, k):
            pool.wait_ge(sem("ln_dve_step"), 2 * ln + 2)
            pool.wait_ge(sem("ln_scaled"), DC * ln + k + 1)
            xk = chunk(x, k)
            pool.tensor_tensor(xk, xk, sum_x[:], ALU.add).then_inc(sem("ln_shifted"), 1)

        def act_norm_affine(act, ln, k):
            g = cols[:, ds(LN_G[ln] + k, 1)]
            b = cols[:, ds(LN_B[ln] + k, 1)]
            act.wait_ge(sem("ln_shifted"), DC * ln + k + 1)
            settle(act)
            act.activation(xs[:, 0, ds(k, 1)].rearrange("p a n -> p (a n)"), chunk(x, k), ACT.Identity, bias=b, scale=g)
            act.activation(chunk(x, k), chunk(x, k), ACT.Identity, bias=b, scale=g).then_inc(sem("ln_x"), 1)

        def dve_norm_lo(dve, ln, k):
            dve.wait_ge(sem("ln_x"), DC * ln + k + 1)
            dve.tensor_tensor(xs[:, 1, ds(k, 1)].rearrange("p a n -> p (a n)"), chunk(x, k),
                              xs[:, 0, ds(k, 1)].bitcast(F32).rearrange("p a n -> p (a n)"),
                              ALU.subtract).then_inc(sem("ln_lo"), 1)

        LN_G, LN_B = [], []
        for L in range(DEPTH):
            for which in ("ln_mix", "ln_x", "ln_ff"):
                LN_G.append(COL[which + "_g"] + DC * L)
                LN_B.append(COL[which + "_b"] + DC * L)

        XS_LO_MIXER = (2 * DC, 4 * DC)

        mk_nat = qx[:, 2:4, 0:D]
        v_tmp = qx[:, 0:2, 0:NMEM]

        def sp_memory(sp, L):
            sp.wait_ge(sem("xs_lo"), XS_LO_MIXER[L])
            sp.dma_start(mem_n[:], A["mem_prompt"][0].rearrange("(a p) d -> p a d", p=P)).then_inc(sem("mem_in"), 16)

        def sp_memory_out(sp, L):
            for out, src in (("mem_k_prompt", mk_nat), ("mem_v_prompt", mem_n[:])):
                sp.wait_ge(sem("mem_rows"), 16 * L + (10 if out == "mem_k_prompt" else 18))
                sp.dma_start(O[out][L, 0].rearrange("(a p) h d -> p a (h d)", p=P), src).then_inc(sem(out + "_stored"), 16)

        def pe_memory_turn(pe, L):
            pe.wait_ge(sem("mem_in"), 16 * (L + 1))
            for r in range(2):
                if r or L:
                    pe.wait_ge(sem("mem_lo"), 2 * L + r)
                for c in range(4):
                    for a in range(2):
                        mm = pe.transpose(ps[:, 6 + c // 2, NMEM * (c % 2) + P * a:NMEM * (c % 2) + P * (a + 1)],
                                          mem_n[:, a, P * (4 * r + c):P * (4 * r + c + 1)], ident[:])
                mm.then_inc(sem("memT_ready"), 1)

        def mem_ps(r):
            return ps[:, 6:8, :].rearrange("p a (c m) -> p (a c) m", m=NMEM)

        def act_memory_turn(act, L):
            for r in range(2):
                act.wait_ge(sem("memT_ready"), 2 * L + r + 1)
                act.copy(mem_s[:, 0, 4 * r:4 * r + 4], mem_ps(r)).then_inc(sem("mem_hi"), 1)

        def dve_memory_turn(dve, L):
            for r in range(2):
                dve.wait_ge(sem("mem_hi"), 2 * L + r + 1)
                dve.tensor_tensor(mem_s[:, 1, 4 * r:4 * r + 4], mem_ps(r), mem_s[:, 0, 4 * r:4 * r + 4].bitcast(F32),
                                  ALU.subtract).then_inc(sem("mem_lo"), 1)

        def sp_mem_weights(sp, L):
            wk, wv = kview(A["w_xk"][L]), kview(A["w_xv"][L])
            g0 = G0[f"mem{L}"]
            for q, w in enumerate((wk, wv)):
                loop(sp, 4, lambda i: load_pair(sp, g0 + 4 * q + i, w[:, :, ds(256 * i, P)], w[:, :, ds(256 * i + P, P)]))

        def pe_memory(pe, L, ln):
            pe.wait_ge(sem("mem_lo"), 2 * (L + 1))
            pe.wait_ge(sem("ln_dve_step"), 2 * ln + 2)
            g0 = G0[f"mem{L}"]
            for q in range(2):
                def body(i):
                    g = g0 + 4 * q + i
                    for s in range(2):
                        product_tile(pe, s, g, mem_s, n=1, width=NMEM)
                    for s in range(2):
                        src = v_tmp[:, s]
                        pe.wait_ge(set_free[s], g + 1)
                        pe.wait_ge(sem("mem_rows"), 16 * L + 8 * q + 2 * i + s + 1)
                        for a in range(2):
                            mm = pe.transpose(ps[:, 6 + s, P * a:P * (a + 1)],
                                              src[:, P * a:P * (a + 1)], ident[:])
                        mm.then_inc(sem("mem_rowsT"), 1)
                loop(pe, 4, body)

        def act_memory(act, L, ln):
            g0 = G0[f"mem{L}"]
            for q in range(2):
                def body(i):
                    g = g0 + 4 * q + i
                    for s in range(2):
                        split_hi(act, 1 - s, g + s)
                        act.wait_ge(tile_done, 2 * g + s + 1)
                        act.wait_ge(sem("mem_rowsT"), 16 * L + 8 * q + 2 * i + s + 1)
                        if q == 0:
                            act.copy(chunk(mkT, 2 * i + s), ps[:, 3 * s, 0:NMEM]).then_inc(sem("mkT_ready"), 1)
                        act.copy(v_tmp[:, s], ps[:, 3 * s, 0:NMEM]).then_inc(set_free[s], 1)
                    act_norm_affine(act, ln, 4 * q + i)
                loop(act, 4, body)

        def dve_memory(dve, L, ln):
            g0 = G0[f"mem{L}"]
            dve_norm_scale(dve, ln, 0)
            for q in range(2):
                def body(i, last=False):
                    g = g0 + 4 * q + i
                    split_lo(dve, 1, g)
                    split_lo(dve, 0, g + 1)
                    if not last:
                        dve_norm_scale(dve, ln, 4 * q + i + 1)
                    for s in range(2):
                        m = 16 * L + 8 * q + 2 * i + s
                        dve.wait_ge(sem("mem_rowsT"), m + 3)
                        dst = (mk_nat if q == 0 else mem_n[:])[:, :, ds(P * (2 * i + s), P)]
                        dve.tensor_copy(dst, ps[:, 6 + s, 0:2 * P].rearrange("p (a n) -> p a n", a=2)).then_inc(sem("mem_rows"), 1)
                    dve_norm_lo(dve, ln, 4 * q + i)
                if q == 0:
                    loop(dve, 4, body)
                else:
                    loop(dve, 3, body)
                    body(3, last=True)

        def pool_memory(pool, L, ln):
            loop(pool, DC, lambda i: pool_norm_shift(pool, ln, i))

        xT_ps = ps[:, 4:6, :].rearrange("p a (b n) -> p (a b) n", n=P)
        xo_ps = ps[:, 6:8, :].rearrange("p a (b n) -> p (a b) n", n=P)
        qx_d = [scratch(f"qx_d{L}", [DECB, D]) for L in range(DEPTH)]

        def square(w):
            v = kview(w)
            return lambda i: (v[:, :, ds(256 * i, P)], v[:, :, ds(256 * i + P, P)])

        def act_xq(act, L):
            def evac(s, i, g):
                act.activation(blocks(chunk(qx, 2 * i + s)), ps_set[s], ACT.Copy, scale=MD ** -0.5).then_inc(set_free[s], 1)
            act.wait_ge(sem("mem_k_prompt_stored"), 16 * (L + 1))
            act_stream(act, f"xq{L}", evac)

        def sp_cross(sp, L):
            sp.wait_ge(tile_done, 2 * G1[f"xq{L}"])
            for f in range(2 * DECB):
                if f >= 4:
                    if f - 4 < DECB:
                        sp.wait_ge(sem("mk_used"), DECB * L + f - 3)
                    else:
                        sp.wait_ge(sem("mv_used"), (DECB + 1) * L + f - 3 - DECB)
                cache = A["cache_mem_k"] if f < DECB else A["cache_mem_v"]
                sp.dma_start(mkv[:, f % 4], cache[L, f % DECB].rearrange("(a p) h d -> p a (h d)", p=P)).then_inc(sem(f"mkv_loaded{f % 4}"), 16)
                if f < DECB:
                    if f == 0:
                        sp.wait_ge(sem("q_stored"), 16 * (L + 3))
                    if f >= 2:
                        sp.wait_ge(sem("mk_used"), DECB * L + f - 1)
                    sp.dma_start(qbx[:, f % 2], qx_d[L][f:f + 1, :].to_broadcast([P, D])).then_inc(sem(f"q_row_loaded{f % 2}"), 16)

        def pe_cross(pe, L):
            N0 = NT * L
            for s in range(2):
                pe.wait_ge(set_free[s], G1[f"xq{L}"])
            for c in range(DC):
                mm = pe.transpose(ps[0:DECB, 6 + c // 4, P * (c % 4):P * (c % 4 + 1)], qx[:, c, SEQ:TOK], ident[:])
            mm.then_inc(sem("qnT_ready"), 1)

            def scores(i):
                if i >= 2:
                    pe.wait_ge(sem("x_exp"), MH * (N0 + i - 1))
                for h in range(MH):
                    for kc in range(2):
                        mm = pe.matmul(ps[:, 2 * (i % 2) + h // 2, NMEM * (h % 2):NMEM * (h % 2 + 1)],
                                       qx[:, 2 * h + kc, P * i:P * (i + 1)], mkT[:, 2 * h + kc],
                                       start=(kc == 0), stop=(kc == 1))
                mm.then_inc(sem("x_scores"), 1)

            def turn(i):
                pe.wait_ge(sem("x_prob"), N0 + i + 1)
                if i:
                    pe.wait_ge(sem("x_pT"), N0 + i)
                for j in range(2 * MH):
                    mm = pe.transpose(xT_ps[:, j], probx[:, i % 2, P * j:P * (j + 1)], ident[:])
                mm.then_inc(sem("x_turned"), 1)

            def values(i):
                pe.wait_ge(sem("x_pT"), N0 + i + 1)
                if i:
                    pe.wait_ge(sem("x_out"), (NT + 1) * L + i)
                else:
                    pe.wait_ge(sem("qn_ready"), L + 1)
                for h in range(MH):
                    for dc in range(2):
                        for a in range(2):
                            mm = pe.matmul(xo_ps[:, 2 * h + dc], mem_n[:, a, MD * h + P * dc:MD * h + P * (dc + 1)],
                                           pTx[:, i % 2, 2 * h + a], start=(a == 0), stop=(a == 1))
                mm.then_inc(sem("x_values"), 1)

            pe.wait_ge(sem("mkT_ready"), DC * (L + 1))
            pe.wait_ge(sem("mem_rows"), 16 * (L + 1) + 2)
            scores(0)
            for i in range(NT + 2):
                if i + 1 < NT:
                    scores(i + 1)
                if 1 <= i <= NT:
                    turn(i - 1)
                if i >= 2:
                    values(i - 2)
            pe.wait_ge(sem("smx_dve_step"), 5 * L + 4)
            pe.wait_ge(sem("x_exp"), MH * (N0 + NT))
            for b in range(DECB):
                pe.wait_ge(sem(f"mkv_loaded{b % 4}"), 16 * (4 * L + 2 + b // 4 + 1))
                for a in range(2):
                    for r in range(2):
                        mm = pe.matmul(ps[0:MH * DECB, r, :], smz[:, b, a].rearrange("p h b -> p (h b)"),
                                       mkv[:, b % 4, a, 512 * r:512 * (r + 1)], start=(b == 0 and a == 0),
                                       stop=(b == DECB - 1 and a == 1))
                mm.then_inc(sem("mv_used"), 1)
            pe.wait_ge(sem("smx_dve_step"), 5 * L + 5)
            for c in range(DC):
                mm = pe.matmul(ps[:, 2, DECB * c:DECB * (c + 1)], probx[0:MH * DECB, 0, P * c:P * (c + 1)], sel_b[:],
                               start=True, stop=True)
            mm.then_inc(sem("mv_used"), 1)

        def act_cross(act, L):
            N0 = NT * L
            act.wait_ge(tile_done, 2 * G1[f"xq{L}"])
            act.wait_ge(sem("qnT_ready"), L + 1)
            act.copy(qn[:], ps[0:DECB, 6:8, :].rearrange("p a n -> p (a n)")).then_inc(sem("qn_ready"), 1)
            act.wait_ge(sem("qn_ready"), L + 1)
            act.dma_start(qx_d[L], qn[:]).then_inc(sem("q_stored"), 16)
            for i in range(NT + 2):
                if i < NT:
                    act.wait_ge(sem("x_max"), N0 + i + 1)
                    if i >= 2:
                        act.wait_ge(sem("x_turned"), N0 + i - 1)
                        act.wait_ge(sem("x_prob"), N0 + i - 1)
                    for h in range(MH):
                        m = MH * (i % 2) + h
                        act.activation(probx[:, i % 2, NMEM * h:NMEM * (h + 1)],
                                       ps[:, 2 * (i % 2) + h // 2, NMEM * (h % 2):NMEM * (h % 2 + 1)], ACT.Exp,
                                       bias=nmax[:, m:m + 1], accum_out=rsum[:, m:m + 1]).then_inc(sem("x_exp"), 1)
                if 1 <= i <= NT:
                    act.wait_ge(sem("x_turned"), N0 + i)
                    if i >= 3:
                        act.wait_ge(sem("x_values"), N0 + i - 2)
                    act.copy(pTx[:, (i - 1) % 2], xT_ps).then_inc(sem("x_pT"), 1)
                if i >= 2:
                    act.wait_ge(sem("x_values"), N0 + i - 1)
                    act.copy(qx[:, :, P * (i - 2):P * (i - 1)], xo_ps).then_inc(sem("x_out"), 1)
                if i == NT:
                    act.wait_ge(sem("smx_dve_step"), 5 * L + 2)
                    act.activation(smx[:], smx[:], ACT.Exp).then_inc(sem("smx_exp"), 1)
            act.wait_ge(sem("mv_used"), (DECB + 1) * (L + 1))
            act.copy(qx[:, :, SEQ:TOK], ps[:, 2, 0:64].rearrange("p (c b) -> p c b", c=DC)).then_inc(sem("x_out"), 1)
            act.wait_ge(sem("x_out"), (NT + 1) * (L + 1))
            for k in range(DC):
                act.copy(xs[:, 0, k], qx[:, k]).then_inc(sem("xs_hi"), 1)

        def dve_cross(dve, L, hi0):
            N0 = NT * L
            then = chain(dve, f"dve_cross{L}")

            def keys(b):
                dve.wait_ge(sem(f"mkv_loaded{b % 4}"), 16 * (4 * L + b // 4 + 1))
                dve.wait_ge(sem(f"q_row_loaded{b % 2}"), 16 * (DECB // 2 * (L + 1) + b // 2 + 1))
                for a in range(2):
                    for h in range(MH):
                        kv = mkv[:, b % 4, a, MD * h:MD * (h + 1)]
                        ins = dve.tensor_tensor_reduce(kv, kv, qbx[:, b % 2, MD * h:MD * (h + 1)], 1.0, 0.0,
                                                       ALU.mult, ALU.add, smx[:, b, a, h:h + 1])
                ins.then_inc(sem("mk_used"), 1)

            for i in range(NT + 1):
                if i < NT:
                    dve.wait_ge(sem("x_scores"), N0 + i + 1)
                    if i >= 2:
                        dve.wait_ge(sem("x_exp"), MH * (N0 + i - 1))
                    dve.tensor_reduce(nmax[:, MH * (i % 2):MH * (i % 2 + 1)],
                                      ps[:, 2 * (i % 2):2 * (i % 2) + 2, :].rearrange("p a (h m) -> p (a h) m", m=NMEM),
                                      AX.X, ALU.max, negate=True).then_inc(sem("x_max"), 1)
                if i:
                    j = (i - 1) % 2
                    dve.wait_ge(sem("x_exp"), MH * (N0 + i))
                    then(dve.reciprocal(rinv[:, MH * j:MH * (j + 1)], rsum[:, MH * j:MH * (j + 1)]))
                    pv = probx[:, j].rearrange("p (h m) -> p h m", h=MH)
                    dve.tensor_tensor(pv, pv, rinv[:, MH * j:MH * (j + 1)].unsqueeze(2).to_broadcast([P, MH, NMEM]),
                                      ALU.mult).then_inc(sem("x_prob"), 1)
                if i < NT:
                    keys(i)
            dve.wait_ge(sem("mk_used"), DECB * (L + 1))
            flat = "p b a h -> p b h a"
            then(dve.tensor_reduce(smr[:, 0], smx[:].rearrange(flat), AX.X, ALU.max))
            dve.sem_inc(sem("smx_dve_step"), 1)
            dve.wait_ge(sem("smx_pool_step"), 3 * L + 2)
            dve.tensor_tensor(smx[:], smx[:], smr[:, 1].unsqueeze(2).to_broadcast([P, DECB, 2, MH]),
                              ALU.subtract).then_inc(sem("smx_dve_step"), 1)
            dve.wait_ge(sem("smx_exp"), L + 1)
            then(dve.tensor_reduce(smr[:, 2], smx[:].rearrange(flat), AX.X, ALU.add))
            dve.sem_inc(sem("smx_dve_step"), 1)
            dve.wait_ge(sem("smx_pool_step"), 3 * L + 3)
            then(dve.reciprocal(smr[:, 3], smr[:, 3]))
            for b in range(DECB):
                ins = dve.tensor_tensor(smz[:, b, :, :, b], smx[:, b], smr[:, 3, b].unsqueeze(1).to_broadcast([P, 2, MH]), ALU.mult)
            ins.then_inc(sem("smx_dve_step"), 1)
            dve.wait_ge(sem("mv_used"), (DECB + 1) * L + DECB)
            dve.wait_ge(sem("x_turned"), NT * (L + 1))
            dve.tensor_tensor(probx[0:MH * DECB, 0].rearrange("p (h d) -> p h d", h=MH),
                              ps[0:MH * DECB, 0:2, :].rearrange("p a (h d) -> p (a h) d", d=MD),
                              own_x[:], ALU.mult).then_inc(sem("smx_dve_step"), 1)
            for k in range(DC):
                split_act_lo(dve, k, qx[:, k], hi0 + k + 1)

        def pool_cross(pool, L):
            then = chain(pool, "pool_")
            pool.wait_ge(sem("q_stored"), 16 * (L + 3))
            then(pool.memset(smz[:], 0.0))
            then(pool.memset(own_x[:], 1.0))
            then(pool.affine_select(out=own_x[:], in_=own_x[:], compare_op=ALU.is_ge, fill=0.0, base=0,
                                    pattern=[[-DECB, MH], [0, MD]], channel_multiplier=1))
            pool.affine_select(out=own_x[:], in_=own_x[:], compare_op=ALU.is_ge, fill=0.0, base=DECB - 1,
                               pattern=[[DECB, MH], [0, MD]], channel_multiplier=-1).then_inc(sem("smx_pool_step"), 1)
            pool.wait_ge(sem("smx_dve_step"), 5 * L + 1)
            pool.partition_all_reduce(smr[:, 1], smr[:, 0], P, RMAX).then_inc(sem("smx_pool_step"), 1)
            pool.wait_ge(sem("smx_dve_step"), 5 * L + 3)
            pool.partition_all_reduce(smr[:, 3], smr[:, 2], P, RADD).then_inc(sem("smx_pool_step"), 1)

        def act_norm(act, ln):
            act_norm_stats(act, ln)
            loop(act, DC, lambda k: act_norm_affine(act, ln, k))

        def pool_norm(pool, ln):
            loop(pool, DC, lambda k: pool_norm_shift(pool, ln, k))

        def dve_norm(dve, ln):
            dve_norm_stats(dve, ln)
            dve_norm_scale(dve, ln, 0)

            def body(k):
                dve_norm_scale(dve, ln, k + 1)
                dve_norm_lo(dve, ln, k)
            loop(dve, DC - 1, body)
            dve_norm_lo(dve, ln, DC - 1)

        def ff_base(L, q):
            return FFC * L + sum(FF_GROUPS[:q])

        def sp_ff(sp, L):
            wg, wu, wd = kview(A["w_gate"][L]), kview(A["w_up"][L]), A["w_down"][L]
            for q, nc_ in enumerate(FF_GROUPS):
                c0 = sum(FF_GROUPS[:q])
                sp_stream(sp, f"gu{L}_{q}", lambda i: (wg[:, :, ds(P * (c0 + i), P)], wu[:, :, ds(P * (c0 + i), P)]))
                v = kview(wd, (P * c0, P * (c0 + nc_)))
                sp_stream(sp, f"down{L}_{q}", lambda i: (v[:, :, ds(256 * i, P)], v[:, :, ds(256 * i + P, P)]), nk=nc_)

        def pe_ff(pe, L):
            for q, n in enumerate(FF_GROUPS):
                pe_stream(pe, f"gu{L}_{q}", xs, split=(sem("ln_lo"), DC * (3 * L + 1)) if q == 0 else None)
                pe.wait_ge(sem("ff_lo"), ff_base(L, q) + n + 1)
                pe_stream(pe, f"down{L}_{q}", hs, nk=n)

        def act_ff(act, L):
            for q, n in enumerate(FF_GROUPS):
                j0 = ff_base(L, q)

                def evac(s, i, g):
                    if s == 0:
                        act.wait_ge(set_free[1], g)
                        settle(act)
                        act.activation(blocks(sq[:]), ps_set[0], ACT.Silu).then_inc(set_free[0], 1)
                    else:
                        act.wait_ge(set_free[1], g + 1)
                        settle(act)
                        act.copy(hs[:, 0, ds(i, 1)].rearrange("p a n -> p (a n)"), sum_x[:]).then_inc(sem("ff_hi"), 1)
                act_stream(act, f"gu{L}_{q}", evac)
                act_stream(act, f"down{L}_{q}", act_square(3 * L + 2) if q == 2 else None)

        def dve_ff(dve, L):
            dve.wait_ge(sem("ln_shifted"), DC * (3 * L + 2))
            for q, n in enumerate(FF_GROUPS):
                j0 = ff_base(L, q)

                def evac(s, i, g):
                    if s == 0:
                        return
                    dve.wait_ge(set_free[0], g + 1)
                    dve.wait_ge(tile_done, 2 * g + 2)
                    dve.wait_ge(sem("ff_hi"), j0 + i + 1)
                    dve.wait_ge(sem("ff_lo"), j0 + i + 1)
                    dve.tensor_tensor(blocks(sum_x[:]), blocks(sq[:]), ps_set[1], ALU.mult).then_inc(set_free[1], 1)
                    dve.wait_ge(sem("ff_hi"), j0 + i + 2)
                    dve.tensor_tensor(hs[:, 1, ds(i, 1)].rearrange("p a n -> p (a n)"), sum_x[:],
                                      hs[:, 0, ds(i, 1)].bitcast(F32).rearrange("p a n -> p (a n)"),
                                      ALU.subtract).then_inc(sem("ff_lo"), 1)
                dve_stream(dve, f"gu{L}_{q}", evac)
                dve_stream(dve, f"down{L}_{q}", dve_residual(False, q == 0))

        def pe_output(pe):
            for n, (t0, m) in enumerate(tiles):
                if n >= 2:
                    pe.wait_ge(sem("xT_copied"), len(tiles) + n - 1)
                for c in range(DC):
                    mm = pe.transpose(ps[0:m, 2 * (n % 2) + c // 4, P * (c % 4):P * (c % 4 + 1)], x[:, c, t0:t0 + m], ident[:])
                mm.then_inc(sem("xT_ready"), 1)

        def act_output(act):
            for n, (t0, m) in enumerate(tiles):
                act.wait_ge(sem("xT_ready"), len(tiles) + n + 1)
                if n >= 2:
                    act.wait_ge(sem(f"rows_stored{n % 2}"), 16 * (NT // 2 + n // 2))
                b = 2 * (n % 2)
                act.copy(xin[0:m, n % 2], ps[0:m, b:b + 2, :].rearrange("p a n -> p (a n)")).then_inc(sem("xT_copied"), 1)
                act.wait_ge(sem("xT_copied"), len(tiles) + n + 1)
                dst = O["y_prompt"][0, t0:t0 + m, :] if n < NT else O["y_sample"][:, 0, :]
                act.dma_start(dst, xin[0:m, n % 2]).then_inc(sem(f"rows_stored{n % 2}"), 16)
            act.wait_ge(sem("rows_stored0"), 16 * (NT // 2 + 5))
            act.wait_ge(sem("rows_stored1"), 16 * (NT // 2 + 4))

        spill_d = scratch("spill_d", [16, P, TOK])
        acs_d = scratch("acs_d", [SH, SEQ])
        ends_d = scratch("ends_d", [SH, NT])
        sd_d = scratch("sd_d", [2, SH, DECB])
        bc_d = scratch("bc_d", [DECB, 2 * SG * SN])
        CD_COL = {"cd_z": 0, "cd_gu": SI + CCH + SH, "cd_xbc": SI, "cd_gv": SI + CCH + SH + GW}
        SPILL = {"cd_z": (0, 0, ACT.Silu), "cd_gu": (8, 4, ACT.Gelu_apprx_tanh), "cd_gv": (12, 6, ACT.Gelu_apprx_tanh)}
        spilled = [sem("spilled0"), sem("spilled1")]
        wcd = kview(A["w_in_cd"][0])
        flat = work[:].rearrange("p a n -> p (a n)")
        wv = [flat[:, TOK * i:TOK * (i + 1)] for i in range(3)]

        def cd_src(name):
            c0 = CD_COL[name]
            return lambda i: (wcd[:, :, ds(c0 + 256 * i, P)], wcd[:, :, ds(c0 + 256 * i + P, P)])

        def sp_cd_in(sp):
            sp.wait_ge(sem("ln_lo"), DC * 3)
            sp.dma_start(work_state, A["state_conv"][0].rearrange("b j c -> (b j) c")).then_inc(sem("w_small_in"), 16)
            sp.dma_start(w_small[:], wcd[:, :, SI + CCH:SI + CCH + SH]).then_inc(sem("w_small_in"), 16)
            for r in range(2):
                with nc.allow_non_contiguous_dma(reason="16 values"):
                    sp.dma_start(dskip[SD * r:SD * (r + 1)], A["d_skip"][0].rearrange("(c r) -> r c", r=2)[r:r + 1].to_broadcast([SD, DC])
                                 ).then_inc(sem("w_small_in"), 16)
            sp.dma_start(O["conv_state_sample"][0, :, 0:CONVW - 2], A["state_conv"][0, :, 1:CONVW - 1]).then_inc(sem("stored"), 16)
            for name in ("cd_z", "cd_gu", "cd_xbc", "cd_gv"):
                sp_stream(sp, name, cd_src(name), skip=(name == "cd_z"))

        work_state = flat[0:DECB * (CONVW - 1), 0:CCH]

        def pe_cd_in(pe):
            pe.wait_ge(sem("w_small_in"), 128)
            n = DECB * (CONVW - 1)
            for c in range(12):
                mm = pe.transpose(ps[:, 6, n * c:n * (c + 1)], work_state[:, P * c:P * (c + 1)], ident[0:n, 0:n])
            mm.then_inc(pe_steps, mark("convT_turned"))
            for name in ("cd_z", "cd_gu", "cd_xbc", "cd_gv"):
                pe_stream(pe, name, xs, split=(sem("ln_lo"), DC * 2) if name == "cd_z" else None)

        def act_cd_in(act):
            act.wait_ge(pe_steps, step("convT_turned"))
            act.copy(convT[:], ps[:, 6, 0:288].rearrange("p (c b j) -> p c b j", c=12, b=DECB)).then_inc(act_steps, mark("convT_ready"))

            def spill(name):
                c0, m0, func = SPILL[name]

                def evac(s, i, g):
                    act.wait_ge(spilled[s], 16 * (m0 + i + 1))
                    if name == "cd_gv":
                        act.wait_ge(sem("conv_done"), 12)
                    settle(act)
                    act.activation(blocks(acc[:, s]), ps_set[s], func).then_inc(set_free[s], 1)
                    act.wait_ge(set_free[s], g + 1)
                    act.dma_start(spill_d[ds(c0 + 2 * i + s, 1)].rearrange("a p n -> (a p) n"), acc[:, s]).then_inc(spilled[s], 16)
                act_stream(act, name, evac)
            spill("cd_z")
            spill("cd_gu")

            def conv_out(c, s):
                settle(act, 5 - s)
                act.wait_ge(sem("conv_sum"), c + 1)
                act.activation(chunk(xbc, c), acc[:, s], ACT.Silu).then_inc(sem("conv_done"), 1)

            g0 = G0["cd_xbc"]

            def body(i, first=False):
                for s in range(2):
                    g, c = g0 + i, 2 * i + s
                    split_hi(act, 1 - s, g + s)
                    act.wait_ge(tile_done, 2 * g + s + 1)
                    settle(act, s)
                    act.activation(blocks(chunk(xbc, c)), ps_set[s], ACT.Copy).then_inc(sem("raw_ready"), 1)
                    if first:
                        act.wait_ge(spilled[s], 16 * 7)
                    else:
                        act.wait_ge(sem("conv_done"), c - 1)
                    settle(act, 2 + s)
                    act.activation(blocks(acc[:, s]), ps_set[s], ACT.Identity,
                                   bias=cols[:, ds(COL["conv_b"] + c, 1)],
                                   scale=cols[:, ds(COL["conv_w"] + 36 + c, 1)]).then_inc(set_free[s], 1)
                    if not (first and s == 0):
                        conv_out(c - 1, 1 - s)
            body(0, first=True)
            loop(act, 5, lambda i: body(i + 1))
            conv_out(11, 1)
            spill("cd_gv")

        def dve_cd_in(dve):
            dve_stream(dve, "cd_z")
            dve_stream(dve, "cd_gu")
            g0 = G0["cd_xbc"]
            dve.wait_ge(act_steps, step("convT_ready"))

            def taps(s, i, g):
                c = 2 * i + s
                dve.wait_ge(sem("raw_ready"), c + 1)
                dve.wait_ge(set_free[s], g + 1)
                raw = chunk(xbc, c)
                dve.tensor_copy(tail[:, ds(c, 1)].rearrange("p a n -> p (a n)"), raw[:, SEQ - CONVW + 1:TOK]).then_inc(sem("tail_ready"), 1)
                for j in range(1, CONVW):
                    w = cols[:, ds(COL["conv_w"] + 12 * (CONVW - 1 - j) + c, 1)]
                    m = 3 * c + j
                    if j > 1:
                        dve.wait_ge(sem("tap_done"), 2 * m - 2)
                    dve.scalar_tensor_tensor(out=acc[:, s, j:SEQ], in0=raw[:, 0:SEQ - j], scalar=w, in1=acc[:, s, j:SEQ],
                                             op0=ALU.mult, op1=ALU.add).then_inc(sem("tap_done"), 1)
                    st = convT[:, ds(c, 1), :, CONVW - 1 - j].rearrange("p a b -> p (a b)")
                    dve.scalar_tensor_tensor(out=acc[:, s, SEQ:TOK], in0=st, scalar=w, in1=acc[:, s, SEQ:TOK],
                                             op0=ALU.mult, op1=ALU.add).then_inc(sem("tap_done"), 1)
                dve.wait_ge(sem("tap_done"), 6 * c + 6)
                dve.sem_inc(sem("conv_sum"), 1)
            dve_stream(dve, "cd_xbc", taps)
            dve_stream(dve, "cd_gv")

        def pe_cd_prep(pe):
            pe.wait_ge(set_free[0], G1["cd_gv"])
            for k in range(DC):
                for t in range(NB):
                    mm = pe.matmul(ps[0:SH, t, 0:TB], w_small[:, k], x[:, k, TB * t:TB * (t + 1)],
                                   start=(k == 0), stop=(k == DC - 1))
            mm.then_inc(pe_steps, mark("dt_logits"))
            pe.wait_ge(set_free[1], G1["cd_gv"])
            pe.wait_ge(sem("tail_ready"), 12)
            for c in range(12):
                mm = pe.transpose(ps[0:CONVW - 1 + DECB, 3 + c // 4, P * (c % 4):P * (c % 4 + 1)], tail[:, c], ident[:])
            mm.then_inc(pe_steps, mark("tailT_ready"))
            pe.wait_ge(sem("conv_done"), 12)
            for q in range(4):
                g, i0 = q // 2, 4 * (q % 2)
                if q:
                    pe.wait_ge(sem("cb_ready"), q)
                for i in range(i0, i0 + 4):
                    cols_ = slice(P * i, P * (i + 1))
                    mm = pe.matmul(ps[:, 7, P * (i - i0):P * (i - i0 + 1)], xbc[:, 8 + g, cols_], xbc[:, 10 + g, cols_],
                                   start=True, stop=True)
                mm.then_inc(sem("cb_products"), 1)
            pe.wait_ge(act_steps, step("ctail_ready"))
            for c in range(4):
                mm = pe.transpose(ps[0:DECB, 3, P * c:P * (c + 1)], xbc[:, 8 + c, SEQ:TOK], ident[:])
            mm.then_inc(pe_steps, mark("s_bcT_ready"))
            pe.wait_ge(dve_steps, step("acs_ready"))
            for w in range(2):
                for i in range(NT):
                    o = SH * (NT * w + i)
                    mm = pe.transpose(ps[:, 6, o:o + SH], rows16[:, 4 * w, P * i:P * (i + 1)], ident[0:SH, 0:SH])
            mm.then_inc(pe_steps, mark("dtT_ready"))
            pe.wait_ge(act_steps, step("dt_row"))
            pe.wait_ge(act_steps, step("s_bc_ready"))
            for i in range(NT):
                if i >= 2:
                    pe.wait_ge(sem("xdt_ready"), i - 1)
                    pe.wait_ge(sem("b_nat_ready"), i - 1)
                b = 2 * (i % 2)
                for c in range(DC):
                    pe.transpose(ps[:, b + c // 4, P * (c % 4):P * (c % 4 + 1)], xbc[:, c, P * i:P * (i + 1)], ident[:])
                for g in range(SG):
                    mm = pe.transpose(ps[:, 4 + i % 2, P * g:P * (g + 1)], xbc[:, 8 + g, P * i:P * (i + 1)], ident[:])
                mm.then_inc(sem("xT_nat"), 1)

        def act_cd_prep(act):
            then = chain(act, "act_")
            act.wait_ge(pe_steps, step("dt_logits"))
            act.wait_ge(tile_done, 2 * G1["cd_gv"])
            then(act.activation(blocks(rows16[:, 0, :]), ps[0:SH, 0:NB, 0:TB], ACT.Identity, bias=tiny[0:SH, 1:2]))
            act.sem_inc(act_steps, mark("dt_row"))
            then(act.activation(rows16[:, 1, :], rows16[:, 0, :], ACT.Abs))
            then(act.activation(rows16[:, 1, :], rows16[:, 1, :], ACT.Exp, scale=-1.0))
            then(act.activation(tiny[0:SH, 3:4], tiny[0:SH, 2:3], ACT.Exp))
            act.activation(rows16[:, 2, :], rows16[:, 1, :], ACT.Ln, bias=1.0).then_inc(act_steps, mark("dt_ln"))
            act.wait_ge(pe_steps, step("tailT_ready"))
            act.copy(ctail[:].rearrange("p (a n) -> p a n", a=3), ps[0:CONVW - 1 + DECB, 3:6, :]).then_inc(act_steps, mark("ctail_ready"))
            act.wait_ge(act_steps, step("ctail_ready"))
            act.dma_start(O["conv_state_prompt"][0, 0], ctail[0:CONVW - 1]).then_inc(sem("stored"), 16)
            act.dma_start(O["conv_state_sample"][0, :, CONVW - 2], ctail[CONVW - 1:]).then_inc(sem("stored"), 16)
            act.wait_ge(pe_steps, step("s_bcT_ready"))
            act.copy(rows16[0:DECB, 3, 0:512], ps[0:DECB, 3, :]).then_inc(act_steps, mark("s_bc_ready"))
            act.wait_ge(act_steps, step("s_bc_ready"))
            act.dma_start(bc_d, rows16[0:DECB, 3, 0:512]).then_inc(sem("cd_rows_out"), 16)
            act.wait_ge(dve_steps, step("acs_ready"))
            then(act.activation(rows16[:, 5, 0:DECB], rows16[:, 5, 8:16], ACT.Exp))
            act.dma_start(acs_d, rows16[:, 4, 0:SEQ]).then_inc(sem("cd_rows_out"), 16)
            act.dma_start(sd_d[0], rows16[:, 0, SEQ:TOK]).then_inc(sem("cd_rows_out"), 16)
            act.dma_start(sd_d[1], rows16[:, 5, 0:DECB]).then_inc(sem("cd_rows_out"), 16)
            with nc.allow_non_contiguous_dma(reason="128 values"):
                act.dma_start(ends_d, rows16[:, 4, P - 1:SEQ:P]).then_inc(sem("cd_rows_out"), 16)
            act.wait_ge(pe_steps, step("dtT_ready"))
            act.copy(dtn[:], ps[:, 6, 0:2 * NT * SH].rearrange("p (w i h) -> p w i h", w=2, h=SH)).then_inc(act_steps, mark("dtn_ready"))
            act.wait_ge(act_steps, step("dtn_ready"))
            for i in range(NT):
                act.wait_ge(sem("xT_nat"), i + 1)
                act.copy(b_nat[:, i], ps[:, 4 + i % 2, 0:2 * SN]).then_inc(sem("b_nat_ready"), 1)
            act.wait_ge(dve_steps, step("dec_diff"))
            act.activation(dec_end[:], dec_end[:], ACT.Exp).then_inc(sem("dec_ready"), 1)
            act.activation(dec_chunk[:], ends[:], ACT.Exp).then_inc(sem("dec_ready"), 1)

        def dve_cd_prep(dve):
            then = chain(dve, "dve_")
            dve.wait_ge(act_steps, step("dt_ln"))
            log1p_fix(dve, then, rows16[:, 1, :], rows16[:, 2, :], rows16[:, 4, :], rows16[:, 5, :])
            then(dve.scalar_tensor_tensor(out=rows16[:, 0, :], in0=rows16[:, 0, :], scalar=0.0, in1=rows16[:, 2, :],
                                          op0=ALU.max, op1=ALU.add))
            then(dve.tensor_scalar(rows16[:, 2, :], rows16[:, 0, :], tiny[0:SH, 3:4], -1.0, ALU.mult, ALU.mult))
            then(dve.memset(rows16[:, 1, :], 1.0))
            then(dve.tensor_copy(rows16[:, 5, 8:16], rows16[:, 2, SEQ:TOK]))
            for i in range(NT):
                b = slice(P * i, P * (i + 1))
                ins = dve.tensor_tensor_scan(rows16[:, 4, b], rows16[:, 1, b], rows16[:, 2, b], 0.0, ALU.mult, ALU.add)
            ins.then_inc(dve_steps, mark("acs_ready"))
            for q in range(4):
                g, i0 = q // 2, 4 * (q % 2)
                dve.wait_ge(sem("cb_products"), q + 1)
                dve.tensor_tensor(cbT[:, g, i0:i0 + 4], ps[:, 7, :].rearrange("p (i n) -> p i n", n=P),
                                  causal[:].unsqueeze(1).to_broadcast([P, 4, P]), ALU.mult).then_inc(sem("cb_ready"), 1)
            dve.wait_ge(act_steps, step("dtn_ready"))
            dve.wait_ge(sem("ends_in"), 80)
            dve.tensor_tensor(dec_end[:], ends[:].rearrange("p h i -> p i h"), dtn[:, 1], ALU.subtract).then_inc(dve_steps, mark("dec_diff"))
            dve.wait_ge(sem("rows16_stored"), 1)
            for i in range(NT):
                dve.wait_ge(sem("xT_nat"), i + 1)
                b = 2 * (i % 2)
                dve.tensor_tensor(xdt[:, i].rearrange("p (h d) -> p h d", h=SH),
                                  ps[:, b:b + 2, :].rearrange("p a (h d) -> p (a h) d", d=SD),
                                  dtn[:, 0, i].unsqueeze(2).to_broadcast([P, SH, SD]), ALU.mult).then_inc(sem("xdt_ready"), 1)

        def sp_cd_prep(sp):
            sp.wait_ge(sem("cd_rows_out"), 80)
            sp.dma_start(ends[:].rearrange("p h i -> p (h i)"), ends_d.rearrange("h i -> (h i)").unsqueeze(0).to_broadcast([P, SH * NT])
                         ).then_inc(sem("ends_in"), 16)
            for w in range(2):
                for r in range(2):
                    sp.dma_start(sdt[SD * r:SD * (r + 1), w],
                                 sd_d[w].rearrange("(c r) b -> r c b", r=2)[r:r + 1].to_broadcast([SD, DC, DECB])).then_inc(sem("ends_in"), 16)
            sp.wait_ge(pe_steps, step("dtT_ready"))
            sp.wait_ge(sem("stored"), 16 * N_STORED_CD)
            sp.sem_inc(sem("rows16_stored"), 1)

        def dve_states(dve):
            then = chain(dve, "dve_")
            dve.wait_ge(sem("dec_ready"), 2)
            dve.wait_ge(spilled[0], 16 * 9)
            dve.wait_ge(spilled[1], 16 * 9)
            dve.wait_ge(sem("xdt_ready"), NT)

            def weigh(i):
                if i >= 2:
                    dve.wait_ge(sem("state_products"), i - 1)
                dve.tensor_tensor(acc[:, i % 2, 0:SI].rearrange("p (h d) -> p h d", h=SH), xdt[:, i].rearrange("p (h d) -> p h d", h=SH),
                                  dec_end[:, i].unsqueeze(2).to_broadcast([P, SH, SD]), ALU.mult).then_inc(sem("weighed"), 1)
            weigh(0)
            for i in range(NT):
                if i + 1 < NT:
                    weigh(i + 1)
                h = hprev[:, i].rearrange("p (h d) -> p h d", h=SH)
                if i:
                    dve.wait_ge(sem("state_ready"), i)
                    then(dve.tensor_tensor(h, hprev[:, i - 1].rearrange("p (h d) -> p h d", h=SH),
                                      dec_chunk[:, :, i].unsqueeze(2).to_broadcast([P, SH, SD]), ALU.mult))
                dve.wait_ge(sem("state_products"), i + 1)
                b = 4 + 2 * (i % 2)
                src = ps[:, b:b + 2, :].rearrange("p a (h d) -> p (a h) d", d=SD)
                if i:
                    dve.tensor_tensor(h, h, src, ALU.add).then_inc(sem("state_ready"), 1)
                else:
                    dve.tensor_copy(h, src).then_inc(sem("state_ready"), 1)

        def pe_states(pe):
            pe.wait_ge(sem("b_nat_ready"), NT)
            pe.wait_ge(act_steps, step("dtn_ready"))
            pe.wait_ge(sem("cb_ready"), 4)
            for i in range(NT):
                pe.wait_ge(sem("weighed"), i + 1)
                if i >= 2:
                    pe.wait_ge(sem("state_ready"), i - 1)
                for g in range(SG):
                    mm = pe.matmul(ps[:, 4 + 2 * (i % 2) + g, :], b_nat[:, i, SN * g:SN * (g + 1)], acc[:, i % 2, 512 * g:512 * (g + 1)],
                                   start=True, stop=True)
                mm.then_inc(sem("state_products"), 1)
            pe.wait_ge(sem("state_ready"), NT)
            pe.wait_ge(sem("xdt_ready"), NT)
            for c in range(DC):
                mm = pe.transpose(ps[:, 4 + c // 4, P * (c % 4):P * (c % 4 + 1)], hprev[:, NT - 1, P * c:P * (c + 1)], ident[:])
            mm.then_inc(pe_steps, mark("lastT_ready"))

        def act_states(act):
            act.wait_ge(pe_steps, step("lastT_ready"))
            act.copy(work[:, 0], ps[:, 4:6, :].rearrange("p a n -> p (a n)")).then_inc(act_steps, mark("last_ready"))
            act.wait_ge(act_steps, step("last_ready"))
            act.dma_start(O["ssm_state_prompt"][0, 0].rearrange("(c r) p n -> (r p) c n", r=2),
                          work[:, 0].rearrange("p (c n) -> p c n", c=DC)).then_inc(sem("last_stored"), 16)

        m_buf = [acc[:, 0, 0:SEQ], acc[:, 1, 0:SEQ], hprev[:, NT - 1]]
        ce_buf = [xbc[:, 8, 0:SEQ], xbc[:, 9, 0:SEQ]]

        def tiled(ap):
            return ap.rearrange("p (i n) -> p i n", n=P)

        def sp_heads(sp):
            sp.wait_ge(sem("last_stored"), 16)
            for h in range(SH):
                if h >= 2:
                    sp.wait_ge(sem("head_exp"), h - 1)
                    sp.wait_ge(sem("head_diff"), h - 1)
                sp.dma_start(work[:, h % 2], acs_d[h:h + 1, :].to_broadcast([P, SEQ])).then_inc(sem(f"row_loaded{h % 2}"), 16)

        def act_heads(act):
            def e(h):
                act.wait_ge(sem(f"row_loaded{h % 2}"), 16 * (FH // 2 + h // 2 + 1))
                if h >= 2:
                    act.wait_ge(sem("head_products"), h - 1)
                act.activation(ce_buf[h % 2], work[:, h % 2], ACT.Exp).then_inc(sem("head_exp"), 1)
            e(0)
            for h in range(SH):
                if h + 1 < SH:
                    e(h + 1)
                act.wait_ge(sem("head_min"), h + 1)
                act.activation(m_buf[h % 3], m_buf[h % 3], ACT.Exp).then_inc(sem("head_seg"), 1)

        def pool_heads(pool):
            for h in range(SH):
                pool.wait_ge(sem("head_diff"), h + 1)
                pool.tensor_scalar(m_buf[h % 3], m_buf[h % 3], 0.0, None, ALU.min).then_inc(sem("head_min"), 1)

        def dve_heads(dve):
            dve.wait_ge(sem("state_products"), NT)

            def diff(h):
                dve.wait_ge(sem(f"row_loaded{h % 2}"), 16 * (FH // 2 + h // 2 + 1))
                if h == 2:
                    dve.wait_ge(pe_steps, step("lastT_ready"))
                if h >= 3:
                    dve.wait_ge(sem("head_products"), h - 2)
                dve.tensor_tensor(tiled(m_buf[h % 3]), tiled(work[:, h % 2]),
                                  dtn[:, 1, :, h].unsqueeze(2).to_broadcast([P, NT, P]), ALU.subtract).then_inc(sem("head_diff"), 1)

            def y(c):
                dve.wait_ge(sem("head_products"), 2 * c + 2)
                b = 2 * (c % 4)
                dve.scalar_tensor_tensor(out=xbc[:, c, 0:SEQ], in0=xbc[:, c, 0:SEQ], scalar=dskip[:, c:c + 1],
                                         in1=ps[:, b:b + 2, :].rearrange("p a n -> p (a n)"),
                                         op0=ALU.mult, op1=ALU.add).then_inc(sem("y_ready"), 1)
            diff(0)
            for h in range(SH):
                g = h // (SH // SG)
                if h + 1 < SH:
                    diff(h + 1)
                dve.wait_ge(sem("head_exp"), h + 1)
                dve.tensor_tensor(ce_buf[h % 2], ce_buf[h % 2], xbc[:, 10 + g, 0:SEQ], ALU.mult).then_inc(sem("ce_ready"), 1)
                dve.wait_ge(sem("head_seg"), h + 1)
                dve.tensor_tensor(tiled(m_buf[h % 3]), tiled(m_buf[h % 3]), cbT[:, g], ALU.mult).then_inc(sem("m_ready"), 1)
                if h % 2 and h > 1:
                    y(h // 2 - 1)
            y(SH // 2 - 1)

        def pe_heads(pe):
            for h in range(SH):
                c = h // 2
                rs = slice(SD * (h % 2), SD * (h % 2 + 1))
                if h == 4:
                    pe.wait_ge(act_steps, step("last_ready"))
                if h % 2 == 0 and c >= 4:
                    pe.wait_ge(sem("y_ready"), c - 3)
                pe.wait_ge(sem("ce_ready"), h + 1)
                pe.wait_ge(sem("m_ready"), h + 1)
                for i in range(NT):
                    out = ps[rs, 2 * (c % 4) + i // 4, P * (i % 4):P * (i % 4 + 1)]
                    cs = slice(SD * h, SD * (h + 1))
                    mm = pe.matmul(out, xdt[:, i, cs], m_buf[h % 3][:, P * i:P * (i + 1)], start=True, stop=(i == 0))
                    if i:
                        mm = pe.matmul(out, hprev[:, i - 1, cs], ce_buf[h % 2][:, P * i:P * (i + 1)], start=False, stop=True)
                mm.then_inc(sem("head_products"), 1)

        w_sp = xbc[:, 9, 0:GW].rearrange("p (g n) -> p g n", g=4)
        wmT = xbc[:, 8, 0:GW].rearrange("p (g n) -> p g n", g=4)
        b_sp = xbc[:, 8, GW:2 * GW].rearrange("p (g n) -> p g n", g=4)
        first_w = xbc[:, 9, GW:GW + 4]
        first_b = xbc[:, 9, GW + 4:GW + 8]
        s_tmp = xbc[:, 9, GW + 8:GW + 40].rearrange("p (g b) -> p g b", g=4)
        v_row = xbc[0:DECB, 10, 0:GW]
        bcb = flat.rearrange("p (b n) -> p b n", b=DECB)
        ssm_view = "b (c r) p n -> (r p) b c n"

        def sp_gmlp(sp):
            sp.wait_ge(sem("head_products"), SH)
            for e, buf in ((12, gv), (8, gu)):
                sp.dma_start(buf[:], spill_d[e:e + 4].rearrange("c p n -> p c n")).then_inc(sem("gmlp_in"), 16)
            sp.dma_start(w_sp, A["w_spatial"][0].rearrange("g t s -> t g s")).then_inc(sem("gmlp_in"), 16)
            sp.dma_start(b_sp.rearrange("p g n -> p (g n)"), A["b_spatial"][0].rearrange("g n -> (g n)").unsqueeze(0).to_broadcast([P, GW])).then_inc(sem("gmlp_in"), 16)
            with nc.allow_non_contiguous_dma(reason="8 values"):
                sp.dma_start(first_w, A["w_spatial"][0, :, 0, 0:1].rearrange("g a -> a g").to_broadcast([P, 4])).then_inc(sem("gmlp_in"), 16)
                sp.dma_start(first_b, A["b_spatial"][0, :, 0:1].rearrange("g a -> a g").to_broadcast([P, 4])).then_inc(sem("gmlp_in"), 16)
            sp.dma_start(sst[:].rearrange("p b c n -> p (b c) n"), A["state_ssm"][0].rearrange("b (c r) p n -> (r p) (b c) n", r=2)).then_inc(sem("sst_in"), 16)
            sp.wait_ge(sem("g_shift"), 1 + 4)
            sp.dma_start(bcb, bc_d.rearrange("b n -> (b n)").unsqueeze(0).to_broadcast([P, DECB * GW])).then_inc(sem("bcb_in"), 16)
            sp.wait_ge(sem("sst_done"), DECB)
            sp.dma_start(O["ssm_state_sample"][0].rearrange("b (c r) p n -> (r p) (b c) n", r=2), sst[:].rearrange("p b c n -> p (b c) n")).then_inc(sem("sst_stored"), 16)
            for c in range(DC):
                sp.wait_ge(sem("sst_done"), DECB)
                if c >= 2:
                    sp.wait_ge(sem("y_gated"), c - 1)
                sp.dma_start(acc[:, c % 2], spill_d[c]).then_inc(sem(f"row_loaded{c % 2}"), 16)

        def pe_gmlp(pe):
            pe.wait_ge(sem("gmlp_in"), 96)
            pe.wait_ge(sem("y_ready"), DC)
            for k in range(4):
                for t in range(NB):
                    pe.matmul(ps_set[0][:, t], ones[:], gv[:, k, TB * t:TB * (t + 1)], start=(k == 0), stop=(k == 3))
            for k in range(4):
                pe.wait_ge(sem("gv_sq"), k + 1)
                for t in range(NB):
                    mm = pe.matmul(ps_set[1][:, t], ones[:], acc[:, k % 2, TB * t:TB * (t + 1)], start=(k == 0), stop=(k == 3))
                mm.then_inc(sem("g_sq_used"), 1)
            for g in range(4):
                mm = pe.transpose(ps[:, 6, P * g:P * (g + 1)], w_sp[:, g], ident[:])
            mm.then_inc(pe_steps, mark("wmT_turned"))
            pe.wait_ge(sem("v_ready"), 4)
            pe.wait_ge(dve_steps, step("wmT_ready"))
            for c in range(4):
                mm = pe.transpose(ps[0:DECB, 7, P * c:P * (c + 1)], gv[:, c, SEQ:TOK], ident[:])
            mm.then_inc(pe_steps, mark("v_rowT"))

            def turn(i):
                if i >= 2:
                    pe.wait_ge(sem("v_nat"), i - 1)
                for c in range(4):
                    mm = pe.transpose(ps[:, i % 2, P * c:P * (c + 1)], gv[:, c, P * i:P * (i + 1)], ident[:])
                mm.then_inc(sem("v_turned"), 1)
            turn(0)
            for i in range(NT):
                if i + 1 < NT:
                    turn(i + 1)
                pe.wait_ge(sem("v_nat"), i + 1)
                if i >= 2:
                    pe.wait_ge(sem("sg_used"), i - 1)
                for g in range(4):
                    mm = pe.matmul(ps[:, 4 + i % 2, P * g:P * (g + 1)], acc[:, i % 2, P * g:P * (g + 1)], wmT[:, g], start=True, stop=True)
                mm.then_inc(sem("sg_ready"), 1)

        def act_gmlp(act):
            act.wait_ge(sem("gmlp_in"), 96)
            act.wait_ge(sem("m_ready"), SH)
            act.wait_ge(sem("head_products"), SH)
            for k in range(4):
                if k >= 2:
                    act.wait_ge(sem("g_sq_used"), k - 1)
                act.activation(acc[:, k % 2], gv[:, k], ACT.Square).then_inc(sem("gv_sq"), 1)
            act.wait_ge(sem("g_sq_used"), 4)
            act.activation(blocks(wv[0]), ps_set[0], ACT.Square, scale=1.0 / GW).then_inc(act_steps, mark("g_mean_sq"))
            act.wait_ge(dve_steps, step("g_var"))
            act.activation(wv[1], wv[1], ACT.Sqrt, bias=eps[:, 0:1]).then_inc(act_steps, mark("g_std"))
            for k in range(4):
                act.wait_ge(sem("g_shift"), 1 + k + 1)
                act.activation(gv[:, k], gv[:, k], ACT.Identity, bias=col("gmlp_ln_b", k), scale=col("gmlp_ln_g", k)).then_inc(sem("v_ready"), 1)
            act.wait_ge(pe_steps, step("v_rowT"))
            act.copy(v_row, ps[0:DECB, 7, :]).then_inc(act_steps, mark("v_row_ready"))
            act.wait_ge(act_steps, step("v_row_ready"))
            act.dma_start(O["gmlp_v_sample"][0, :, 0, :], v_row).then_inc(sem("v_row_stored"), 16)
            for i in range(NT):
                act.wait_ge(sem("v_turned"), i + 1)
                if i >= 2:
                    act.wait_ge(sem("sg_ready"), i - 1)
                act.copy(acc[:, i % 2, 0:GW], ps[:, i % 2, :]).then_inc(sem("v_nat"), 1)

        def dve_gmlp(dve):
            then = chain(dve, "dve_")
            dve.wait_ge(act_steps, step("g_mean_sq"))
            dve.scalar_tensor_tensor(out=blocks(wv[1]), in0=ps_set[1], scalar=1.0 / GW, in1=blocks(wv[0]),
                                     op0=ALU.mult, op1=ALU.subtract).then_inc(dve_steps, mark("g_var"))
            dve.wait_ge(act_steps, step("g_std"))
            then(dve.reciprocal(wv[1], wv[1]))
            dve.scalar_tensor_tensor(out=blocks(wv[2]), in0=ps_set[0], scalar=-1.0 / GW, in1=blocks(wv[1]),
                                     op0=ALU.mult, op1=ALU.mult).then_inc(sem("g_shift"), 1)
            for k in range(4):
                then(dve.tensor_tensor(gv[:, k], gv[:, k], wv[1], ALU.mult))
                dve.wait_ge(sem("g_shift"), 1 + k)
                dve.tensor_tensor(gv[:, k], gv[:, k], wv[2], ALU.add).then_inc(sem("g_shift"), 1)
            dve.wait_ge(pe_steps, step("wmT_turned"))
            dve.tensor_tensor(wmT, ps[:, 6, :].rearrange("p (g n) -> p g n", g=4),
                              causal[:].unsqueeze(1).to_broadcast([P, 4, P]), ALU.mult).then_inc(dve_steps, mark("wmT_ready"))
            dve.wait_ge(sem("v_ready"), 4)
            then(dve.tensor_tensor(s_tmp, gv[:, :, SEQ:TOK], first_w.unsqueeze(2).to_broadcast([P, 4, DECB]), ALU.mult))
            then(dve.tensor_tensor(s_tmp, s_tmp, first_b.unsqueeze(2).to_broadcast([P, 4, DECB]), ALU.add))
            dve.tensor_tensor(gu[:, :, SEQ:TOK], gu[:, :, SEQ:TOK], s_tmp, ALU.mult).then_inc(sem("yd_ready"), 1)
            for i in range(NT):
                dve.wait_ge(sem("sg_ready"), i + 1)
                tmp = acc[:, i % 2, GW:2 * GW].rearrange("p (g n) -> p g n", g=4)
                then(dve.tensor_tensor(tmp, ps[:, 4 + i % 2, :].rearrange("p (g n) -> p g n", g=4), b_sp, ALU.add))
                dve.sem_inc(sem("sg_used"), 1)
                b = slice(P * i, P * (i + 1))
                dve.tensor_tensor(gu[:, :, b], gu[:, :, b], tmp, ALU.mult).then_inc(sem("yd_ready"), 1)

        def act_sample_state(act):
            act.wait_ge(sem("bcb_in"), 16)
            act.wait_ge(dve_steps, step("xdt_s"))
            act.wait_ge(sem("yd_ready"), NT + 1)
            act.wait_ge(sem("sg_ready"), NT)
            for b in range(DECB):
                if b >= 2:
                    act.wait_ge(sem("sst_done"), b - 1)
                for c in range(DC):
                    ins = act.activation(acc[:, b % 2, SN * c:SN * (c + 1)], bcb[:, b, SN * (c // 4):SN * (c // 4 + 1)], ACT.Copy,
                                         scale=sdt[:, 0, c, b:b + 1])
                ins.then_inc(sem("outer_ready"), 1)

        def dve_sample_state(dve):
            then = chain(dve, "dve_")
            dve.wait_ge(sem("ends_in"), 80)
            dve.tensor_tensor(sdt[:, 0], sdt[:, 0], xbc[:, 0:DC, SEQ:TOK], ALU.mult).then_inc(dve_steps, mark("xdt_s"))
            dve.wait_ge(sem("sst_in"), 16)
            for b in range(DECB):
                dve.wait_ge(sem("outer_ready"), b + 1)
                for c in range(DC):
                    ins = dve.scalar_tensor_tensor(out=sst[:, b, c], in0=sst[:, b, c], scalar=sdt[:, 1, c, b:b + 1],
                                                   in1=acc[:, b % 2, SN * c:SN * (c + 1)], op0=ALU.mult, op1=ALU.add)
                then(ins)
                for c in range(DC):
                    ins = dve.tensor_tensor_reduce(acc[:, b % 2, SN * c:SN * (c + 1)], sst[:, b, c],
                                                   bcb[:, b, SN * (2 + c // 4):SN * (3 + c // 4)], 1.0, 0.0, ALU.mult, ALU.add,
                                                   ys[:, c, b:b + 1])
                ins.then_inc(sem("sst_done"), 1)
            dve.wait_ge(sem("sst_done"), DECB)
            y = xbc[:, 0:DC, SEQ:TOK]
            then(dve.tensor_tensor(y, y, dskip[:].unsqueeze(2).to_broadcast([P, DC, DECB]), ALU.mult))
            then(dve.tensor_tensor(y, y, ys[:], ALU.add))

        def dve_gate(dve):
            for c in range(DC):
                dve.wait_ge(sem(f"row_loaded{c % 2}"), 16 * ((FH + SH) // 2 + c // 2 + 1))
                dve.tensor_tensor(xbc[:, c], xbc[:, c], acc[:, c % 2], ALU.mult).then_inc(sem("y_gated"), 1)
            then = chain(dve, "dve_")
            dve.wait_ge(act_steps, step("rms_rstd"))
            for c in range(DC):
                dve.tensor_tensor(xbc[:, c], xbc[:, c], wv[2], ALU.mult).then_inc(sem("y_scaled"), 1)
            dve.wait_ge(sem("y_scaled"), DC)
            for k in range(4):
                dve.wait_ge(sem("yd_hi"), k + 1)
                dve.tensor_tensor(yd_s[:, 1, k], gu[:, k], yd_s[:, 0, k].bitcast(F32), ALU.subtract).then_inc(sem("yd_lo"), 1)
            for k in range(DC):
                split_act_lo(dve, k, xbc[:, k], 3 * DC + k + 1)

        def act_gate(act):
            act.wait_ge(sem("sst_done"), DECB)
            for c in range(DC):
                act.wait_ge(sem("y_gated"), c + 1)
                if c >= 2:
                    act.wait_ge(sem("rms_used"), c - 1)
                act.activation(wv[c % 2], xbc[:, c], ACT.Square).then_inc(sem("rms_sq"), 1)
            act.wait_ge(sem("rms_used"), DC)
            chain(act, "act_")(act.activation(blocks(wv[2]), ps_set[0], ACT.Ln, bias=eps[:, 0:1], scale=1.0 / SI))
            act.activation(wv[2], wv[2], ACT.Exp, scale=-0.5).then_inc(act_steps, mark("rms_rstd"))
            act.wait_ge(sem("y_scaled"), DC)
            act.wait_ge(sem("v_row_stored"), 16)
            for k in range(4):
                act.copy(yd_s[:, 0, k], gu[:, k]).then_inc(sem("yd_hi"), 1)
            act.wait_ge(sem("yd_lo"), 4)
            act.wait_ge(sem("sst_stored"), 16)
            for k in range(DC):
                w = col("ssm_norm_w", k)
                act.activation(xs[:, 0, k], xbc[:, k], ACT.Copy, scale=w)
                act.activation(xbc[:, k], xbc[:, k], ACT.Copy, scale=w).then_inc(sem("xs_hi"), 1)

        def pe_gate(pe):
            pe.wait_ge(sem("v_nat"), NT)
            for c in range(DC):
                pe.wait_ge(sem("rms_sq"), c + 1)
                for t in range(NB):
                    mm = pe.matmul(ps_set[0][:, t], ones[:], wv[c % 2][:, TB * t:TB * (t + 1)], start=(c == 0), stop=(c == DC - 1))
                mm.then_inc(sem("rms_used"), 1)
            pe.wait_ge(act_steps, step("rms_rstd"))

        def sp_cd_out(sp, skip):
            wy, wd = kview(A["w_out_cd"][0], (0, SI)), kview(A["w_out_cd"][0], (SI, SI + GW))
            sp_stream(sp, "cd_out_y", lambda i: (wy[:, :, ds(256 * i, P)], wy[:, :, ds(256 * i + P, P)]), skip=skip)
            sp_stream(sp, "cd_out_d", lambda i: (wd[:, :, ds(256 * i, P)], wd[:, :, ds(256 * i + P, P)]), nk=4)

        N_STORED_CD = 13 + 3

        block = ctx.enter_context(nc.Block())

        @block.sync
        def _(sp):
            sp_setup(sp)
            sp_ab_in(sp)
            sp_naturals(sp)
            wo = square(A["w_out_ab"][0])
            load_pair(sp, G0["ab_out"], *wo(0))
            sp_attention(sp)
            for L in range(DEPTH):
                if L == 0:
                    sp_memory(sp, 0)
                    sp_stream(sp, "ab_out", wo, skip=1)
                else:
                    load_pair(sp, G0["cd_z"], *cd_src("cd_z")(0))
                    sp_cd_in(sp)
                    wy = kview(A["w_out_cd"][0], (0, SI))
                    load_pair(sp, G0["cd_out_y"], wy[:, :, 0:P], wy[:, :, P:2 * P])
                    sp_cd_prep(sp)
                    sp_heads(sp)
                    sp_gmlp(sp)
                    sp_memory(sp, 1)
                    sp_cd_out(sp, 1)
                sp_mem_weights(sp, L)
                wq = square(A["w_xq"][L])
                load_pair(sp, G0[f"xq{L}"], *wq(0))
                sp_memory_out(sp, L)
                sp_stream(sp, f"xq{L}", wq, skip=1)
                wo = square(A["w_xo"][L])
                load_pair(sp, G0[f"xo{L}"], *wo(0))
                sp_cross(sp, L)
                sp_stream(sp, f"xo{L}", wo, skip=1)
                sp_ff(sp, L)
            sp.wait_ge(sem("stored"), 16 * N_STORED_CD)
            sp.wait_ge(sem("mem_k_prompt_stored"), 16 * DEPTH)
            sp.wait_ge(sem("mem_v_prompt_stored"), 16 * DEPTH)

        @block.gpsimd
        def _(pool):
            pool_setup(pool)
            pool_gates(pool)
            pool_attention(pool)
            for L in range(DEPTH):
                if L == 1:
                    pool_heads(pool)
                pool_sums(pool, ("ab_out", "cd_out_d")[L], 3 * L)
                pool_memory(pool, L, 3 * L)
                pool_cross(pool, L)
                pool_sums(pool, f"xo{L}", 3 * L + 1)
                pool_norm(pool, 3 * L + 1)
                pool_sums(pool, f"down{L}_2", 3 * L + 2)
                pool_norm(pool, 3 * L + 2)

        @block.tensor
        def _(pe):
            pe_setup(pe)
            pe_ab_in(pe)
            pe_gates(pe)
            pe_naturals(pe)
            pe_gate_rows(pe)
            pe_pool(pe)
            pe_attention(pe)
            for L in range(DEPTH):
                if L == 0:
                    pe_stream(pe, "ab_out", xs, split=(sem("xs_lo"), DC))
                else:
                    pe_cd_in(pe)
                    pe_cd_prep(pe)
                    pe_states(pe)
                    pe_heads(pe)
                    pe_gmlp(pe)
                    pe_gate(pe)
                    pe_stream(pe, "cd_out_y", xs, split=(sem("xs_lo"), 3 * DC))
                    pe_stream(pe, "cd_out_d", yd_s, nk=4)
                pe_memory_turn(pe, L)
                pe_norm(pe, 3 * L, G1[("ab_out", "cd_out_d")[L]])
                pe_memory(pe, L, 3 * L)
                pe.wait_ge(sem("ln_lo"), DC * (3 * L + 1))
                pe_stream(pe, f"xq{L}", xs)
                pe_cross(pe, L)
                pe_stream(pe, f"xo{L}", xs, split=(sem("xs_lo"), XS_LO_MIXER[L]))
                pe_norm(pe, 3 * L + 1, G1[f"xo{L}"])
                pe_ff(pe, L)
                pe_norm(pe, 3 * L + 2, G1[f"down{L}_2"])
            pe.wait_ge(sem("ln_x"), DC * 3 * DEPTH)
            pe_output(pe)

        @block.scalar
        def _(act):
            act_setup(act)
            act_ab_in(act)
            act_gates(act)
            act_naturals(act)
            act_gate_rows(act)
            act.wait_ge(dve_steps, step("new_scores"))
            act.dma_start(ks_d, tiny[0:DECB, 8:8 + FH]).then_inc(sem("q_stored"), 16)
            act_pool(act)
            act_attention(act)
            for L in range(DEPTH):
                if L == 0:
                    act_stream(act, "ab_out", act_square(0))
                else:
                    act_cd_in(act)
                    act_cd_prep(act)
                    act_states(act)
                    act_heads(act)
                    act_gmlp(act)
                    act_sample_state(act)
                    act_gate(act)
                    act_stream(act, "cd_out_y")
                    act_stream(act, "cd_out_d", act_square(3))
                act_memory_turn(act, L)
                act_norm_stats(act, 3 * L)
                act_memory(act, L, 3 * L)
                act_xq(act, L)
                act_cross(act, L)
                act_stream(act, f"xo{L}", act_square(3 * L + 1))
                act_norm(act, 3 * L + 1)
                act_ff(act, L)
                act_norm(act, 3 * L + 2)
            act_output(act)

        @block.vector
        def _(dve):
            dve_setup(dve)
            dve_ab_in(dve)
            dve_gates(dve)
            dve_state_sums(dve)
            dve_naturals(dve)
            dve_new_scores(dve)
            dve_pool(dve)
            dve_attention(dve)
            for L in range(DEPTH):
                if L == 0:
                    dve_stream(dve, "ab_out", dve_residual(True, True))
                else:
                    dve_cd_in(dve)
                    dve_cd_prep(dve)
                    dve_states(dve)
                    dve_heads(dve)
                    dve_gmlp(dve)
                    dve_sample_state(dve)
                    dve_gate(dve)
                    dve_stream(dve, "cd_out_y", dve_residual(False, True))
                    dve_stream(dve, "cd_out_d", dve_residual(False, False))
                dve_memory_turn(dve, L)
                dve_norm_stats(dve, 3 * L)
                dve_memory(dve, L, 3 * L)
                dve_stream(dve, f"xq{L}")
                dve_cross(dve, L, XS_LO_MIXER[L])
                dve_stream(dve, f"xo{L}", dve_residual(False, True))
                dve_norm(dve, 3 * L + 1)
                dve_ff(dve, L)
                dve_norm(dve, 3 * L + 2)


_INPUTS = ("x_prompt", "x_sample", "cache_fox_k", "cache_fox_v", "cache_fox_logf", "state_pool", "state_conv",
           "state_ssm", "cache_mem_k", "cache_mem_v", "page_table", "mem_prompt", "w_in_ab", "b_forget", "w_pool",
           "pool_scale", "w_out_ab", "w_in_cd", "conv_w", "conv_b", "dt_bias", "a_log", "d_skip", "ssm_norm_w",
           "gmlp_ln_g", "gmlp_ln_b", "w_spatial", "b_spatial", "w_out_cd", "ln_mix_g", "ln_mix_b", "w_xq", "w_xk",
           "w_xv", "w_xo", "ln_x_g", "ln_x_b", "w_gate", "w_up", "w_down", "ln_ff_g", "ln_ff_b")
_OUTPUTS = (("y_prompt", (1, SEQ, D)), ("y_sample", (DECB, 1, D)),
            ("fox_k_prompt", (1, 1, SEQ, FH, FD)), ("fox_v_prompt", (1, 1, SEQ, FH, FD)),
            ("fox_logf_prompt", (1, 1, SEQ, FH)),
            ("fox_k_sample", (1, DECB, 1, FH, FD)), ("fox_v_sample", (1, DECB, 1, FH, FD)),
            ("fox_logf_sample", (1, DECB, 1, FH)),
            ("pool_state_prompt", (1, 1, PBUF, FW)), ("pool_state_sample", (1, DECB, PBUF, FW)),
            ("conv_state_prompt", (1, 1, CONVW - 1, CCH)), ("conv_state_sample", (1, DECB, CONVW - 1, CCH)),
            ("ssm_state_prompt", (1, 1, SH, SD, SN)), ("ssm_state_sample", (1, DECB, SH, SD, SN)),
            ("gmlp_v_sample", (1, DECB, 1, GW)),
            ("mem_k_prompt", (DEPTH, 1, NMEM, MH, MD)), ("mem_v_prompt", (DEPTH, 1, NMEM, MH, MD)))


def kernel(**inputs):
    import numpy as np
    import concourse.bacc as bacc
    from concourse.bass_utils import run_bass_kernel_spmd

    nc = bacc.Bacc("TRN2", target_bir_lowering=False, num_devices=1)
    arrays, a, o = {}, {}, {}
    for name in _INPUTS:
        arrays["in_" + name] = np.ascontiguousarray(inputs[name])
        a[name] = nc.dram_tensor("in_" + name, arrays["in_" + name].shape,
                                 mybir.dt.from_np(arrays["in_" + name].dtype), kind="ExternalInput").ap()
    for name, shape in _OUTPUTS:
        o[name] = nc.dram_tensor("out_" + name, shape, F32, kind="ExternalOutput").ap()
    hybrid_step(nc, a, o)
    r = run_bass_kernel_spmd(nc, [arrays], core_ids=[0])
    return tuple(r.results[0]["out_" + name] for name, _ in _OUTPUTS)
```

```python
from contextlib import ExitStack

import concourse.bass as bass
from concourse import mybir

F32 = mybir.dt.float32
F32R = mybir.dt.float32r
I32 = mybir.dt.int32
ALU = mybir.AluOpType
ACT = mybir.ActivationFunctionType
AX = mybir.AxisListType
RMAX = bass.bass_isa.ReduceOp.max
RADD = bass.bass_isa.ReduceOp.add
ds = bass.ds

P = 128
D = 1024
DC = D // P
SEQ = 1024
NT = SEQ // P
DECB = 8
TOK = SEQ + DECB
NB = 3
TB = TOK // NB
DEPTH = 2
ALPHA = (2 * DEPTH) ** 0.25
LN_EPS = 1e-5
BIG = 1e30
FH, FD = 8, 64
FW = FH * FD
PAGE, NPG = 128, 16
NPHYS = 160
WINDOWS = (2, 4, 8, 16)
PBUF = 15
NMEM, MH, MD = 256, 4, 256
SH, SD, SN, SG = 16, 64, 128, 2
SI = SH * SD
CCH = SI + 2 * SG * SN
CONVW = 4
GW = 512
FFC = 22
FF = FFC * P
FF_GROUPS = (8, 8, 6)


def hybrid_step(nc, A, O):
    with ExitStack() as ctx:
        sems = {}

        def sem(name):
            if name not in sems:
                sems[name] = ctx.enter_context(nc.semaphore(name))
            return sems[name]

        def sb(name, shape, dt=F32, at=None):
            return (at or ctx).enter_context(nc.sbuf_tensor(name, shape, dt))

        def scratch(name, shape):
            return nc.dram_tensor(name, shape, F32, kind="Internal").ap()

        x = sb("x", [P, DC, TOK])
        raw_w = sb("raw_w", [P, 2, DC, P])
        spl_w = sb("spl_w", [P, 2, 2, DC, P], F32R)
        ident = sb("ident", [P, P])
        ones = sb("ones", [P, P])
        causal = sb("causal", [P, P])
        later = sb("later", [P, P])
        future = sb("future", [P, P])
        cols = sb("cols", [P, 192])
        eps = sb("eps", [P, 1])
        tiny = sb("tiny", [P, 64])
        tmax = sb("tmax", [P, 4])
        nmax = sb("nmax", [P, 8])
        rsum = sb("rsum", [P, 8])
        rinv = sb("rinv", [P, 8])
        st_sum = sb("st_sum", [P, 4, DECB])
        page_idx = sb("page_idx", [1, DECB * NPG], I32)
        lf_new = sb("lf_new", [P, DECB * FH])
        sc_new = sb("sc_new", [1, DECB * FH])
        gates = sb("gates", [P, 5, (NT + 1) * SH])
        s_red = gates[:].rearrange("p a n -> p (a n)")[:, 0:4 * DECB * FH].rearrange(
            "p (a n) -> p a n", a=4)
        smx = sb("smx", [P, DECB, 2, MH])
        sel_b = sb("sel_b", [MH * DECB, DECB])
        smr = sb("smr", [P, 4, DECB, MH])
        dskip = sb("dskip", [P, DC])
        s_new = sb("s_new", [P, 4, DECB])
        s_sum = sb("s_sum", [P, 4, DECB])
        inv_cnt = sb("inv_cnt", [P, 4, 16])
        w_small = sb("w_small", [P, DC, SH])

        xs_area = ExitStack()
        xs = sb("xs", [P, 2, DC, TOK], F32R, xs_area)

        rest = ExitStack()
        proj = sb("proj", [P, 16, TOK], F32, rest)
        rows_area = ExitStack()
        fl_rows = sb("fl_rows", [FH, TOK], F32, rows_area)
        rows_area.close()
        kst = sb("kst", [P, 2, FW], F32, rest)
        w_pl = sb("w_pl", [P, 4, P], F32, rest)
        lf_pg = sb("lf_pg", [P, DECB, NPG, FH], F32, rest)
        ulast = sb("ulast", [PBUF, FW], F32, rest)
        own = w_pl[0:FH].rearrange("p g n -> p (g n)")
        rest.close()
        rest = ExitStack()
        xin = sb("xin", [P, 2, D], F32, rest)
        prow = sb("prow", [P, 2, P], F32, rest)
        rest.close()
        rest = ExitStack()
        sum_x = sb("sum_x", [P, TOK], F32, rest)
        sum_sq = sb("sum_sq", [P, TOK], F32, rest)
        sq = sb("sq", [P, TOK], F32, rest)
        ln_rest = ExitStack()
        y_out = sb("y_out", [P, 2, NT, P], F32, ln_rest)
        y_s = sb("y_s", [DECB, 2, P], F32, ln_rest)
        ln_rest.close()
        ln_rest = ExitStack()
        hs = sb("hs", [P, 2, DC, TOK], F32R, ln_rest)
        ln_rest.close()
        ln_rest = ExitStack()
        qx = sb("qx", [P, DC, TOK], F32, ln_rest)
        mem_s = sb("mem_s", [P, 2, DC, NMEM], F32R, ln_rest)
        mkT = sb("mkT", [P, DC, NMEM], F32, ln_rest)
        mem_n = sb("mem_n", [P, 2, D], F32, ln_rest)
        ln_rest.close()
        rest.close()

        xs_area.close()
        xs_area = ExitStack()
        cb = sb("cb", [P, 2, SEQ], F32, xs_area)
        cbd = sb("cbd", [P, 2, NT, P], F32, xs_area)
        prob = sb("prob", [P, 3, SEQ], F32, xs_area)
        pT = sb("pT", [P, 2, NT, P], F32, xs_area)
        kp_area = ExitStack()
        kpage = sb("kpage", [P, 4, 2, FW], F32, kp_area)
        kp_area.close()
        s_nat = sb("s_nat", [DECB, 4, FW], F32, xs_area)
        s_qk = sb("s_qk", [P, 4, FW], F32, xs_area)
        qb = sb("qb", [P, 2, FW], F32, xs_area)
        sc_area = ExitStack()
        sc = sb("sc", [P, DECB, FH, NPG + 1], F32, sc_area)
        sc_area.close()
        sc_area = ExitStack()
        win = sb("win", [P, 2, TOK], F32, sc_area)
        sc_area.close()
        xs_area.close()
        xs_area = ExitStack()
        mkv = sb("mkv", [P, 4, 2, D], F32, xs_area)
        qbx = sb("qbx", [P, 2, D], F32, xs_area)
        probx = sb("probx", [P, 2, D], F32, xs_area)
        pTx = sb("pTx", [P, 2, 2 * MH, P], F32, xs_area)
        qn_area = ExitStack()
        qn = sb("qn", [DECB, D], F32, qn_area)
        qn_area.close()
        own_x = sb("own_x", [MH * DECB, MH, MD], F32, xs_area)
        smz = sb("smz", [P, DECB, 2, MH, DECB], F32, xs_area)
        xs_area.close()

        rest = ExitStack()
        sb("beside_xs", [P, 2, DC, TOK], F32R, rest)
        xbc = sb("xbc", [P, 12, TOK], F32, rest)
        acc = sb("acc", [P, 2, TOK], F32, rest)
        work = sb("work", [P, 4, 1024], F32, rest)
        tail = sb("tail", [P, 12, CONVW - 1 + DECB], F32, rest)
        convT = sb("convT", [P, 12, DECB, CONVW - 1], F32, rest)
        acs_n = sb("acs_n", [P, NT, SH], F32, rest)
        ends = sb("ends", [P, SH, NT], F32, rest)
        sdt = sb("sdt", [P, 2, DC, DECB], F32, rest)
        dec_end = sb("dec_end", [P, NT, SH], F32, rest)
        dec_chunk = sb("dec_chunk", [P, SH, NT], F32, rest)
        ys = sb("ys", [P, DC, DECB], F32, rest)
        rest.close()
        rest = ExitStack()
        sb("beside_xs_too", [P, 2, DC, TOK], F32R, rest)
        sb("under_yd", [P, DC, TOK], F32, rest)
        yd_lo = sb("yd_lo", [P, 4, TOK], F32R, rest)
        rest.close()
        b_nat = work[:, 0:2].rearrange("p a (i n) -> p (a i) n", n=2 * SN)
        cbT = work[:, 2:4].rearrange("p g (i n) -> p g i n", n=P)
        xs_area = ExitStack()
        xdt = sb("xdt", [P, NT, SI], F32, xs_area)
        hprev = sb("hprev", [P, NT, SI], F32, xs_area)
        xs_area.close()
        xs_area = ExitStack()
        bc_row = sb("bc_row", [DECB, 2 * SG * SN], F32, xs_area)
        ctail = sb("ctail", [CONVW - 1 + DECB, CCH], F32, xs_area)
        xs_area.close()
        xs_area = ExitStack()
        gv = sb("gv", [P, 4, TOK], F32, xs_area)
        gu = sb("gu", [P, 4, TOK], F32, xs_area)
        sst = sb("sst", [P, DECB, DC, SN], F32, xs_area)
        xs_area.close()

        xs_area = ExitStack()
        yd_hi = sb("yd_hi", [P, 4, TOK], F32R, xs_area)
        xs_area.close()

        ps = ctx.enter_context(nc.psum_tensor("ps", [P, 8, 512], F32))
        ps_set = [ps[:, 0:3, 0:TB], ps[:, 3:6, 0:TB]]

        lf_flat = lf_pg[:].rearrange("p b g h -> p (b g h)")
        suf = kst[:].rearrange("p a n -> p (a n)")

        STEPS = {
            "pe": ("colsT_ready", "gate_logits0", "gate_logits1", "gate_logits2", "gate_turned", "gate_sums",
                    "gate_rowsT", "stateT_ready", "ulastT_ready", "s_natT_ready", "s_values_ready",
                    "convT_turned", "dt_logits0", "dt_logits1", "dt_logits2", "dt_turned", "dt_sums",
                    "dt_rowsT", "tailT_ready", "s_bcT_ready", "lastT_ready", "wmT_turned", "v_rowT"),
            "act": ("gate_rows0", "gate_rows1", "gate_rows2", "gate_ln", "gate_token_rows", "ulast_ready",
                    "s_nat_ready", "sc_exp", "convT_ready", "dt_rows0", "dt_rows1", "dt_rows2", "dt_ln",
                    "dt_token_rows", "s_decay_ready", "ctail_ready", "s_bc_ready", "last_ready", "g_mean_sq",
                    "g_std", "v_row_ready", "rms_rstd"),
            "dve": ("inv_cnt_ready", "sel_b_ready", "gate_biased", "logf_ready", "c_ready", "new_scores",
                    "sc_cleared", "s_max_ready", "sc_shifted", "s_sum_ready", "sc_ready", "dt_biased",
                    "da_ready", "dec_diff", "g_var", "wmT_ready", "xdt_s"),
            "pool": ("own_ready", "s_max_all", "s_sum_all"),
        }
        pe_steps, act_steps, dve_steps, pool_steps = (sem(f"{e}_steps") for e in ("pe", "act", "dve", "pool"))
        marked = {e: 0 for e in STEPS}

        def step(name):
            return next(names.index(name) + 1 for names in STEPS.values() if name in names)

        def mark(name):
            e = next(e for e, names in STEPS.items() if name in names)
            marked[e] += 1
            assert marked[e] == step(name), (name, marked[e])
            return 1

        w_loaded = [sem("w_loaded0"), sem("w_loaded1")]
        hi_ready, lo_ready, tile_done = sem("hi_ready"), sem("lo_ready"), sem("tile_done")
        set_free = [sem("set0_free"), sem("set1_free")]

        def kview(w, rows=None):
            w = w if rows is None else w[rows[0]:rows[1], :]
            return w.rearrange("(k p) n -> p k n", p=P)

        def loop(eng, n, body):
            if n == 1:
                body(0)
            else:
                with eng.Fori(0, n) as i:
                    body(i)

        def load_pair(sp, g, src0, src1, nk=DC, first=False):
            for s, src in enumerate((src0, src1)):
                if not first:
                    sp.wait_ge(hi_ready, 2 * g - 1 + s)
                    sp.wait_ge(lo_ready, 2 * g - 1 + s)
                sp.dma_start(raw_w[:, s, 0:nk, :], src).then_inc(w_loaded[s], 16)

        def split_hi(act, s, g, first=False):
            act.wait_ge(w_loaded[s], 16 * (g + 1))
            if not first:
                act.wait_ge(tile_done, 2 * g - 1 + s)
            act.copy(spl_w[:, s, 0], raw_w[:, s]).then_inc(hi_ready, 1)

        def split_lo(dve, s, g):
            dve.wait_ge(hi_ready, 2 * g + s + 1)
            dve.tensor_tensor(spl_w[:, s, 1], raw_w[:, s], spl_w[:, s, 0].bitcast(F32),
                              ALU.subtract).then_inc(lo_ready, 1)

        def product_tile(pe, s, g, act_in, nk=DC, n=NB, width=TB, first=False, split=None):
            pe.wait_ge(lo_ready, 2 * g + s + 1)
            if not first:
                pe.wait_ge(set_free[s], g)
            for k in range(nk):
                if split:
                    pe.wait_ge(split[0], split[1] + k + 1)
                for step, (a, b) in enumerate(((0, 0), (0, 1), (1, 0))):
                    for t in range(n):
                        part = act_in[b] if isinstance(act_in, tuple) else act_in[:, b]
                        mm = pe.matmul(ps[:, 3 * s + t, 0:width], spl_w[:, s, a, k],
                                       part[:, k, width * t:width * (t + 1)],
                                       start=(k == 0 and step == 0), stop=(k == nk - 1 and step == 2))
            mm.then_inc(tile_done, 1)

        sizes = [("ab_q", 2), ("ab_kv", 4), ("ab_u", 2), ("ab_out", 4)]
        for L in range(DEPTH):
            if L == 1:
                sizes += [("cd_z", 4), ("cd_gu", 2), ("cd_xbc", 6), ("cd_gv", 2),
                          ("cd_out_d", 4), ("cd_out_y", 4)]
            sizes += [(f"mem{L}", 8), (f"xq{L}", 4), (f"xo{L}", 4)]
            for q, c in enumerate(FF_GROUPS):
                sizes += [(f"gu{L}_{q}", c), (f"down{L}_{q}", 4)]
        G0, G1, at = {}, {}, 0
        for name, n in sizes:
            G0[name] = at
            at += n
            G1[name] = at
        N_PAIRS = at

        COL = {"ln_mix_g": 0, "ln_mix_b": 16, "ln_x_g": 32, "ln_x_b": 48, "ln_ff_g": 64,
               "ln_ff_b": 80, "pool_scale": 96, "conv_b": 100, "ssm_norm_w": 112,
               "gmlp_ln_g": 120, "gmlp_ln_b": 124, "conv_w": 128}

        def col(name, c):
            return cols[:, COL[name] + c:COL[name] + c + 1]

        q_d = scratch("q_d", [DECB, FW])
        ks_d = scratch("ks_d", [DECB, FH])
        c_d = scratch("c_d", [FH, SEQ])

        chains = {}

        def chain(eng, name):
            name = name.split("_")[0] + "_chain"
            s, n = sem(name), chains.setdefault(name, [0])

            def then(ins):
                n[0] += 1
                ins.then_inc(s, 1)
                eng.wait_ge(s, n[0])
            return then

        h_vec = tiny[:, 16:64].rearrange("p (a h) -> p a h", a=3)

        tiles = [(i * P, P) for i in range(NT)] + [(SEQ, DECB)]

        def sp_setup(sp):
            for n, name in enumerate(("ln_mix_g", "ln_mix_b", "ln_x_g", "ln_x_b", "ln_ff_g", "ln_ff_b",
                                      "pool_scale", "conv_b", "ssm_norm_w", "gmlp_ln_g", "gmlp_ln_b")):
                src = A[name].rearrange("a (c p) -> (a c) p", p=P)
                sp.dma_start(prow[COL[name]:COL[name] + src.shape[0], 0, :], src).then_inc(sem("rows_in"), 16)
            sp.dma_start(prow[0:48, 1, :], A["conv_w"].rearrange("a j (c p) -> (a j c) p", p=P)).then_inc(sem("rows_in"), 16)
            sp.dma_start(w_small[:, :, 0:FH], win_ab[:, :, 3 * FW:3 * FW + FH]).then_inc(sem("w_small_in"), 16)
            for n, (name, H) in enumerate((("b_forget", FH), ("dt_bias", SH), ("a_log", SH))):
                sp.dma_start(h_vec[:, n, 0:H], A[name].to_broadcast([P, H])).then_inc(sem("w_small_in"), 16)
            for n, (t0, m) in enumerate(tiles):
                if n >= 2:
                    sp.wait_ge(sem("xT_ready"), n - 1)
                src = A["x_prompt"][0, t0:t0 + m, :] if n < NT else A["x_sample"][:, 0, :]
                sp.dma_start(xin[0:m, n % 2, :], src).then_inc(sem(f"xin_loaded{n % 2}"), 16)
            load_pair(sp, 0, win_ab[:, :, 0:P], win_ab[:, :, P:2 * P], first=True)
            sp.dma_start(page_idx[:], A["page_table"].rearrange("b g -> (b g)").unsqueeze(0)).then_inc(sem("pages_in"), 16)

        def pool_setup(pool):
            then = chain(pool, "pool_setup")
            then(pool.memset(ident[:], 0.0))
            then(pool.memset(future[:], 0.0))
            then(pool.memset(ones[:], 1.0))
            pool.sem_inc(sem("sum_x_ready"), 1)
            pool.sem_inc(sem("sq_used"), 1)
            pool.sem_inc(sem("spilled0"), 16)
            pool.sem_inc(sem("spilled1"), 16)
            pool.sem_inc(sem("ff_hi"), 1)
            pool.sem_inc(sem("ff_lo"), 1)
            pool.sem_inc(sem("mem_rows"), 2)
            pool.sem_inc(sem("mem_rowsT"), 2)
            pool.memset(eps[:], LN_EPS).then_inc(sem("const_ready"), 1)
            pool.affine_select(out=ident[:], in_=ident[:], compare_op=ALU.not_equal, fill=1.0, base=0,
                               pattern=[[-1, P]], channel_multiplier=1).then_inc(sem("const_ready"), 1)
            pool.affine_select(out=future[:], in_=future[:], compare_op=ALU.is_ge, fill=BIG, base=0,
                               pattern=[[-1, P]], channel_multiplier=1).then_inc(sem("const_ready"), 1)
            pool.affine_select(out=later[:], in_=ones[:], compare_op=ALU.is_gt, fill=0.0, base=0,
                               pattern=[[-1, P]], channel_multiplier=1).then_inc(sem("const_ready"), 1)
            pool.affine_select(out=causal[:], in_=ones[:], compare_op=ALU.is_ge, fill=0.0, base=0,
                               pattern=[[1, P]], channel_multiplier=-1).then_inc(sem("const_ready"), 1)
            then(pool.iota(inv_cnt[:], pattern=[[0, 4], [1, 16]], base=1, channel_multiplier=0,
                           allow_small_or_imprecise_dtypes=True))
            for g, w in enumerate(WINDOWS):
                pool.tensor_scalar(inv_cnt[:, g], inv_cnt[:, g], float(w), None, ALU.min).then_inc(sem("const_ready"), 1)

        N_CONST = 9

        def pe_setup(pe):
            pe.wait_ge(sem("const_ready"), N_CONST)
            pe.wait_ge(sem("rows_in"), 16 * 12)
            pe.transpose(ps[:, 0, 0:P], prow[:, 0, :], ident[:])
            pe.transpose(ps[:, 0, P:P + 48], prow[0:48, 1, :], ident[0:48, 0:48]).then_inc(pe_steps, mark("colsT_ready"))
            for n, (t0, m) in enumerate(tiles):
                pe.wait_ge(sem(f"xin_loaded{n % 2}"), 16 * (n // 2 + 1))
                if n >= 2:
                    pe.wait_ge(sem("xT_copied"), n - 1)
                for c in range(DC):
                    mm = pe.transpose(ps[:, 2 + 2 * (n % 2) + c // 4, m * (c % 4):m * (c % 4 + 1)],
                                      xin[0:m, n % 2, P * c:P * (c + 1)], ident[0:m, 0:m])
                mm.then_inc(sem("xT_ready"), 1)
                if n in (4, 7, 8):
                    pe.wait_ge(sem("w_small_in"), 64)
                    pe.wait_ge(sem("xT_copied"), 9 if n == 8 else n - 1)
                    pe_logits(pe, "gate", FH, (4, 7, 8).index(n))
            pe_logits_turn(pe, "gate", FH, fl_rows)

        def act_setup(act):
            act.wait_ge(pe_steps, step("colsT_ready"))
            act.copy(cols[:, 0:176], ps[:, 0, 0:176]).then_inc(sem("cols_ready"), 1)
            for n, (t0, m) in enumerate(tiles):
                act.wait_ge(sem("xT_ready"), n + 1)
                b = 2 + 2 * (n % 2)
                act.copy(x[:, :, t0:t0 + m].rearrange("p (a c) t -> p a c t", a=2),
                         ps[:, b:b + 2, 0:4 * m].rearrange("p a (c t) -> p a c t", c=4)).then_inc(sem("xT_copied"), 1)
                if n in (4, 7, 8):
                    act_logits(act, "gate", FH, (4, 7, 8).index(n), fl_rows)
            split_hi(act, 0, 0, first=True)
            act.wait_ge(sem("xT_copied"), NT + 1)
            for k in range(DC):
                act.copy(xs[:, 0, k], x[:, k]).then_inc(sem("xs_hi"), 1)

        def dve_setup(dve):
            dve.wait_ge(sem("const_ready"), N_CONST)
            dve.reciprocal(inv_cnt[:], inv_cnt[:]).then_inc(dve_steps, mark("inv_cnt_ready"))
            n = MH * DECB
            dve.tensor_reduce(sel_b[:], ident[0:n, 0:n].rearrange("p (h b) -> p b h", h=MH), AX.X, ALU.add
                              ).then_inc(dve_steps, mark("sel_b_ready"))
            split_lo(dve, 0, 0)
            for k in range(DC):
                split_act_lo(dve, k, x[:, k], k + 1)
            dve_logits(dve, "gate", FH, 0)

        def split_act_lo(dve, k, src, n_hi):
            dve.wait_ge(sem("xs_hi"), n_hi)
            dve.tensor_tensor(xs[:, 1, k], src, xs[:, 0, k].bitcast(F32), ALU.subtract).then_inc(sem("xs_lo"), 1)

        def sp_stream(sp, name, src, nk=DC, skip=0):
            g0, n = G0[name], G1[name] - G0[name]
            if skip < n:
                loop(sp, n - skip, lambda i: load_pair(sp, g0 + skip + i, *src(i + skip), nk=nk))

        def pe_stream(pe, name, act_in, nk=DC, n=NB, width=TB, split=None):
            g0, cnt = G0[name], G1[name] - G0[name]
            if split:
                for s in range(2):
                    product_tile(pe, s, g0, act_in, nk, n, width, first=(g0 == 0), split=split if s == 0 else None)
                g0, cnt = g0 + 1, cnt - 1
            def body(i):
                for s in range(2):
                    product_tile(pe, s, g0 + i, act_in, nk, n, width)
            loop(pe, cnt, body)

        def act_stream(act, name, evac=None):
            g0, cnt = G0[name], G1[name] - G0[name]
            def body(i, last=False, first=False):
                g = g0 + i
                split_hi(act, 1, g, first=first)
                if evac:
                    act.wait_ge(tile_done, 2 * g + 1)
                    settle(act)
                    evac(0, i, g)
                if not last:
                    split_hi(act, 0, g + 1)
                if evac:
                    act.wait_ge(tile_done, 2 * g + 2)
                    settle(act)
                    evac(1, i, g)
            if g0 == 0:
                body(0, first=True)
                loop(act, cnt - 1, lambda i: body(i + 1))
            elif G1[name] == N_PAIRS:
                loop(act, cnt - 1, body)
                body(cnt - 1, last=True)
            else:
                loop(act, cnt, body)

        def dve_stream(dve, name, evac=None):
            g0, cnt = G0[name], G1[name] - G0[name]
            def body(i, last=False):
                g = g0 + i
                split_lo(dve, 1, g)
                if evac:
                    evac(0, i, g)
                if not last:
                    split_lo(dve, 0, g + 1)
                if evac:
                    evac(1, i, g)
            if G1[name] == N_PAIRS:
                loop(dve, cnt - 1, body)
                body(cnt - 1, last=True)
            else:
                loop(dve, cnt, body)

        def settle(act, n=0):
            act.wait_ge(sem(("cols_ready", "xT_copied", "const_ready", "rows_in", "xin_loaded0", "w_small_in")[n]), 1)

        def chunk(t, c):
            return t[:, ds(c, 1), :].rearrange("p a n -> p (a n)")

        def blocks(ap):
            return ap.rearrange("p (b n) -> p b n", b=NB)

        win_ab = kview(A["w_in_ab"][0])
        AB_COL = {"ab_q": 0, "ab_kv": FW, "ab_u": 3 * FW + FH}

        def sp_ab_in(sp):
            for name in ("ab_q", "ab_kv", "ab_u"):
                c0 = AB_COL[name]
                sp_stream(sp, name, lambda i, c0=c0: (win_ab[:, :, ds(c0 + 256 * i, P)],
                                                      win_ab[:, :, ds(c0 + P + 256 * i, P)]),
                          skip=(name == "ab_q"))

        def pe_ab_in(pe):
            pe_stream(pe, "ab_q", xs, split=(sem("xs_lo"), 0))
            pe_stream(pe, "ab_kv", xs)
            pe_token_sums(pe, "gate", FH, gate(0, FH))
            pe_stream(pe, "ab_u", xs)
            pe_token_rows(pe, "gate", FH)

        def act_ab_in(act):
            for name, c0, scale in (("ab_q", 0, FD ** -0.5), ("ab_kv", 4, 1.0), ("ab_u", 12, 1.0)):
                def evac(s, i, g, c0=c0, scale=scale):
                    act.activation(blocks(chunk(proj, c0 + 2 * i + s)), ps_set[s], ACT.Copy,
                                   scale=scale).then_inc(set_free[s], 1)
                act_stream(act, name, evac)
                if name == "ab_q":
                    act_softplus(act, "gate", FH)
                if name == "ab_kv":
                    act.wait_ge(dve_steps, step("logf_ready"))
                    act.dma_start(O["fox_logf_prompt"][0, 0].rearrange("(n p) h -> p n h", p=P), gate(0, FH)[:, 0:NT]).then_inc(sem("lf_stored"), 16)
                    act.dma_start(O["fox_logf_sample"][0, :, 0, :], gate(0, FH)[0:DECB, NT]).then_inc(sem("lf_stored"), 16)
            act_token_rows(act, "gate", FH)
            act.dma_start(c_d.rearrange("h (i p) -> (h i) p", p=P), token_rows[0:FH * NT]).then_inc(sem("lf_stored"), 16)

        def dve_ab_in(dve):
            dve_stream(dve, "ab_q")
            dve_gates(dve)
            dve_stream(dve, "ab_kv")
            dve_gate_sums(dve)
            dve_stream(dve, "ab_u")

        token_rows = gates[:, 3, 0:P]

        def gate(r, H):
            return gates[:, r, 0:(NT + 1) * H].rearrange("p (n h) -> p n h", h=H)

        def pe_logits(pe, pre, H, t):
            if t == 2:
                pe.wait_ge(act_steps, step(pre + "_rows0"))
            for k in range(DC):
                mm = pe.matmul(ps[0:H, 6 + t % 2, 0:TB], w_small[:, k, 0:H], x[:, k, TB * t:TB * (t + 1)],
                               start=(k == 0), stop=(k == DC - 1))
            mm.then_inc(pe_steps, mark(f"{pre}_logits{t}"))

        def act_logits(act, pre, H, t, buf):
            act.wait_ge(pe_steps, step(f"{pre}_logits{t}"))
            act.copy(buf[0:H, TB * t:TB * (t + 1)], ps[0:H, 6 + t % 2, 0:TB]).then_inc(act_steps, mark(f"{pre}_rows{t}"))

        def pe_logits_turn(pe, pre, H, buf):
            pe.wait_ge(act_steps, step(pre + "_rows2"))
            for n, (t0, m) in enumerate(tiles):
                mm = pe.transpose(ps[0:m, 7, H * n:H * (n + 1)], buf[0:H, t0:t0 + m], ident[0:H, 0:H])
            mm.then_inc(pe_steps, mark(pre + "_turned"))

        def dve_logits(dve, pre, H, bias):
            then = chain(dve, "dve_")
            then(dve.memset(gate(0, H)[:, NT], 0.0))
            dve.wait_ge(pe_steps, step(pre + "_turned"))
            b = h_vec[:, bias, 0:H]
            dve.tensor_tensor(gate(0, H)[:, 0:NT], ps[:, 7, 0:NT * H].rearrange("p (n h) -> p n h", h=H),
                              b.unsqueeze(1).to_broadcast([P, NT, H]), ALU.add)
            dve.tensor_tensor(gate(0, H)[0:DECB, NT], ps[0:DECB, 7, NT * H:(NT + 1) * H], b[0:DECB],
                              ALU.add).then_inc(dve_steps, mark(pre + "_biased"))

        def act_softplus(act, pre, H):
            then = chain(act, "act_")
            act.wait_ge(dve_steps, step(pre + "_biased"))
            then(act.activation(gate(1, H), gate(0, H), ACT.Abs))
            then(act.activation(gate(1, H), gate(1, H), ACT.Exp, scale=-1.0))
            if pre == "dt":
                then(act.activation(h_vec[:, 2], h_vec[:, 2], ACT.Exp))
            act.activation(gate(2, H), gate(1, H), ACT.Ln, bias=1.0).then_inc(act_steps, mark(pre + "_ln"))

        def log1p_fix(dve, then, e, ln, u, d):
            then(dve.tensor_scalar(u, e, 1.0, None, ALU.add))
            then(dve.scalar_tensor_tensor(out=d, in0=u, scalar=-1.0, in1=e, op0=ALU.add, op1=ALU.subtract))
            then(dve.reciprocal(u, u))
            then(dve.tensor_tensor(d, d, u, ALU.mult))
            then(dve.tensor_tensor(ln, ln, d, ALU.subtract))

        def pe_token_sums(pe, pre, H, src):
            n = NT * H
            pe.wait_ge(dve_steps, step("logf_ready" if pre == "gate" else "da_ready"))
            pe.matmul(ps[:, 6, 0:n], causal[:], src[:, 0:NT], start=True, stop=True)
            pe.matmul(ps[:, 6, n:2 * n], ones[:], src[:, 0:NT], start=True, stop=True).then_inc(pe_steps, mark(pre + "_sums"))

        def pe_token_rows(pe, pre, H):
            pe.wait_ge(dve_steps, step("c_ready" if pre == "gate" else "dec_diff"))
            pe.transpose(ps[0:NT * H, 6, 256:256 + P], gates[:, 1 if pre == "gate" else 2, 0:NT * H],
                         ident[:]).then_inc(pe_steps, mark(pre + "_rowsT"))

        def act_token_rows(act, pre, H):
            act.wait_ge(pe_steps, step(pre + "_rowsT"))
            act.copy(token_rows[0:NT * H], ps[0:NT * H, 6, 256:256 + P]).then_inc(act_steps, mark(pre + "_token_rows"))
            act.wait_ge(act_steps, step(pre + "_token_rows"))

        def dve_gates(dve):
            then = chain(dve, "dve_")
            dve.wait_ge(act_steps, step("gate_ln"))
            log1p_fix(dve, then, gate(1, FH), gate(2, FH), gate(3, FH), gate(4, FH))
            dve.scalar_tensor_tensor(out=gate(0, FH), in0=gate(0, FH), scalar=0.0, in1=gate(2, FH),
                                     op0=ALU.min, op1=ALU.subtract).then_inc(dve_steps, mark("logf_ready"))

        def dve_gate_sums(dve):
            then = chain(dve, "dve_")
            n = NT * FH
            dve.wait_ge(pe_steps, step("gate_sums"))
            within, total = ps[:, 6, 0:n].rearrange("p (n h) -> p h n", h=FH), gate(2, FH)
            c = gates[:, 1, 0:n].rearrange("p (h n) -> p h n", h=FH)
            dve.tensor_copy(c, within)
            then(dve.tensor_copy(total[:, 0:NT], ps[:, 6, n:2 * n].rearrange("p (n h) -> p n h", h=FH)))
            for i in range(1, NT - 1):
                then(dve.tensor_tensor(total[:, i], total[:, i], total[:, i - 1], ALU.add))
            dve.tensor_tensor(c[:, :, 1:NT], c[:, :, 1:NT], total[:, 0:NT - 1].rearrange("p n h -> p h n"),
                              ALU.add).then_inc(dve_steps, mark("c_ready"))

        def sp_naturals(sp):
            sp.dma_start(w_pl[:], A["w_pool"][0].rearrange("g c e -> c g e")).then_inc(sem("w_pool_in"), 16)
            sp.dma_start(kst[0:DECB * PBUF, 0, :],
                         A["state_pool"][0].rearrange("b t c -> (b t) c")).then_inc(sem("w_pool_in"), 16)
            sp.dma_start(O["pool_state_sample"][0, :, 0:PBUF - 1, :], A["state_pool"][0, :, 1:PBUF, :]).then_inc(sem("stored"), 16)

        def pe_naturals(pe):
            pe.wait_ge(sem("w_pool_in"), 32)
            pe.wait_ge(act_steps, step("gate_token_rows"))
            pe.wait_ge(set_free[1], G1["ab_u"])
            n_state = DECB * PBUF
            for g in range(4):
                mm = pe.transpose(ps[:, 7, n_state * g:n_state * (g + 1)], kst[0:n_state, 0, P * g:P * (g + 1)],
                                  ident[0:n_state, 0:n_state])
            mm.then_inc(pe_steps, mark("stateT_ready"))
            for n in range(2 * NT):
                if n >= 4:
                    pe.wait_ge(sem("k_copied" if n % 2 == 0 else "v_copied"), n // 2 - 1)
                for c in range(4):
                    mm = pe.transpose(ps[:, 3 + n % 4, P * c:P * (c + 1)],
                                      proj[:, 4 + 4 * (n % 2) + c, P * (n // 2):P * (n // 2 + 1)], ident[:])
                mm.then_inc(sem("natT_ready"), 1)
            pe.wait_ge(sem("state_taken"), 1)
            for c in range(4):
                mm = pe.transpose(ps[0:PBUF, 7, P * c:P * (c + 1)], proj[:, 12 + c, SEQ - PBUF:SEQ], ident[:])
            mm.then_inc(pe_steps, mark("ulastT_ready"))
            pe.wait_ge(sem("k_copied"), NT)
            pe.wait_ge(sem("v_copied"), NT)
            for c in range(16):
                mm = pe.transpose(ps[0:DECB, 3 + c // 4, P * (c % 4):P * (c % 4 + 1)], proj[:, c, SEQ:TOK], ident[:])
            mm.then_inc(pe_steps, mark("s_natT_ready"))

        def act_naturals(act):
            for i in range(NT):
                act.wait_ge(sem("natT_ready"), 2 * i + 1)
                if i >= 2:
                    act.wait_ge(sem(f"rows_stored{i % 2}"), 16 * (i // 2))
                elif i == 0:
                    act.wait_ge(pe_steps, step("stateT_ready"))
                act.copy(kst[:, i % 2], ps[:, 3 + (2 * i) % 4, :]).then_inc(sem("k_copied"), 1)
                act.wait_ge(sem("k_copied"), i + 1)
                act.dma_start(O["fox_k_prompt"][0, 0, P * i:P * (i + 1)].rearrange("t h d -> t (h d)"),
                              kst[:, i % 2]).then_inc(sem(f"rows_stored{i % 2}"), 16)
                act.wait_ge(sem("v_copied"), i + 1)
                act.dma_start(O["fox_v_prompt"][0, 0, P * i:P * (i + 1)].rearrange("t h d -> t (h d)").rearrange("t (c n) -> t c n", c=4),
                              proj[:, 8:12, P * i:P * (i + 1)]).then_inc(sem("stored"), 16)
            act.wait_ge(pe_steps, step("ulastT_ready"))
            act.copy(ulast[:], ps[0:PBUF, 7, :]).then_inc(act_steps, mark("ulast_ready"))
            act.wait_ge(act_steps, step("ulast_ready"))
            act.dma_start(O["pool_state_prompt"][0, 0], ulast[:]).then_inc(sem("stored"), 16)
            act.wait_ge(pe_steps, step("s_natT_ready"))
            act.copy(s_nat[:], ps[0:DECB, 3:7, :]).then_inc(act_steps, mark("s_nat_ready"))
            act.wait_ge(act_steps, step("s_nat_ready"))
            act.dma_start(q_d, s_nat[:, 0]).then_inc(sem("q_stored"), 16)
            act.dma_start(O["fox_k_sample"][0, :, 0].rearrange("b h d -> b (h d)"), s_nat[:, 1]).then_inc(sem("stored"), 16)
            act.dma_start(O["fox_v_sample"][0, :, 0].rearrange("b h d -> b (h d)"), s_nat[:, 2]).then_inc(sem("stored"), 16)
            act.dma_start(O["pool_state_sample"][0, :, PBUF - 1, :], s_nat[:, 3]).then_inc(sem("stored"), 16)

        def dve_naturals(dve):
            for i in range(NT):
                dve.wait_ge(sem("natT_ready"), 2 * i + 2)
                dve.tensor_copy(proj[:, 8:12, P * i:P * (i + 1)],
                                ps[:, 3 + (2 * i + 1) % 4, :].rearrange("p (c n) -> p c n", c=4)).then_inc(sem("v_copied"), 1)

        def dve_new_scores(dve):
            then = chain(dve, "dve_new_chain")
            dve.wait_ge(act_steps, step("s_nat_ready"))
            then(dve.tensor_tensor(s_qk[0:DECB, 0], s_nat[:, 0], s_nat[:, 1], ALU.mult))
            dve.tensor_reduce(tiny[0:DECB, 8:8 + FH], s_qk[0:DECB, 0].rearrange("b (h d) -> b h d", h=FH),
                              AX.X, ALU.add).then_inc(dve_steps, mark("new_scores"))

        def dve_state_sums(dve):
            dve.wait_ge(pe_steps, step("stateT_ready"))
            st = ps[:, 7, 0:4 * DECB * PBUF].rearrange("p (g b t) -> p g b t", g=4, t=PBUF)
            for g, w in enumerate(WINDOWS):
                dve.tensor_reduce(st_sum[:, g], st[:, g, :, PBUF - (w - 1):PBUF], AX.X,
                                  ALU.add).then_inc(sem("state_taken"), 1)

        windows = [win[:], prob[:].rearrange("p a n -> p (a n)")[:, 0:2 * TOK].rearrange("p (a n) -> p a n", a=2)]

        def dve_pool(dve):
            then = chain(dve, "dve_pool_chain")
            dve.wait_ge(dve_steps, step("inv_cnt_ready"))
            dve.wait_ge(sem("state_taken"), 4)
            dve.wait_ge(set_free[1], G1["ab_u"])
            dve.wait_ge(set_free[0], G1["ab_u"])
            dve.wait_ge(tile_done, 2 * G1["ab_u"])
            for g, w in enumerate(WINDOWS):
                u, us = proj[:, 12 + g, 0:SEQ], proj[:, 12 + g, SEQ:TOK]
                if g >= 2:
                    dve.wait_ge(sem("pool_products"), g - 1)
                src, span, slot = u, 1, 0
                while span < w:
                    dst = windows[g % 2][:, slot, 0:SEQ]
                    dve.tensor_copy(dst[:, 0:span], src[:, 0:span])
                    then(dve.tensor_tensor(dst[:, span:SEQ], src[:, span:SEQ], src[:, 0:SEQ - span], ALU.add))
                    src, span, slot = dst, 2 * span, 1 - slot
                out_s = windows[g % 2][:, g % 2, SEQ:TOK]
                dve.tensor_tensor(out_s, st_sum[:, g], us, ALU.add)
                then(dve.tensor_tensor(src[:, 0:16], src[:, 0:16], inv_cnt[:, g], ALU.mult))
                dve.tensor_tensor(src[:, 0:16], src[:, 0:16], u[:, 0:16], ALU.subtract)
                dve.scalar_tensor_tensor(out=out_s, in0=out_s, scalar=1.0 / w, in1=us,
                                         op0=ALU.mult, op1=ALU.subtract)
                dve.scalar_tensor_tensor(out=src[:, 16:SEQ], in0=src[:, 16:SEQ], scalar=1.0 / w, in1=u[:, 16:SEQ],
                                         op0=ALU.mult, op1=ALU.subtract).then_inc(sem("pool_ready"), 1)

        def pe_pool(pe):
            pe.wait_ge(set_free[0], G1["ab_u"])
            pe.wait_ge(act_steps, step("s_nat_ready"))
            for g in range(4):
                pe.wait_ge(sem("pool_ready"), g + 1)
                if g >= 2:
                    pe.wait_ge(sem("pool_copied"), g - 1)
                for t in range(NB):
                    mm = pe.matmul(ps_set[g % 2][:, t], w_pl[:, g], windows[g % 2][:, g % 2, TB * t:TB * (t + 1)],
                                   start=True, stop=True)
                mm.then_inc(sem("pool_products"), 1)

        def act_pool(act):
            for g in range(4):
                act.wait_ge(sem("pool_products"), g + 1)
                act.activation(blocks(proj[:, 12 + g]), ps_set[g % 2], ACT.Copy,
                               scale=col("pool_scale", g)).then_inc(sem("pool_copied"), 1)

        N_ATT = FH * NT
        score_ps = [ps[:, 0:2, :].rearrange("p a n -> p (a n)"), ps[:, 2:4, :].rearrange("p a n -> p (a n)")]
        pT_ps = ps[:, 4:6, :].rearrange("p a (b n) -> p (a b) n", n=P)

        def head_rows(h):
            return slice(FD * (h % 2), FD * (h % 2 + 1))

        def act_load_c(act, h):
            if h >= 2:
                act.wait_ge(sem("scores_shifted"), NT * (h - 1))
                act.wait_ge(sem("masked"), h - 1)
            act.dma_start(cb[:, h % 2], c_d[h:h + 1, :].to_broadcast([P, SEQ])).then_inc(sem(f"row_loaded{h % 2}"), 16)

        def pool_mask(pool, h):
            pool.wait_ge(sem(f"row_loaded{h % 2}"), 16 * (h // 2 + 1))
            if h >= 2:
                pool.wait_ge(sem("scores_shifted"), NT * (h - 1))
            pool.tensor_tensor(cbd[:, h % 2], cb[:, h % 2].rearrange("p (i n) -> p i n", n=P),
                               future[:].unsqueeze(1).to_broadcast([P, NT, P]), ALU.add).then_inc(sem("masked"), 1)

        def pe_scores(pe, n):
            h, i = divmod(n, NT)
            if n >= 2:
                pe.wait_ge(sem("scores_shifted"), n - 1)
            r = head_rows(h)
            for k0 in range(0, P * (i + 1), 512):
                k1 = min(k0 + 512, P * (i + 1))
                mm = pe.matmul(score_ps[n % 2][:, k0:k1], proj[r, h // 2, P * i:P * (i + 1)],
                               proj[r, 4 + h // 2, k0:k1], start=True, stop=True)
            mm.then_inc(sem("scores_ready"), 1)

        def dve_shift(dve, n):
            h, i = divmod(n, NT)
            dve.wait_ge(sem("scores_ready"), n + 1)
            if i == 0:
                dve.wait_ge(sem("masked"), h + 1)
            if n >= 3:
                dve.wait_ge(sem("pT_ready"), n - 2)
            if n >= 2:
                dve.wait_ge(sem("nmax_ready"), n - 1)
                dve.wait_ge(sem("exp_done"), n - 1)
            k, t0 = P * i, 2 * (n % 2)
            if i:
                dve.tensor_tensor_reduce(prob[:, n % 3, 0:k], score_ps[n % 2][:, 0:k], cb[:, h % 2, 0:k], 1.0, -BIG,
                                         ALU.subtract, ALU.max, tmax[:, t0:t0 + 1])
            dve.tensor_tensor_reduce(prob[:, n % 3, k:k + P], score_ps[n % 2][:, k:k + P], cbd[:, h % 2, i], 1.0, -BIG,
                                     ALU.subtract, ALU.max, tmax[:, t0 + 1:t0 + 2]).then_inc(sem("scores_shifted"), 1)
            dve.wait_ge(sem("scores_shifted"), n + 1)
            dve.tensor_reduce(nmax[:, n % 2:n % 2 + 1], tmax[:, t0 + (0 if i else 1):t0 + 2], AX.X, ALU.max,
                              negate=True).then_inc(sem("nmax_ready"), 1)

        def act_exp(act, n):
            k = P * (n % NT + 1)
            act.wait_ge(sem("nmax_ready"), n + 1)
            if n >= 2:
                act.wait_ge(sem("prob_ready"), n - 1)
            act.activation(prob[:, n % 3, 0:k], prob[:, n % 3, 0:k], ACT.Exp, bias=nmax[:, n % 2:n % 2 + 1],
                           accum_out=rsum[:, n % 2:n % 2 + 1]).then_inc(sem("exp_done"), 1)

        def dve_normalize(dve, n):
            k = P * (n % NT + 1)
            dve.wait_ge(sem("exp_done"), n + 1)
            chain(dve, "dve_")(dve.reciprocal(rinv[:, n % 2:n % 2 + 1], rsum[:, n % 2:n % 2 + 1]))
            dve.tensor_scalar(prob[:, n % 3, 0:k], prob[:, n % 3, 0:k], rinv[:, n % 2:n % 2 + 1], None,
                              ALU.mult).then_inc(sem("prob_ready"), 1)

        def pe_turn(pe, n):
            pe.wait_ge(sem("prob_ready"), n + 1)
            if n:
                pe.wait_ge(sem("pT_copied"), n)
            for j in range(n % NT + 1):
                mm = pe.transpose(pT_ps[:, j], prob[:, n % 3, P * j:P * (j + 1)], ident[:])
            mm.then_inc(sem("pT_ready"), 1)

        def act_turn(act, n):
            j = n % NT + 1
            act.wait_ge(sem("pT_ready"), n + 1)
            if n >= 2:
                act.wait_ge(sem("out_ready"), n - 1)
            act.copy(pT[:, n % 2, 0:j], pT_ps[:, 0:j]).then_inc(sem("pT_copied"), 1)

        def pe_values(pe, n):
            h, i = divmod(n, NT)
            pe.wait_ge(sem("pT_copied"), n + 1)
            if n:
                pe.wait_ge(sem("out_copied"), n)
            for j in range(i + 1):
                v0 = P * j + FD * (h % 2)
                mm = pe.matmul(ps[head_rows(h), 6, 0:P], proj[:, 8 + h // 2, v0:v0 + FD],
                               pT[:, n % 2, j], start=(j == 0), stop=(j == i))
            mm.then_inc(sem("out_ready"), 1)

        def act_out(act, n):
            h, i = divmod(n, NT)
            act.wait_ge(sem("out_ready"), n + 1)
            act.copy(proj[head_rows(h), h // 2, P * i:P * (i + 1)],
                     ps[head_rows(h), 6, 0:P]).then_inc(sem("out_copied"), 1)

        page_loaded = [sem(f"page_loaded{slot}") for slot in range(4)]
        pages_used = sem("pages_used")
        N_STEP = DECB * NPG // 2
        KEYS_END = 48
        VALUES_FROM = 50
        V_PER_TILE = N_STEP // (N_ATT + 2 - VALUES_FROM)

        def key_steps(n):
            return range(N_STEP * n // KEYS_END, N_STEP * (n + 1) // KEYS_END) if n < KEYS_END else range(0)

        def value_steps(n):
            return range(V_PER_TILE * (n - VALUES_FROM), V_PER_TILE * (n - VALUES_FROM + 1)) if n >= VALUES_FROM else range(0)

        def sample_done(n):
            u = V_PER_TILE * (n - VALUES_FROM)
            return u // (NPG // 2) - 1 if u > 0 and u % (NPG // 2) == 0 else None

        def sp_pages(sp):
            sp.wait_ge(sem("pages_in"), 16)
            sp.wait_ge(sem("q_stored"), 32)
            sp.wait_ge(sem("stored"), 16 * 13)
            sp.wait_ge(sem("lf_stored"), 48)
            sp.dma_start(lf_new[:], O["fox_logf_sample"].rearrange("a b t h -> a (b t h)").to_broadcast([P, DECB * FH])).then_inc(sem("new_in"), 16)
            sp.dma_start(sc_new[:], ks_d.rearrange("b h -> (b h)").unsqueeze(0)).then_inc(sem("new_in"), 16)

            def page(j):
                return sp.value_load(page_idx[0:1, ds(j, 1)], min_val=0, max_val=NPHYS - 1)

            def fill(slot, u, j, cache):
                sp.wait_ge(pages_used, u + 1)
                for e in range(2):
                    sp.dma_start(kpage[:, slot, e], cache[0, ds(page(j + e), 1)].rearrange("a t h d -> (a t) (h d)")
                                 ).then_inc(page_loaded[slot], 16)

            def keys(b2):
                for r in range(2):
                    u0 = (2 * b2 + r) * (NPG // 2)
                    sp.wait_ge(pages_used, u0 + 1)
                    sp.dma_start(qb[:, r], q_d[ds(2 * b2 + r, 1), :].to_broadcast([P, FW])).then_inc(sem(f"q_row_loaded{r}"), 16)
                    for v in range(NPG // 2):
                        fill(v % 4, u0 + v, 2 * (u0 + v), A["cache_fox_k"])
            loop(sp, DECB // 2, keys)

            def values(m):
                for slot in range(4):
                    fill(slot, N_STEP + 4 * m + slot, 2 * (4 * m + slot), A["cache_fox_v"])
            loop(sp, N_STEP // 4, values)

        def pool_keys(pool, u):
            b, slot = u // (NPG // 2), u % 4
            pool.wait_ge(page_loaded[slot], 32 * (u // 4 + 1))
            pool.wait_ge(sem(f"q_row_loaded{b % 2}"), 16 * (b // 2 + 1))
            pool.tensor_tensor(kpage[:, slot], kpage[:, slot], qb[:, b % 2].unsqueeze(1).to_broadcast([P, 2, FW]),
                               ALU.mult).then_inc(sem("keys_multiplied"), 1)

        def dve_keys(dve, u):
            b, g, slot = u // (NPG // 2), 2 * (u % (NPG // 2)), u % 4
            dve.wait_ge(sem("keys_multiplied"), u + 1)
            dve.tensor_reduce(sc[:, b, :, g:g + 2].rearrange("p h g -> p g h"),
                              kpage[:, slot].rearrange("p g (h d) -> p g h d", h=FH), AX.X,
                              ALU.add).then_inc(pages_used, 1)

        def pe_suffix(pe, q):
            pe.wait_ge(sem("lf_loaded"), 16 * DECB * NPG)
            if q:
                pe.wait_ge(sem("suffix_copied"), 2 * q)
            src = lf_flat[:, 256 * q:256 * (q + 1)]
            pe.matmul(ps[:, 7, 0:256], later[:], src, start=True, stop=True)
            pe.matmul(ps[:, 7, 256:512], ones[:], src, start=True, stop=True).then_inc(sem("suffix_ready"), 1)

        def dve_suffix(dve, q):
            dve.wait_ge(sem("suffix_ready"), q + 1)
            if q == 0:
                for r in range(2):
                    dve.wait_ge(sem(f"rows_stored{r}"), 16 * NT // 2)
            dve.tensor_copy(suf[:, 256 * q:256 * (q + 1)], ps[:, 7, 0:256]).then_inc(sem("suffix_copied"), 1)
            dve.tensor_copy(lf_flat[:, 256 * q:256 * (q + 1)], ps[:, 7, 256:512]).then_inc(sem("suffix_copied"), 1)

        def dve_later_pages(dve):
            then = chain(dve, "dve_pages_chain")
            dve.wait_ge(sem("suffix_copied"), 8)
            dve.wait_ge(sem("new_in"), 32)
            for g in range(NPG - 2, -1, -1):
                then(dve.tensor_tensor(lf_pg[:, :, g], lf_pg[:, :, g], lf_pg[:, :, g + 1], ALU.add))
            sv = suf.rearrange("p (b g h) -> p b g h", b=DECB, h=FH)
            then(dve.tensor_tensor(sv[:, :, 0:NPG - 1], sv[:, :, 0:NPG - 1], lf_pg[:, :, 1:NPG], ALU.add))
            then(dve.tensor_tensor(sv, sv, lf_new[:].rearrange("p (b h) -> p b h", b=DECB).unsqueeze(2)
                                   .to_broadcast([P, DECB, NPG, FH]), ALU.add))

        def dve_sample_softmax(dve):
            then = chain(dve, "dve_softmax_chain")
            dve.wait_ge(pages_used, N_STEP + 4)
            bh = "p (b h) -> p b h"
            past = sc[:, :, :, 0:NPG]
            sv = suf.rearrange("p (b g h) -> p b h g", b=DECB, h=FH)
            then(dve.tensor_tensor(past, past, sv, ALU.add))
            then(dve.tensor_copy(sc[0:1, :, :, NPG], sc_new[:].rearrange(bh, b=DECB)))
            dve.tensor_reduce(s_red[:, 0].rearrange(bh, b=DECB), sc[:], AX.X, ALU.max).then_inc(dve_steps, mark("s_max_ready"))
            dve.wait_ge(pool_steps, step("s_max_all"))
            dve.tensor_tensor(sc[:], sc[:], s_red[:, 1].rearrange(bh, b=DECB).unsqueeze(3)
                              .to_broadcast([P, DECB, FH, NPG + 1]), ALU.subtract).then_inc(dve_steps, mark("sc_shifted"))
            dve.wait_ge(act_steps, step("sc_exp"))
            dve.tensor_reduce(s_red[:, 2].rearrange(bh, b=DECB), sc[:], AX.X, ALU.add).then_inc(dve_steps, mark("s_sum_ready"))
            dve.wait_ge(pool_steps, step("s_sum_all"))
            then(dve.reciprocal(s_red[:, 3], s_red[:, 3]))
            dve.tensor_tensor(sc[:], sc[:], s_red[:, 3].rearrange(bh, b=DECB).unsqueeze(3)
                              .to_broadcast([P, DECB, FH, NPG + 1]), ALU.mult).then_inc(dve_steps, mark("sc_ready"))

        def pool_sample_softmax(pool):
            pool.wait_ge(dve_steps, step("s_max_ready"))
            pool.partition_all_reduce(s_red[:, 1], s_red[:, 0], P, RMAX).then_inc(pool_steps, mark("s_max_all"))
            pool.wait_ge(dve_steps, step("s_sum_ready"))
            pool.partition_all_reduce(s_red[:, 3], s_red[:, 2], P, RADD).then_inc(pool_steps, mark("s_sum_all"))

        def act_sample_softmax(act):
            act.wait_ge(dve_steps, step("sc_shifted"))
            act.activation(sc[:], sc[:], ACT.Exp).then_inc(act_steps, mark("sc_exp"))

        def pe_sample_values(pe, u):
            b, slot = u // (NPG // 2), u % 4
            pe.wait_ge(page_loaded[slot], 32 * ((N_STEP + u) // 4 + 1))
            if u == 0:
                pe.wait_ge(dve_steps, step("sc_ready"))
                pe.wait_ge(sem("suffix_copied"), 8)
            if u % (NPG // 2) == 0 and b:
                pe.wait_ge(sem("s_own_step"), 2 * b)
            for e in range(2):
                g = 2 * (u % (NPG // 2)) + e
                mm = pe.matmul(ps[0:FH, 7, :], sc[:, b, :, g], kpage[:, slot, e], start=(g == 0), stop=(g == NPG - 1))
            mm.then_inc(pages_used, 1)

        def dve_sample_own(dve, b):
            if b == 0:
                dve.wait_ge(pool_steps, step("own_ready"))
            dve.wait_ge(pages_used, N_STEP + 4 + (NPG // 2) * (b + 1))
            if b >= 2:
                dve.wait_ge(sem("s_columns"), b - 1)
            dve.tensor_tensor(qb[0:FH, b % 2], ps[0:FH, 7, :], own, ALU.mult).then_inc(sem("s_own_step"), 1)

        def pe_sample_columns(pe, b):
            pe.wait_ge(sem("s_own_step"), 2 * b + 1)
            for c in range(4):
                mm = pe.matmul(ps[:, 7, c:c + 1], qb[0:FH, b % 2, P * c:P * (c + 1)], ones[0:FH, 0:1], start=True, stop=True)
            mm.then_inc(sem("s_columns"), 1)

        def dve_sample_columns(dve, b):
            dve.wait_ge(sem("s_columns"), b + 1)
            dve.tensor_copy(s_sum[:, :, b], ps[:, 7, 0:4]).then_inc(sem("s_own_step"), 1)

        def pe_sample_new(pe):
            pe.wait_ge(sem("s_own_step"), 2 * DECB)
            pe.matmul(ps[:, 7, 128:192], ones[0:1, :], sc[0:1, :, :, NPG].rearrange("p b h -> p b h"),
                      start=True, stop=True).then_inc(pe_steps, mark("s_values_ready"))

        def dve_sample_out(dve):
            dve.wait_ge(pe_steps, step("s_values_ready"))
            p_new = ps[:, 7, 128:192].rearrange("p (b c r) -> p r c b", b=DECB, r=2)
            for r in range(2):
                rs = slice(FD * r, FD * (r + 1))
                ins = dve.tensor_tensor(s_new[rs], proj[rs, 8:12, SEQ:TOK], p_new[rs, r], ALU.mult)
            chain(dve, "dve_")(ins)
            for r in range(2):
                rs = slice(FD * r, FD * (r + 1))
                dve.tensor_tensor(proj[rs, 0:4, SEQ:TOK], s_new[rs], s_sum[rs], ALU.add).then_inc(sem("s_att_ready"), 1)

        def sp_attention(sp):
            sp_pages(sp)

        def pool_gates(pool):
            pool.wait_ge(sem("pages_in"), 16)

            def gates(j):
                page = pool.value_load(page_idx[0:1, ds(j, 1)], min_val=0, max_val=NPHYS - 1)
                pool.dma_start(lf_flat[:, ds(FH * j, FH)], A["cache_fox_logf"][0, ds(page, 1)].rearrange("a t h -> (a t) h")
                               ).then_inc(sem("lf_loaded"), 16)
            loop(pool, DECB * NPG, gates)

        def pool_own(pool):
            then = chain(pool, "pool_")
            pool.wait_ge(sem("pool_copied"), 4)
            then(pool.memset(own, 1.0))
            then(pool.affine_select(out=own, in_=own, compare_op=ALU.is_ge, fill=0.0, base=0,
                                    pattern=[[1, FW]], channel_multiplier=-FD))
            pool.affine_select(out=own, in_=own, compare_op=ALU.is_ge, fill=0.0, base=FD - 1,
                               pattern=[[-1, FW]], channel_multiplier=FD).then_inc(pool_steps, mark("own_ready"))

        def pool_attention(pool):
            pool.sem_inc(pages_used, 4)
            pool.wait_ge(dve_steps, step("new_scores"))
            pool_mask(pool, 0)
            for n in range(N_ATT):
                if n % NT == 4 and n // NT + 1 < FH:
                    pool_mask(pool, n // NT + 1)
                for u in key_steps(n):
                    pool_keys(pool, u)
                if n == 8:
                    pool_own(pool)
                if n == KEYS_END:
                    pool_sample_softmax(pool)

        def pe_attention(pe):
            pe.wait_ge(set_free[0], G1["ab_u"])
            pe.wait_ge(act_steps, step("s_nat_ready"))
            pe.wait_ge(sem("v_copied"), NT)
            pe.wait_ge(act_steps, step("ulast_ready"))
            pe.wait_ge(sem("pool_copied"), 4)
            pe_scores(pe, 0)
            for n in range(N_ATT + 2):
                if n + 1 < N_ATT:
                    pe_scores(pe, n + 1)
                if 1 <= n <= N_ATT:
                    pe_turn(pe, n - 1)
                if n >= 2:
                    pe_values(pe, n - 2)
                if 8 <= n < 12:
                    pe_suffix(pe, n - 8)
                if sample_done(n) is not None:
                    pe_sample_columns(pe, sample_done(n))
                for u in value_steps(n):
                    pe_sample_values(pe, u)
            pe_sample_columns(pe, DECB - 1)
            pe_sample_new(pe)

        def act_attention(act):
            for n in range(N_ATT + 2):
                if n < N_ATT:
                    act_exp(act, n)
                    if n % NT == NT - 1 and n // NT + 2 < FH:
                        act_load_c(act, n // NT + 2)
                if 1 <= n <= N_ATT:
                    act_turn(act, n - 1)
                if n >= 2:
                    act_out(act, n - 2)
                if n == KEYS_END:
                    act_sample_softmax(act)
            for k in range(DC):
                if k == 0:
                    act.wait_ge(sem("s_att_ready"), 2)
                    act.wait_ge(sem("out_copied"), N_ATT)
                act.copy(xs[:, 0, k], proj[:, AB_CHUNKS[k]]).then_inc(sem("xs_hi"), 1)

        AB_CHUNKS = (0, 1, 2, 3, 12, 13, 14, 15)

        def dve_attention(dve):
            dve.wait_ge(sem("pool_copied"), 4)
            dve.memset(sc[:, :, :, NPG], -BIG).then_inc(dve_steps, mark("sc_cleared"))
            dve.wait_ge(dve_steps, step("sc_cleared"))
            for n in range(N_ATT + 2):
                if n < N_ATT:
                    dve_shift(dve, n)
                if 1 <= n <= N_ATT:
                    dve_normalize(dve, n - 1)
                for u in key_steps(n):
                    dve_keys(dve, u)
                if 9 <= n < 13:
                    dve_suffix(dve, n - 9)
                if n == 13:
                    dve_later_pages(dve)
                if n == KEYS_END:
                    dve_sample_softmax(dve)
                if sample_done(n) is not None:
                    dve_sample_own(dve, sample_done(n))
                    dve_sample_columns(dve, sample_done(n))
            dve_sample_own(dve, DECB - 1)
            dve_sample_columns(dve, DECB - 1)
            dve_sample_out(dve)
            for k in range(DC):
                split_act_lo(dve, k, proj[:, AB_CHUNKS[k]], DC + k + 1)

        def dve_residual(first, alpha):
            def evac(s, i, g):
                dve = nc.vector
                dve.wait_ge(tile_done, 2 * g + s + 1)
                xm = blocks(chunk(x, 2 * i + s))
                if alpha:
                    ins = dve.scalar_tensor_tensor(out=xm, in0=xm, scalar=ALPHA, in1=ps_set[s], op0=ALU.mult, op1=ALU.add)
                else:
                    ins = dve.tensor_tensor(xm, xm, ps_set[s], ALU.add)
                ins.then_inc(set_free[s], 1)
            return evac

        def act_square(ln):
            def evac(s, i, g):
                act = nc.scalar
                act.wait_ge(set_free[s], g + 1)
                act.wait_ge(sem("sq_used"), DC * ln + 2 * i + s + 1)
                settle(act)
                act.activation(sq[:], chunk(x, 2 * i + s), ACT.Square).then_inc(sem("sq_ready"), 1)
            return evac

        def pool_sums(pool, name, ln):
            g0, cnt = G0[name], G1[name] - G0[name]
            if ln:
                pool.wait_ge(sem("ln_scaled"), DC * ln)
                pool.wait_ge(sem("ln_shifted"), DC * ln)
            if ln in (2, 5):
                pool.wait_ge(sem("ff_hi"), FFC * (ln // 3 + 1) + 1)
                pool.wait_ge(sem("ff_lo"), FFC * (ln // 3 + 1) + 1)
            if ln in (0, 3):
                pool.wait_ge(sem("xs_lo"), XS_LO_MIXER[ln // 3])
            then = chain(pool, f"pool_ln{ln}")
            then(pool.memset(sum_x[:], 0.0))
            then(pool.memset(sum_sq[:], 0.0))

            def body(i):
                for s in range(2):
                    m = DC * ln + 2 * i + s
                    pool.wait_ge(set_free[s], g0 + i + 1)
                    pool.wait_ge(sem("sum_x_ready"), m + 1)
                    pool.tensor_tensor(sum_x[:], sum_x[:], chunk(x, 2 * i + s), ALU.add).then_inc(sem("sum_x_ready"), 1)
                    pool.wait_ge(sem("sq_ready"), m + 1)
                    pool.wait_ge(sem("sq_used"), m + 1)
                    pool.tensor_tensor(sum_sq[:], sum_sq[:], sq[:], ALU.add).then_inc(sem("sq_used"), 1)
            loop(pool, cnt, body)

        def pe_norm(pe, ln, g_end):
            pe.wait_ge(sem("sum_x_ready"), DC * (ln + 1) + 1)
            pe.wait_ge(set_free[0], g_end)
            pe.wait_ge(set_free[1], g_end)
            for t in range(NB):
                pe.matmul(ps_set[0][:, t], ones[:], sum_x[:, TB * t:TB * (t + 1)], start=True, stop=True)
            pe.wait_ge(sem("sq_used"), DC * (ln + 1) + 1)
            for t in range(NB):
                mm = pe.matmul(ps_set[1][:, t], ones[:], sum_sq[:, TB * t:TB * (t + 1)], start=True, stop=True)
            mm.then_inc(sem("ln_sums"), 1)

        def act_norm_stats(act, ln):
            act.wait_ge(sem("ln_sums"), ln + 1)
            act.activation(blocks(sq[:]), ps_set[0], ACT.Square, scale=1.0 / D).then_inc(sem("ln_act_step"), 1)
            act.wait_ge(sem("ln_dve_step"), 2 * ln + 1)
            chain(act, "act_")(act.activation(sum_sq[:], sum_sq[:], ACT.Ln, bias=eps[:, 0:1]))
            act.activation(sum_sq[:], sum_sq[:], ACT.Exp, scale=-0.5).then_inc(sem("ln_act_step"), 1)

        def dve_norm_stats(dve, ln):
            dve.wait_ge(sem("ln_act_step"), 2 * ln + 1)
            dve.scalar_tensor_tensor(out=blocks(sum_sq[:]), in0=ps_set[1], scalar=1.0 / D, in1=blocks(sq[:]),
                                     op0=ALU.mult, op1=ALU.subtract).then_inc(sem("ln_dve_step"), 1)
            dve.wait_ge(sem("ln_act_step"), 2 * ln + 2)
            dve.scalar_tensor_tensor(out=blocks(sum_x[:]), in0=ps_set[0], scalar=-1.0 / D, in1=blocks(sum_sq[:]),
                                     op0=ALU.mult, op1=ALU.mult).then_inc(sem("ln_dve_step"), 1)

        def dve_norm_scale(dve, ln, k):
            xk = chunk(x, k)
            dve.tensor_tensor(xk, xk, sum_sq[:], ALU.mult).then_inc(sem("ln_scaled"), 1)

        def pool_norm_shift(pool, ln, k):
            pool.wait_ge(sem("ln_dve_step"), 2 * ln + 2)
            pool.wait_ge(sem("ln_scaled"), DC * ln + k + 1)
            xk = chunk(x, k)
            pool.tensor_tensor(xk, xk, sum_x[:], ALU.add).then_inc(sem("ln_shifted"), 1)

        def act_norm_affine(act, ln, k):
            g = cols[:, ds(LN_G[ln] + k, 1)]
            b = cols[:, ds(LN_B[ln] + k, 1)]
            act.wait_ge(sem("ln_shifted"), DC * ln + k + 1)
            settle(act)
            act.activation(xs[:, 0, ds(k, 1)].rearrange("p a n -> p (a n)"), chunk(x, k), ACT.Identity, bias=b, scale=g)
            act.activation(chunk(x, k), chunk(x, k), ACT.Identity, bias=b, scale=g).then_inc(sem("ln_x"), 1)

        def dve_norm_lo(dve, ln, k):
            dve.wait_ge(sem("ln_x"), DC * ln + k + 1)
            dve.tensor_tensor(xs[:, 1, ds(k, 1)].rearrange("p a n -> p (a n)"), chunk(x, k),
                              xs[:, 0, ds(k, 1)].bitcast(F32).rearrange("p a n -> p (a n)"),
                              ALU.subtract).then_inc(sem("ln_lo"), 1)

        LN_G, LN_B = [], []
        for L in range(DEPTH):
            for which in ("ln_mix", "ln_x", "ln_ff"):
                LN_G.append(COL[which + "_g"] + DC * L)
                LN_B.append(COL[which + "_b"] + DC * L)

        XS_LO_MIXER = (2 * DC, 4 * DC)

        mk_nat = qx[:, 2:4, 0:D]
        v_tmp = qx[:, 0:2, 0:NMEM]

        def sp_memory(sp, L):
            sp.wait_ge(sem("xs_lo"), XS_LO_MIXER[L])
            sp.dma_start(mem_n[:], A["mem_prompt"][0].rearrange("(a p) d -> p a d", p=P)).then_inc(sem("mem_in"), 16)

        def sp_memory_out(sp, L):
            for out, src in (("mem_k_prompt", mk_nat), ("mem_v_prompt", mem_n[:])):
                sp.wait_ge(sem("mem_rows"), 16 * L + (10 if out == "mem_k_prompt" else 18))
                sp.dma_start(O[out][L, 0].rearrange("(a p) h d -> p a (h d)", p=P), src).then_inc(sem(out + "_stored"), 16)

        def pe_memory_turn(pe, L):
            pe.wait_ge(sem("mem_in"), 16 * (L + 1))
            for r in range(2):
                if r or L:
                    pe.wait_ge(sem("mem_lo"), 2 * L + r)
                for c in range(4):
                    for a in range(2):
                        mm = pe.transpose(ps[:, 6 + c // 2, NMEM * (c % 2) + P * a:NMEM * (c % 2) + P * (a + 1)],
                                          mem_n[:, a, P * (4 * r + c):P * (4 * r + c + 1)], ident[:])
                mm.then_inc(sem("memT_ready"), 1)

        def mem_ps(r):
            return ps[:, 6:8, :].rearrange("p a (c m) -> p (a c) m", m=NMEM)

        def act_memory_turn(act, L):
            for r in range(2):
                act.wait_ge(sem("memT_ready"), 2 * L + r + 1)
                act.copy(mem_s[:, 0, 4 * r:4 * r + 4], mem_ps(r)).then_inc(sem("mem_hi"), 1)

        def dve_memory_turn(dve, L):
            for r in range(2):
                dve.wait_ge(sem("mem_hi"), 2 * L + r + 1)
                dve.tensor_tensor(mem_s[:, 1, 4 * r:4 * r + 4], mem_ps(r), mem_s[:, 0, 4 * r:4 * r + 4].bitcast(F32),
                                  ALU.subtract).then_inc(sem("mem_lo"), 1)

        def sp_mem_weights(sp, L):
            wk, wv = kview(A["w_xk"][L]), kview(A["w_xv"][L])
            g0 = G0[f"mem{L}"]
            for q, w in enumerate((wk, wv)):
                loop(sp, 4, lambda i: load_pair(sp, g0 + 4 * q + i, w[:, :, ds(256 * i, P)], w[:, :, ds(256 * i + P, P)]))

        def pe_memory(pe, L, ln):
            pe.wait_ge(sem("mem_lo"), 2 * (L + 1))
            pe.wait_ge(sem("ln_dve_step"), 2 * ln + 2)
            g0 = G0[f"mem{L}"]
            for q in range(2):
                def body(i):
                    g = g0 + 4 * q + i
                    for s in range(2):
                        product_tile(pe, s, g, mem_s, n=1, width=NMEM)
                    for s in range(2):
                        src = v_tmp[:, s]
                        pe.wait_ge(set_free[s], g + 1)
                        pe.wait_ge(sem("mem_rows"), 16 * L + 8 * q + 2 * i + s + 1)
                        for a in range(2):
                            mm = pe.transpose(ps[:, 6 + s, P * a:P * (a + 1)],
                                              src[:, P * a:P * (a + 1)], ident[:])
                        mm.then_inc(sem("mem_rowsT"), 1)
                loop(pe, 4, body)

        def act_memory(act, L, ln):
            g0 = G0[f"mem{L}"]
            for q in range(2):
                def body(i):
                    g = g0 + 4 * q + i
                    for s in range(2):
                        split_hi(act, 1 - s, g + s)
                        act.wait_ge(tile_done, 2 * g + s + 1)
                        act.wait_ge(sem("mem_rowsT"), 16 * L + 8 * q + 2 * i + s + 1)
                        if q == 0:
                            act.copy(chunk(mkT, 2 * i + s), ps[:, 3 * s, 0:NMEM]).then_inc(sem("mkT_ready"), 1)
                        act.copy(v_tmp[:, s], ps[:, 3 * s, 0:NMEM]).then_inc(set_free[s], 1)
                    act_norm_affine(act, ln, 4 * q + i)
                loop(act, 4, body)

        def dve_memory(dve, L, ln):
            g0 = G0[f"mem{L}"]
            dve_norm_scale(dve, ln, 0)
            for q in range(2):
                def body(i, last=False):
                    g = g0 + 4 * q + i
                    split_lo(dve, 1, g)
                    split_lo(dve, 0, g + 1)
                    if not last:
                        dve_norm_scale(dve, ln, 4 * q + i + 1)
                    for s in range(2):
                        m = 16 * L + 8 * q + 2 * i + s
                        dve.wait_ge(sem("mem_rowsT"), m + 3)
                        dst = (mk_nat if q == 0 else mem_n[:])[:, :, ds(P * (2 * i + s), P)]
                        dve.tensor_copy(dst, ps[:, 6 + s, 0:2 * P].rearrange("p (a n) -> p a n", a=2)).then_inc(sem("mem_rows"), 1)
                    dve_norm_lo(dve, ln, 4 * q + i)
                if q == 0:
                    loop(dve, 4, body)
                else:
                    loop(dve, 3, body)
                    body(3, last=True)

        def pool_memory(pool, L, ln):
            loop(pool, DC, lambda i: pool_norm_shift(pool, ln, i))

        xT_ps = ps[:, 4:6, :].rearrange("p a (b n) -> p (a b) n", n=P)
        xo_ps = ps[:, 6:8, :].rearrange("p a (b n) -> p (a b) n", n=P)
        qx_d = [scratch(f"qx_d{L}", [DECB, D]) for L in range(DEPTH)]

        def square(w):
            v = kview(w)
            return lambda i: (v[:, :, ds(256 * i, P)], v[:, :, ds(256 * i + P, P)])

        def act_xq(act, L):
            def evac(s, i, g):
                act.activation(blocks(chunk(qx, 2 * i + s)), ps_set[s], ACT.Copy, scale=MD ** -0.5).then_inc(set_free[s], 1)
            act.wait_ge(sem("mem_k_prompt_stored"), 16 * (L + 1))
            act_stream(act, f"xq{L}", evac)

        def sp_cross(sp, L):
            sp.wait_ge(tile_done, 2 * G1[f"xq{L}"])
            for f in range(2 * DECB):
                if f >= 4:
                    if f - 4 < DECB:
                        sp.wait_ge(sem("mk_used"), DECB * L + f - 3)
                    else:
                        sp.wait_ge(sem("mv_used"), (DECB + 1) * L + f - 3 - DECB)
                cache = A["cache_mem_k"] if f < DECB else A["cache_mem_v"]
                sp.dma_start(mkv[:, f % 4], cache[L, f % DECB].rearrange("(a p) h d -> p a (h d)", p=P)).then_inc(sem(f"mkv_loaded{f % 4}"), 16)
                if f < DECB:
                    if f == 0:
                        sp.wait_ge(sem("q_stored"), 16 * (L + 3))
                    if f >= 2:
                        sp.wait_ge(sem("mk_used"), DECB * L + f - 1)
                    sp.dma_start(qbx[:, f % 2], qx_d[L][f:f + 1, :].to_broadcast([P, D])).then_inc(sem(f"q_row_loaded{f % 2}"), 16)

        def pe_cross(pe, L):
            N0 = NT * L
            for s in range(2):
                pe.wait_ge(set_free[s], G1[f"xq{L}"])
            for c in range(DC):
                mm = pe.transpose(ps[0:DECB, 6 + c // 4, P * (c % 4):P * (c % 4 + 1)], qx[:, c, SEQ:TOK], ident[:])
            mm.then_inc(sem("qnT_ready"), 1)

            def scores(i):
                if i >= 2:
                    pe.wait_ge(sem("x_exp"), MH * (N0 + i - 1))
                for h in range(MH):
                    for kc in range(2):
                        mm = pe.matmul(ps[:, 2 * (i % 2) + h // 2, NMEM * (h % 2):NMEM * (h % 2 + 1)],
                                       qx[:, 2 * h + kc, P * i:P * (i + 1)], mkT[:, 2 * h + kc],
                                       start=(kc == 0), stop=(kc == 1))
                mm.then_inc(sem("x_scores"), 1)

            def turn(i):
                pe.wait_ge(sem("x_prob"), N0 + i + 1)
                if i:
                    pe.wait_ge(sem("x_pT"), N0 + i)
                for j in range(2 * MH):
                    mm = pe.transpose(xT_ps[:, j], probx[:, i % 2, P * j:P * (j + 1)], ident[:])
                mm.then_inc(sem("x_turned"), 1)

            def values(i):
                pe.wait_ge(sem("x_pT"), N0 + i + 1)
                if i:
                    pe.wait_ge(sem("x_out"), (NT + 1) * L + i)
                else:
                    pe.wait_ge(sem("qn_ready"), L + 1)
                for h in range(MH):
                    for dc in range(2):
                        for a in range(2):
                            mm = pe.matmul(xo_ps[:, 2 * h + dc], mem_n[:, a, MD * h + P * dc:MD * h + P * (dc + 1)],
                                           pTx[:, i % 2, 2 * h + a], start=(a == 0), stop=(a == 1))
                mm.then_inc(sem("x_values"), 1)

            pe.wait_ge(sem("mkT_ready"), DC * (L + 1))
            pe.wait_ge(sem("mem_rows"), 16 * (L + 1) + 2)
            scores(0)
            for i in range(NT + 2):
                if i + 1 < NT:
                    scores(i + 1)
                if 1 <= i <= NT:
                    turn(i - 1)
                if i >= 2:
                    values(i - 2)
            pe.wait_ge(sem("smx_dve_step"), 5 * L + 4)
            pe.wait_ge(sem("x_exp"), MH * (N0 + NT))
            for b in range(DECB):
                pe.wait_ge(sem(f"mkv_loaded{b % 4}"), 16 * (4 * L + 2 + b // 4 + 1))
                for a in range(2):
                    for r in range(2):
                        mm = pe.matmul(ps[0:MH * DECB, r, :], smz[:, b, a].rearrange("p h b -> p (h b)"),
                                       mkv[:, b % 4, a, 512 * r:512 * (r + 1)], start=(b == 0 and a == 0),
                                       stop=(b == DECB - 1 and a == 1))
                mm.then_inc(sem("mv_used"), 1)
            pe.wait_ge(sem("smx_dve_step"), 5 * L + 5)
            for c in range(DC):
                mm = pe.matmul(ps[:, 2, DECB * c:DECB * (c + 1)], probx[0:MH * DECB, 0, P * c:P * (c + 1)], sel_b[:],
                               start=True, stop=True)
            mm.then_inc(sem("mv_used"), 1)

        def act_cross(act, L):
            N0 = NT * L
            act.wait_ge(tile_done, 2 * G1[f"xq{L}"])
            act.wait_ge(sem("qnT_ready"), L + 1)
            act.copy(qn[:], ps[0:DECB, 6:8, :].rearrange("p a n -> p (a n)")).then_inc(sem("qn_ready"), 1)
            act.wait_ge(sem("qn_ready"), L + 1)
            act.dma_start(qx_d[L], qn[:]).then_inc(sem("q_stored"), 16)
            for i in range(NT + 2):
                if i < NT:
                    act.wait_ge(sem("x_max"), N0 + i + 1)
                    if i >= 2:
                        act.wait_ge(sem("x_turned"), N0 + i - 1)
                        act.wait_ge(sem("x_prob"), N0 + i - 1)
                    for h in range(MH):
                        m = MH * (i % 2) + h
                        act.activation(probx[:, i % 2, NMEM * h:NMEM * (h + 1)],
                                       ps[:, 2 * (i % 2) + h // 2, NMEM * (h % 2):NMEM * (h % 2 + 1)], ACT.Exp,
                                       bias=nmax[:, m:m + 1], accum_out=rsum[:, m:m + 1]).then_inc(sem("x_exp"), 1)
                if 1 <= i <= NT:
                    act.wait_ge(sem("x_turned"), N0 + i)
                    if i >= 3:
                        act.wait_ge(sem("x_values"), N0 + i - 2)
                    act.copy(pTx[:, (i - 1) % 2], xT_ps).then_inc(sem("x_pT"), 1)
                if i >= 2:
                    act.wait_ge(sem("x_values"), N0 + i - 1)
                    act.copy(qx[:, :, P * (i - 2):P * (i - 1)], xo_ps).then_inc(sem("x_out"), 1)
                if i == NT:
                    act.wait_ge(sem("smx_dve_step"), 5 * L + 2)
                    act.activation(smx[:], smx[:], ACT.Exp).then_inc(sem("smx_exp"), 1)
            act.wait_ge(sem("mv_used"), (DECB + 1) * (L + 1))
            act.copy(qx[:, :, SEQ:TOK], ps[:, 2, 0:64].rearrange("p (c b) -> p c b", c=DC)).then_inc(sem("x_out"), 1)
            act.wait_ge(sem("x_out"), (NT + 1) * (L + 1))
            for k in range(DC):
                act.copy(xs[:, 0, k], qx[:, k]).then_inc(sem("xs_hi"), 1)

        def dve_cross(dve, L, hi0):
            N0 = NT * L
            then = chain(dve, f"dve_cross{L}")

            def keys(b):
                dve.wait_ge(sem(f"mkv_loaded{b % 4}"), 16 * (4 * L + b // 4 + 1))
                dve.wait_ge(sem(f"q_row_loaded{b % 2}"), 16 * (DECB // 2 * (L + 1) + b // 2 + 1))
                for a in range(2):
                    for h in range(MH):
                        kv = mkv[:, b % 4, a, MD * h:MD * (h + 1)]
                        ins = dve.tensor_tensor_reduce(kv, kv, qbx[:, b % 2, MD * h:MD * (h + 1)], 1.0, 0.0,
                                                       ALU.mult, ALU.add, smx[:, b, a, h:h + 1])
                ins.then_inc(sem("mk_used"), 1)

            for i in range(NT + 1):
                if i < NT:
                    dve.wait_ge(sem("x_scores"), N0 + i + 1)
                    if i >= 2:
                        dve.wait_ge(sem("x_exp"), MH * (N0 + i - 1))
                    dve.tensor_reduce(nmax[:, MH * (i % 2):MH * (i % 2 + 1)],
                                      ps[:, 2 * (i % 2):2 * (i % 2) + 2, :].rearrange("p a (h m) -> p (a h) m", m=NMEM),
                                      AX.X, ALU.max, negate=True).then_inc(sem("x_max"), 1)
                if i:
                    j = (i - 1) % 2
                    dve.wait_ge(sem("x_exp"), MH * (N0 + i))
                    then(dve.reciprocal(rinv[:, MH * j:MH * (j + 1)], rsum[:, MH * j:MH * (j + 1)]))
                    pv = probx[:, j].rearrange("p (h m) -> p h m", h=MH)
                    dve.tensor_tensor(pv, pv, rinv[:, MH * j:MH * (j + 1)].unsqueeze(2).to_broadcast([P, MH, NMEM]),
                                      ALU.mult).then_inc(sem("x_prob"), 1)
                if i < NT:
                    keys(i)
            dve.wait_ge(sem("mk_used"), DECB * (L + 1))
            flat = "p b a h -> p b h a"
            then(dve.tensor_reduce(smr[:, 0], smx[:].rearrange(flat), AX.X, ALU.max))
            dve.sem_inc(sem("smx_dve_step"), 1)
            dve.wait_ge(sem("smx_pool_step"), 3 * L + 2)
            dve.tensor_tensor(smx[:], smx[:], smr[:, 1].unsqueeze(2).to_broadcast([P, DECB, 2, MH]),
                              ALU.subtract).then_inc(sem("smx_dve_step"), 1)
            dve.wait_ge(sem("smx_exp"), L + 1)
            then(dve.tensor_reduce(smr[:, 2], smx[:].rearrange(flat), AX.X, ALU.add))
            dve.sem_inc(sem("smx_dve_step"), 1)
            dve.wait_ge(sem("smx_pool_step"), 3 * L + 3)
            then(dve.reciprocal(smr[:, 3], smr[:, 3]))
            for b in range(DECB):
                ins = dve.tensor_tensor(smz[:, b, :, :, b], smx[:, b], smr[:, 3, b].unsqueeze(1).to_broadcast([P, 2, MH]), ALU.mult)
            ins.then_inc(sem("smx_dve_step"), 1)
            dve.wait_ge(sem("mv_used"), (DECB + 1) * L + DECB)
            dve.wait_ge(sem("x_turned"), NT * (L + 1))
            dve.tensor_tensor(probx[0:MH * DECB, 0].rearrange("p (h d) -> p h d", h=MH),
                              ps[0:MH * DECB, 0:2, :].rearrange("p a (h d) -> p (a h) d", d=MD),
                              own_x[:], ALU.mult).then_inc(sem("smx_dve_step"), 1)
            for k in range(DC):
                split_act_lo(dve, k, qx[:, k], hi0 + k + 1)

        def pool_cross(pool, L):
            then = chain(pool, "pool_")
            pool.wait_ge(sem("q_stored"), 16 * (L + 3))
            then(pool.memset(smz[:], 0.0))
            then(pool.memset(own_x[:], 1.0))
            then(pool.affine_select(out=own_x[:], in_=own_x[:], compare_op=ALU.is_ge, fill=0.0, base=0,
                                    pattern=[[-DECB, MH], [0, MD]], channel_multiplier=1))
            pool.affine_select(out=own_x[:], in_=own_x[:], compare_op=ALU.is_ge, fill=0.0, base=DECB - 1,
                               pattern=[[DECB, MH], [0, MD]], channel_multiplier=-1).then_inc(sem("smx_pool_step"), 1)
            pool.wait_ge(sem("smx_dve_step"), 5 * L + 1)
            pool.partition_all_reduce(smr[:, 1], smr[:, 0], P, RMAX).then_inc(sem("smx_pool_step"), 1)
            pool.wait_ge(sem("smx_dve_step"), 5 * L + 3)
            pool.partition_all_reduce(smr[:, 3], smr[:, 2], P, RADD).then_inc(sem("smx_pool_step"), 1)

        def act_norm(act, ln):
            act_norm_stats(act, ln)
            loop(act, DC, lambda k: act_norm_affine(act, ln, k))

        def pool_norm(pool, ln):
            loop(pool, DC, lambda k: pool_norm_shift(pool, ln, k))

        def dve_norm(dve, ln):
            dve_norm_stats(dve, ln)
            dve_norm_scale(dve, ln, 0)

            def body(k):
                dve_norm_scale(dve, ln, k + 1)
                dve_norm_lo(dve, ln, k)
            loop(dve, DC - 1, body)
            dve_norm_lo(dve, ln, DC - 1)

        def ff_base(L, q):
            return FFC * L + sum(FF_GROUPS[:q])

        def sp_ff(sp, L):
            wg, wu, wd = kview(A["w_gate"][L]), kview(A["w_up"][L]), A["w_down"][L]
            for q, nc_ in enumerate(FF_GROUPS):
                c0 = sum(FF_GROUPS[:q])
                sp_stream(sp, f"gu{L}_{q}", lambda i: (wg[:, :, ds(P * (c0 + i), P)], wu[:, :, ds(P * (c0 + i), P)]))
                v = kview(wd, (P * c0, P * (c0 + nc_)))
                sp_stream(sp, f"down{L}_{q}", lambda i: (v[:, :, ds(256 * i, P)], v[:, :, ds(256 * i + P, P)]), nk=nc_)

        def pe_ff(pe, L):
            for q, n in enumerate(FF_GROUPS):
                pe_stream(pe, f"gu{L}_{q}", xs, split=(sem("ln_lo"), DC * (3 * L + 1)) if q == 0 else None)
                pe.wait_ge(sem("ff_lo"), ff_base(L, q) + n + 1)
                pe_stream(pe, f"down{L}_{q}", hs, nk=n)

        def act_ff(act, L):
            for q, n in enumerate(FF_GROUPS):
                j0 = ff_base(L, q)

                def evac(s, i, g):
                    if s == 0:
                        act.wait_ge(set_free[1], g)
                        settle(act)
                        act.activation(blocks(sq[:]), ps_set[0], ACT.Silu).then_inc(set_free[0], 1)
                    else:
                        act.wait_ge(set_free[1], g + 1)
                        settle(act)
                        act.copy(hs[:, 0, ds(i, 1)].rearrange("p a n -> p (a n)"), sum_x[:]).then_inc(sem("ff_hi"), 1)
                act_stream(act, f"gu{L}_{q}", evac)
                act_stream(act, f"down{L}_{q}", act_square(3 * L + 2) if q == 2 else None)

        def dve_ff(dve, L):
            dve.wait_ge(sem("ln_shifted"), DC * (3 * L + 2))
            for q, n in enumerate(FF_GROUPS):
                j0 = ff_base(L, q)

                def evac(s, i, g):
                    if s == 0:
                        return
                    dve.wait_ge(set_free[0], g + 1)
                    dve.wait_ge(tile_done, 2 * g + 2)
                    dve.wait_ge(sem("ff_hi"), j0 + i + 1)
                    dve.wait_ge(sem("ff_lo"), j0 + i + 1)
                    dve.tensor_tensor(blocks(sum_x[:]), blocks(sq[:]), ps_set[1], ALU.mult).then_inc(set_free[1], 1)
                    dve.wait_ge(sem("ff_hi"), j0 + i + 2)
                    dve.tensor_tensor(hs[:, 1, ds(i, 1)].rearrange("p a n -> p (a n)"), sum_x[:],
                                      hs[:, 0, ds(i, 1)].bitcast(F32).rearrange("p a n -> p (a n)"),
                                      ALU.subtract).then_inc(sem("ff_lo"), 1)
                dve_stream(dve, f"gu{L}_{q}", evac)
                dve_stream(dve, f"down{L}_{q}", dve_residual(False, q == 0))

        LAST = 3 * DEPTH - 1

        def pe_output(pe):
            for c in range(DC):
                pe.wait_ge(sem("ln_x"), DC * LAST + c + 1)
                if c >= 2:
                    pe.wait_ge(sem("xT_copied"), len(tiles) + c - 1)
                b = 3 * (c % 2)
                for n, (t0, m) in enumerate(tiles):
                    mm = pe.transpose(ps[0:m, b + n // 4, P * (n % 4):P * (n % 4 + 1)], x[:, c, t0:t0 + m], ident[:])
                mm.then_inc(sem("xT_ready"), 1)

        def act_last_norm(act):
            act_norm_stats(act, LAST)
            for k in range(DC):
                act.wait_ge(sem("ln_shifted"), DC * LAST + k + 1)
                act.activation(x[:, k], x[:, k], ACT.Identity, bias=cols[:, LN_B[LAST] + k:LN_B[LAST] + k + 1],
                               scale=cols[:, LN_G[LAST] + k:LN_G[LAST] + k + 1]).then_inc(sem("ln_x"), 1)

        def dve_output(dve):
            dve_norm_stats(dve, LAST)
            dve_norm_scale(dve, LAST, 0)
            dve_norm_scale(dve, LAST, 1)
            for c in range(DC):
                if c + 2 < DC:
                    dve_norm_scale(dve, LAST, c + 2)
                dve.wait_ge(sem("xT_ready"), len(tiles) + c + 1)
                if c >= 2:
                    dve.wait_ge(sem(f"rows_stored{c % 2}"), 16 * (NT // 2 + 2 * (c // 2)))
                b = 3 * (c % 2)
                dve.tensor_copy(y_out[:, c % 2], ps[:, b:b + 2, :].rearrange("p a (n e) -> p (a n) e", e=P))
                dve.tensor_copy(y_s[:, c % 2], ps[0:DECB, b + 2, 0:P]).then_inc(sem("xT_copied"), 1)

        def sp_output(sp):
            for c in range(DC):
                sp.wait_ge(sem("xT_copied"), len(tiles) + c + 1)
                cs = slice(P * c, P * (c + 1))
                sp.dma_start(O["y_prompt"][0].rearrange("(n p) d -> p n d", p=P)[:, :, cs], y_out[:, c % 2]).then_inc(sem(f"rows_stored{c % 2}"), 16)
                sp.dma_start(O["y_sample"][:, 0, cs], y_s[:, c % 2]).then_inc(sem(f"rows_stored{c % 2}"), 16)
            for r in range(2):
                sp.wait_ge(sem(f"rows_stored{r}"), 16 * (NT // 2 + DC))

        spill_d = scratch("spill_d", [16, P, TOK])
        acs_d = scratch("acs_d", [SH, SEQ])
        sd_d = scratch("sd_d", [2, SH, DECB])
        bc_d = scratch("bc_d", [DECB, 2 * SG * SN])
        CD_COL = {"cd_z": 0, "cd_gu": SI + CCH + SH, "cd_xbc": SI, "cd_gv": SI + CCH + SH + GW}
        SPILL = {"cd_z": (0, 0, ACT.Silu), "cd_gu": (8, 4, ACT.Gelu_apprx_tanh), "cd_gv": (12, 6, ACT.Gelu_apprx_tanh)}
        spilled = [sem("spilled0"), sem("spilled1")]
        wcd = kview(A["w_in_cd"][0])
        flat = work[:].rearrange("p a n -> p (a n)")
        wv = [flat[:, TOK * i:TOK * (i + 1)] for i in range(3)]

        def cd_src(name):
            c0 = CD_COL[name]
            return lambda i: (wcd[:, :, ds(c0 + 256 * i, P)], wcd[:, :, ds(c0 + 256 * i + P, P)])

        def sp_cd_in(sp):
            sp.wait_ge(sem("ln_lo"), DC * 3)
            sp.dma_start(work_state, A["state_conv"][0].rearrange("b j c -> (b j) c")).then_inc(sem("w_small_in"), 16)
            sp.dma_start(w_small[:], wcd[:, :, SI + CCH:SI + CCH + SH]).then_inc(sem("w_small_in"), 16)
            for r in range(2):
                with nc.allow_non_contiguous_dma(reason="16 values"):
                    sp.dma_start(dskip[SD * r:SD * (r + 1)], A["d_skip"][0].rearrange("(c r) -> r c", r=2)[r:r + 1].to_broadcast([SD, DC])
                                 ).then_inc(sem("w_small_in"), 16)
            sp.dma_start(O["conv_state_sample"][0, :, 0:CONVW - 2], A["state_conv"][0, :, 1:CONVW - 1]).then_inc(sem("stored"), 16)
            for name in ("cd_z", "cd_gu", "cd_xbc", "cd_gv"):
                sp_stream(sp, name, cd_src(name), skip=(name == "cd_z"))

        work_state = flat[0:DECB * (CONVW - 1), 0:CCH]

        def pe_cd_in(pe):
            pe_stream(pe, "cd_z", xs, split=(sem("ln_lo"), DC * 2))
            pe.wait_ge(sem("w_small_in"), 128)
            n = DECB * (CONVW - 1)
            for c in range(12):
                mm = pe.transpose(ps[:, 7, n * c:n * (c + 1)], work_state[:, P * c:P * (c + 1)], ident[0:n, 0:n])
            mm.then_inc(pe_steps, mark("convT_turned"))
            for t in range(NB):
                if t == 1:
                    pe.wait_ge(act_steps, step("convT_ready"))
                pe_logits(pe, "dt", SH, t)
            pe_logits_turn(pe, "dt", SH, acc[:, 0])
            pe_stream(pe, "cd_gu", xs)
            pe_stream(pe, "cd_xbc", xs)
            pe_token_sums(pe, "dt", SH, gate(1, SH))
            pe_stream(pe, "cd_gv", xs)
            pe_token_rows(pe, "dt", SH)

        def act_cd_in(act):

            def spill(name):
                c0, m0, func = SPILL[name]

                def evac(s, i, g):
                    act.wait_ge(spilled[s], 16 * (m0 + i + 1))
                    if name == "cd_gv":
                        act.wait_ge(sem("conv_done"), 12)
                    settle(act)
                    act.activation(blocks(acc[:, s]), ps_set[s], func).then_inc(set_free[s], 1)
                    act.wait_ge(set_free[s], g + 1)
                    act.dma_start(spill_d[ds(c0 + 2 * i + s, 1)].rearrange("a p n -> (a p) n"), acc[:, s]).then_inc(spilled[s], 16)
                act_stream(act, name, evac)
            spill("cd_z")
            act.wait_ge(pe_steps, step("convT_turned"))
            act.copy(convT[:], ps[:, 7, 0:288].rearrange("p (c b j) -> p c b j", c=12, b=DECB)).then_inc(act_steps, mark("convT_ready"))
            act.wait_ge(spilled[0], 16 * 5)
            for t in range(NB):
                act_logits(act, "dt", SH, t, acc[:, 0])
            act.wait_ge(pe_steps, step("dt_turned"))
            spill("cd_gu")
            act_softplus(act, "dt", SH)

            def conv_out(c, s):
                settle(act, 5 - s)
                act.wait_ge(sem("conv_sum"), c + 1)
                act.activation(chunk(xbc, c), acc[:, s], ACT.Silu).then_inc(sem("conv_done"), 1)

            g0 = G0["cd_xbc"]

            def body(i, first=False):
                for s in range(2):
                    g, c = g0 + i, 2 * i + s
                    split_hi(act, 1 - s, g + s)
                    act.wait_ge(tile_done, 2 * g + s + 1)
                    settle(act, s)
                    act.activation(blocks(chunk(xbc, c)), ps_set[s], ACT.Copy).then_inc(sem("raw_ready"), 1)
                    if first:
                        act.wait_ge(spilled[s], 16 * 7)
                    else:
                        act.wait_ge(sem("conv_done"), c - 1)
                    settle(act, 2 + s)
                    act.activation(blocks(acc[:, s]), ps_set[s], ACT.Identity,
                                   bias=cols[:, ds(COL["conv_b"] + c, 1)],
                                   scale=cols[:, ds(COL["conv_w"] + 36 + c, 1)]).then_inc(set_free[s], 1)
                    if not (first and s == 0):
                        conv_out(c - 1, 1 - s)
            body(0, first=True)
            loop(act, 5, lambda i: body(i + 1))
            conv_out(11, 1)
            spill("cd_gv")

        def dve_cd_in(dve):
            dve_stream(dve, "cd_z")
            dve_logits(dve, "dt", SH, 1)
            dve_stream(dve, "cd_gu")
            dve_dt(dve)
            g0 = G0["cd_xbc"]
            dve.wait_ge(act_steps, step("convT_ready"))

            def taps(s, i, g):
                c = 2 * i + s
                dve.wait_ge(sem("raw_ready"), c + 1)
                dve.wait_ge(set_free[s], g + 1)
                raw = chunk(xbc, c)
                dve.tensor_copy(tail[:, ds(c, 1)].rearrange("p a n -> p (a n)"), raw[:, SEQ - CONVW + 1:TOK]).then_inc(sem("tail_ready"), 1)
                for j in range(1, CONVW):
                    w = cols[:, ds(COL["conv_w"] + 12 * (CONVW - 1 - j) + c, 1)]
                    m = 3 * c + j
                    if j > 1:
                        dve.wait_ge(sem("tap_done"), 2 * m - 2)
                    dve.scalar_tensor_tensor(out=acc[:, s, j:SEQ], in0=raw[:, 0:SEQ - j], scalar=w, in1=acc[:, s, j:SEQ],
                                             op0=ALU.mult, op1=ALU.add).then_inc(sem("tap_done"), 1)
                    st = convT[:, ds(c, 1), :, CONVW - 1 - j].rearrange("p a b -> p (a b)")
                    dve.scalar_tensor_tensor(out=acc[:, s, SEQ:TOK], in0=st, scalar=w, in1=acc[:, s, SEQ:TOK],
                                             op0=ALU.mult, op1=ALU.add).then_inc(sem("tap_done"), 1)
                dve.wait_ge(sem("tap_done"), 6 * c + 6)
                dve.sem_inc(sem("conv_sum"), 1)
            dve_stream(dve, "cd_xbc", taps)
            dve_dt_sums(dve)
            dve_stream(dve, "cd_gv")

        dt_n = gate(0, SH)

        def dve_dt(dve):
            then = chain(dve, "dve_")
            dve.wait_ge(act_steps, step("dt_ln"))
            log1p_fix(dve, then, gate(1, SH), gate(2, SH), gate(3, SH), gate(4, SH))
            then(dve.scalar_tensor_tensor(out=dt_n, in0=dt_n, scalar=0.0, in1=gate(2, SH), op0=ALU.max, op1=ALU.add))
            dve.scalar_tensor_tensor(out=gate(1, SH), in0=dt_n, scalar=-1.0, in1=h_vec[:, 2].unsqueeze(1).to_broadcast([P, NT + 1, SH]),
                                     op0=ALU.mult, op1=ALU.mult).then_inc(dve_steps, mark("da_ready"))

        def dve_dt_sums(dve):
            then = chain(dve, "dve_")
            n = NT * SH
            dve.wait_ge(pe_steps, step("dt_sums"))
            dve.tensor_copy(gates[:, 2, 0:n].rearrange("p (h i) -> p h i", h=SH), ps[:, 6, 0:n].rearrange("p (i h) -> p h i", h=SH))
            dve.tensor_copy(ends[:], ps[:, 6, n:2 * n].rearrange("p (i h) -> p h i", h=SH))
            then(dve.tensor_copy(acs_n[:], ps[:, 6, 0:n].rearrange("p (i h) -> p i h", h=SH)))
            dve.tensor_tensor(dec_end[:], ends[:].rearrange("p h i -> p i h"), acs_n[:], ALU.subtract).then_inc(dve_steps, mark("dec_diff"))

        def pe_cd_prep(pe):
            pe.wait_ge(set_free[0], G1["cd_gv"])
            pe.wait_ge(set_free[1], G1["cd_gv"])
            pe.wait_ge(sem("tail_ready"), 12)
            for c in range(12):
                mm = pe.transpose(ps[0:CONVW - 1 + DECB, 3 + c // 4, P * (c % 4):P * (c % 4 + 1)], tail[:, c], ident[:])
            mm.then_inc(pe_steps, mark("tailT_ready"))
            pe.wait_ge(sem("conv_done"), 12)
            pe.wait_ge(set_free[0], G1["cd_gv"])
            for c in range(4):
                mm = pe.transpose(ps[0:DECB, 0, P * c:P * (c + 1)], xbc[:, 8 + c, SEQ:TOK], ident[:])
            mm.then_inc(pe_steps, mark("s_bcT_ready"))
            pe.wait_ge(act_steps, step("dt_token_rows"))
            for q in range(4):
                g, i0 = q // 2, 4 * (q % 2)
                if q >= 2:
                    pe.wait_ge(sem("cb_ready"), q - 1)
                for i in range(i0, i0 + 4):
                    cols_ = slice(P * i, P * (i + 1))
                    mm = pe.matmul(ps[:, 6 + q % 2, P * (i - i0):P * (i - i0 + 1)], xbc[:, 8 + g, cols_], xbc[:, 10 + g, cols_],
                                   start=True, stop=True)
                mm.then_inc(sem("cb_products"), 1)
            pe.wait_ge(act_steps, step("s_bc_ready"))
            for i in range(NT):
                if i >= 2:
                    pe.wait_ge(sem("xdt_ready"), i - 1)
                    pe.wait_ge(sem("b_nat_ready"), i - 1)
                b = 2 * (i % 2)
                for c in range(DC):
                    pe.transpose(ps[:, b + c // 4, P * (c % 4):P * (c % 4 + 1)], xbc[:, c, P * i:P * (i + 1)], ident[:])
                for g in range(SG):
                    mm = pe.transpose(ps[:, 4 + i % 2, P * g:P * (g + 1)], xbc[:, 8 + g, P * i:P * (i + 1)], ident[:])
                mm.then_inc(sem("xT_nat"), 1)

        def act_cd_prep(act):
            act_token_rows(act, "dt", SH)
            act.dma_start(acs_d.rearrange("h (i p) -> (h i) p", p=P), token_rows).then_inc(sem("cd_rows_out"), 16)
            s_decay = gate(4, SH)[0:DECB, NT]
            act.activation(s_decay, gate(1, SH)[0:DECB, NT], ACT.Exp).then_inc(act_steps, mark("s_decay_ready"))
            act.wait_ge(act_steps, step("s_decay_ready"))
            with nc.allow_non_contiguous_dma(reason="2 * 128 values"):
                act.dma_start(sd_d[0].rearrange("h b -> b h"), dt_n[0:DECB, NT]).then_inc(sem("cd_rows_out"), 16)
                act.dma_start(sd_d[1].rearrange("h b -> b h"), s_decay).then_inc(sem("cd_rows_out"), 16)
            act.wait_ge(dve_steps, step("dec_diff"))
            act.activation(dec_end[:], dec_end[:], ACT.Exp).then_inc(sem("dec_ready"), 1)
            act.activation(dec_chunk[:], ends[:], ACT.Exp).then_inc(sem("dec_ready"), 1)
            act.wait_ge(tile_done, 2 * G1["cd_gv"])
            act.wait_ge(pe_steps, step("tailT_ready"))
            act.copy(ctail[:].rearrange("p (a n) -> p a n", a=3), ps[0:CONVW - 1 + DECB, 3:6, :]).then_inc(act_steps, mark("ctail_ready"))
            act.wait_ge(act_steps, step("ctail_ready"))
            act.dma_start(O["conv_state_prompt"][0, 0], ctail[0:CONVW - 1]).then_inc(sem("stored"), 16)
            act.dma_start(O["conv_state_sample"][0, :, CONVW - 2], ctail[CONVW - 1:]).then_inc(sem("stored"), 16)
            act.wait_ge(pe_steps, step("s_bcT_ready"))
            act.copy(bc_row[:], ps[0:DECB, 0, :]).then_inc(act_steps, mark("s_bc_ready"))
            act.wait_ge(act_steps, step("s_bc_ready"))
            act.dma_start(bc_d, bc_row[:]).then_inc(sem("cd_rows_out"), 16)
            for i in range(NT):
                act.wait_ge(sem("xT_nat"), i + 1)
                act.copy(b_nat[:, i], ps[:, 4 + i % 2, 0:2 * SN]).then_inc(sem("b_nat_ready"), 1)

        def dve_cd_prep(dve):
            for q in range(4):
                g, i0 = q // 2, 4 * (q % 2)
                dve.wait_ge(sem("cb_products"), q + 1)
                dve.tensor_tensor(cbT[:, g, i0:i0 + 4], ps[:, 6 + q % 2, :].rearrange("p (i n) -> p i n", n=P),
                                  causal[:].unsqueeze(1).to_broadcast([P, 4, P]), ALU.mult).then_inc(sem("cb_ready"), 1)
            dve.wait_ge(sem("cd_rows_stored"), 1)
            for i in range(NT):
                dve.wait_ge(sem("xT_nat"), i + 1)
                b = 2 * (i % 2)
                dve.tensor_tensor(xdt[:, i].rearrange("p (h d) -> p h d", h=SH),
                                  ps[:, b:b + 2, :].rearrange("p a (h d) -> p (a h) d", d=SD),
                                  dt_n[:, i].unsqueeze(2).to_broadcast([P, SH, SD]), ALU.mult).then_inc(sem("xdt_ready"), 1)

        def sp_cd_prep(sp):
            sp.wait_ge(sem("cd_rows_out"), 64)
            for w in range(2):
                for r in range(2):
                    sp.dma_start(sdt[SD * r:SD * (r + 1), w],
                                 sd_d[w].rearrange("(c r) b -> r c b", r=2)[r:r + 1].to_broadcast([SD, DC, DECB])).then_inc(sem("sdt_in"), 16)
            sp.wait_ge(sem("stored"), 16 * N_STORED_CD)
            sp.sem_inc(sem("cd_rows_stored"), 1)

        def pool_states(pool):
            pool.wait_ge(sem("dec_ready"), 2)
            for r in range(2):
                pool.wait_ge(spilled[r], 16 * 9)
            for i in range(NT):
                pool.wait_ge(sem("xdt_ready"), i + 1)
                if i >= 2:
                    pool.wait_ge(sem("state_products"), i - 1)
                pool.tensor_tensor(acc[:, i % 2, 0:SI].rearrange("p (h d) -> p h d", h=SH), xdt[:, i].rearrange("p (h d) -> p h d", h=SH),
                                   dec_end[:, i].unsqueeze(2).to_broadcast([P, SH, SD]), ALU.mult).then_inc(sem("weighed"), 1)

        def dve_states(dve):
            then = chain(dve, "dve_")
            dve.wait_ge(sem("dec_ready"), 2)
            for i in range(NT):
                h = hprev[:, i].rearrange("p (h d) -> p h d", h=SH)
                if i:
                    dve.wait_ge(sem("state_ready"), i)
                    then(dve.tensor_tensor(h, hprev[:, i - 1].rearrange("p (h d) -> p h d", h=SH),
                                           dec_chunk[:, :, i].unsqueeze(2).to_broadcast([P, SH, SD]), ALU.mult))
                dve.wait_ge(sem("state_products"), i + 1)
                b = 4 + 2 * (i % 2)
                src = ps[:, b:b + 2, :].rearrange("p a (h d) -> p (a h) d", d=SD)
                if i:
                    dve.tensor_tensor(h, h, src, ALU.add).then_inc(sem("state_ready"), 1)
                else:
                    dve.tensor_copy(h, src).then_inc(sem("state_ready"), 1)

        def pe_states(pe):
            pe.wait_ge(sem("b_nat_ready"), NT)
            pe.wait_ge(act_steps, step("dt_token_rows"))
            pe.wait_ge(sem("cb_ready"), 4)
            for i in range(NT):
                pe.wait_ge(sem("weighed"), i + 1)
                if i >= 2:
                    pe.wait_ge(sem("state_ready"), i - 1)
                for g in range(SG):
                    mm = pe.matmul(ps[:, 4 + 2 * (i % 2) + g, :], b_nat[:, i, SN * g:SN * (g + 1)], acc[:, i % 2, 512 * g:512 * (g + 1)],
                                   start=True, stop=True)
                mm.then_inc(sem("state_products"), 1)
            pe.wait_ge(sem("state_ready"), NT)
            pe.wait_ge(sem("xdt_ready"), NT)
            for c in range(DC):
                mm = pe.transpose(ps[:, 4 + c // 4, P * (c % 4):P * (c % 4 + 1)], hprev[:, NT - 1, P * c:P * (c + 1)], ident[:])
            mm.then_inc(pe_steps, mark("lastT_ready"))

        def act_states(act):
            act.wait_ge(pe_steps, step("lastT_ready"))
            act.wait_ge(sem("state_products"), NT)
            act.copy(work[:, 1], ps[:, 4:6, :].rearrange("p a n -> p (a n)")).then_inc(act_steps, mark("last_ready"))
            act.wait_ge(act_steps, step("last_ready"))
            act.dma_start(O["ssm_state_prompt"][0, 0].rearrange("(c r) p n -> (r p) c n", r=2),
                          work[:, 1].rearrange("p (c n) -> p c n", c=DC)).then_inc(sem("last_stored"), 16)

        m_buf = [acc[:, 0, 0:SEQ], acc[:, 1, 0:SEQ], hprev[:, NT - 1]]
        ce_buf = [xbc[:, 8, 0:SEQ], xbc[:, 9, 0:SEQ]]

        def tiled(ap):
            return ap.rearrange("p (i n) -> p i n", n=P)

        def sp_heads(sp):
            sp.wait_ge(sem("state_products"), NT)
            for h in range(SH):
                if h == 1:
                    sp.wait_ge(sem("last_stored"), 16)
                if h >= 2:
                    sp.wait_ge(sem("head_exp"), h - 1)
                    sp.wait_ge(sem("head_diff"), h - 1)
                sp.dma_start(work[:, h % 2], acs_d[h:h + 1, :].to_broadcast([P, SEQ])).then_inc(sem(f"row_loaded{h % 2}"), 16)

        def act_heads(act):
            def e(h):
                act.wait_ge(sem(f"row_loaded{h % 2}"), 16 * (FH // 2 + h // 2 + 1))
                if h >= 2:
                    act.wait_ge(sem("head_products"), h - 1)
                act.activation(ce_buf[h % 2], work[:, h % 2], ACT.Exp).then_inc(sem("head_exp"), 1)

            def seg(h):
                act.wait_ge(sem("head_diff"), h + 1)
                act.activation(m_buf[h % 3], m_buf[h % 3], ACT.Exp).then_inc(sem("head_seg"), 1)
            e(0)
            e(1)
            seg(0)
            for h in range(SH):
                if h + 1 < SH:
                    seg(h + 1)
                if h + 2 < SH:
                    e(h + 2)

        def pool_heads(pool):
            for h in range(SH):
                pool.wait_ge(sem("head_exp"), h + 1)
                pool.tensor_tensor(ce_buf[h % 2], ce_buf[h % 2], xbc[:, 10 + h // (SH // SG), 0:SEQ],
                                   ALU.mult).then_inc(sem("ce_ready"), 1)

        def dve_heads(dve):
            dve.wait_ge(sem("state_products"), NT)

            def diff(h):
                dve.wait_ge(sem(f"row_loaded{h % 2}"), 16 * (FH // 2 + h // 2 + 1))
                if h == 2:
                    dve.wait_ge(pe_steps, step("lastT_ready"))
                if h >= 3:
                    dve.wait_ge(sem("head_products"), h - 2)
                for i in range(NT):
                    b = slice(P * i, P * (i + 1))
                    ins = dve.tensor_scalar(m_buf[h % 3][:, b], work[:, h % 2, b], acs_n[:, i, h:h + 1], 0.0,
                                            ALU.subtract, ALU.min)
                ins.then_inc(sem("head_diff"), 1)

            def y(c):
                dve.wait_ge(sem("head_products"), 2 * c + 2)
                b = 2 * (c % 4)
                dve.scalar_tensor_tensor(out=xbc[:, c, 0:SEQ], in0=xbc[:, c, 0:SEQ], scalar=dskip[:, c:c + 1],
                                         in1=ps[:, b:b + 2, :].rearrange("p a n -> p (a n)"),
                                         op0=ALU.mult, op1=ALU.add).then_inc(sem("y_ready"), 1)
            diff(0)
            for h in range(SH):
                g = h // (SH // SG)
                if h + 1 < SH:
                    diff(h + 1)
                dve.wait_ge(sem("head_seg"), h + 1)
                dve.tensor_tensor(tiled(m_buf[h % 3]), tiled(m_buf[h % 3]), cbT[:, g], ALU.mult).then_inc(sem("m_ready"), 1)
                if h % 2 and h > 1:
                    y(h // 2 - 1)
            y(SH // 2 - 1)

        def pe_heads(pe):
            for h in range(SH):
                c = h // 2
                rs = slice(SD * (h % 2), SD * (h % 2 + 1))
                if h == 4:
                    pe.wait_ge(act_steps, step("last_ready"))
                if h % 2 == 0 and c >= 4:
                    pe.wait_ge(sem("y_ready"), c - 3)
                pe.wait_ge(sem("ce_ready"), h + 1)
                pe.wait_ge(sem("m_ready"), h + 1)
                for i in range(NT):
                    out = ps[rs, 2 * (c % 4) + i // 4, P * (i % 4):P * (i % 4 + 1)]
                    cs = slice(SD * h, SD * (h + 1))
                    mm = pe.matmul(out, xdt[:, i, cs], m_buf[h % 3][:, P * i:P * (i + 1)], start=True, stop=(i == 0))
                    if i:
                        mm = pe.matmul(out, hprev[:, i - 1, cs], ce_buf[h % 2][:, P * i:P * (i + 1)], start=False, stop=True)
                mm.then_inc(sem("head_products"), 1)

        w_sp = xbc[:, 9, 0:GW].rearrange("p (g n) -> p g n", g=4)
        wmT = xbc[:, 8, 0:GW].rearrange("p (g n) -> p g n", g=4)
        b_sp = xbc[:, 8, GW:2 * GW].rearrange("p (g n) -> p g n", g=4)
        first_w = xbc[:, 9, GW:GW + 4]
        first_b = xbc[:, 9, GW + 4:GW + 8]
        s_tmp = xbc[:, 9, GW + 8:GW + 40].rearrange("p (g b) -> p g b", g=4)
        v_row = xbc[0:DECB, 10, 0:GW]
        bcb = flat.rearrange("p (b n) -> p b n", b=DECB)
        ssm_view = "b (c r) p n -> (r p) b c n"

        w_out_y = square(A["w_out_cd"][0, 0:SI])
        w_out_d = square(A["w_out_cd"][0, SI:SI + GW])

        gv_in = [sem("gv_in0"), sem("gv_in1")]

        def sp_gmlp(sp):
            sp.wait_ge(sem("head_products"), SH)
            for k in range(2):
                sp.dma_start(gv[:, 2 * k:2 * k + 2], spill_d[12 + 2 * k:14 + 2 * k].rearrange("c p n -> p c n")).then_inc(gv_in[k], 16)
            sp.dma_start(gu[:], spill_d[8:12].rearrange("c p n -> p c n")).then_inc(sem("gmlp_in"), 16)
            sp.dma_start(w_sp, A["w_spatial"][0].rearrange("g t s -> t g s")).then_inc(sem("gmlp_in"), 16)
            sp.dma_start(b_sp.rearrange("p g n -> p (g n)"), A["b_spatial"][0].rearrange("g n -> (g n)").unsqueeze(0).to_broadcast([P, GW])).then_inc(sem("gmlp_in"), 16)
            with nc.allow_non_contiguous_dma(reason="8 values"):
                sp.dma_start(first_w, A["w_spatial"][0, :, 0, 0:1].rearrange("g a -> a g").to_broadcast([P, 4])).then_inc(sem("gmlp_in"), 16)
                sp.dma_start(first_b, A["b_spatial"][0, :, 0:1].rearrange("g a -> a g").to_broadcast([P, 4])).then_inc(sem("gmlp_in"), 16)
            sp.dma_start(sst[:].rearrange("p b c n -> p (b c) n"), A["state_ssm"][0].rearrange("b (c r) p n -> (r p) (b c) n", r=2)).then_inc(sem("sst_in"), 16)
            sp.wait_ge(sem("g_shift"), 1 + 4)
            sp.dma_start(bcb, bc_d.rearrange("b n -> (b n)").unsqueeze(0).to_broadcast([P, DECB * GW])).then_inc(sem("bcb_in"), 16)
            sp_stream(sp, "cd_out_d", w_out_d, nk=4, skip=1)
            load_pair(sp, G0["cd_out_y"], *w_out_y(0))
            sp.wait_ge(sem("sst_done"), DECB)
            sp.dma_start(O["ssm_state_sample"][0].rearrange("b (c r) p n -> (r p) (b c) n", r=2), sst[:].rearrange("p b c n -> p (b c) n")).then_inc(sem("sst_stored"), 16)
            for c in range(DC):
                sp.wait_ge(sem("sst_done"), DECB)
                if c >= 2:
                    sp.wait_ge(sem("y_gated"), c - 1)
                sp.dma_start(acc[:, c % 2], spill_d[c]).then_inc(sem(f"row_loaded{c % 2}"), 16)

        def pe_gmlp(pe):
            pe.wait_ge(sem("y_ready"), DC)
            for k in range(4):
                pe.wait_ge(gv_in[k // 2], 16)
                for t in range(NB):
                    pe.matmul(ps_set[0][:, t], ones[:], gv[:, k, TB * t:TB * (t + 1)], start=(k == 0), stop=(k == 3))
            for k in range(4):
                pe.wait_ge(sem("gv_sq"), k + 1)
                for t in range(NB):
                    mm = pe.matmul(ps_set[1][:, t], ones[:], acc[:, k % 2, TB * t:TB * (t + 1)], start=(k == 0), stop=(k == 3))
                mm.then_inc(sem("g_sq_used"), 1)
            pe.wait_ge(sem("gmlp_in"), 80)
            for g in range(4):
                mm = pe.transpose(ps[:, 6, P * g:P * (g + 1)], w_sp[:, g], ident[:])
            mm.then_inc(pe_steps, mark("wmT_turned"))
            pe.wait_ge(sem("v_ready"), 4)
            pe.wait_ge(dve_steps, step("wmT_ready"))
            for c in range(4):
                mm = pe.transpose(ps[0:DECB, 7, P * c:P * (c + 1)], gv[:, c, SEQ:TOK], ident[:])
            mm.then_inc(pe_steps, mark("v_rowT"))

            def turn(i):
                if i >= 2:
                    pe.wait_ge(sem("v_nat"), i - 1)
                for c in range(4):
                    mm = pe.transpose(ps[:, i % 2, P * c:P * (c + 1)], gv[:, c, P * i:P * (i + 1)], ident[:])
                mm.then_inc(sem("v_turned"), 1)
            turn(0)
            for i in range(NT):
                if i + 1 < NT:
                    turn(i + 1)
                pe.wait_ge(sem("v_nat"), i + 1)
                if i >= 2:
                    pe.wait_ge(sem("sg_used"), i - 1)
                for g in range(4):
                    mm = pe.matmul(ps[:, 4 + i % 2, P * g:P * (g + 1)], acc[:, i % 2, P * g:P * (g + 1)], wmT[:, g], start=True, stop=True)
                mm.then_inc(sem("sg_ready"), 1)

        def act_gmlp(act):
            act.wait_ge(sem("m_ready"), SH)
            act.wait_ge(sem("head_products"), SH)
            for k in range(4):
                act.wait_ge(gv_in[k // 2], 16)
                if k >= 2:
                    act.wait_ge(sem("g_sq_used"), k - 1)
                act.activation(acc[:, k % 2], gv[:, k], ACT.Square).then_inc(sem("gv_sq"), 1)
            act.wait_ge(sem("g_sq_used"), 4)
            act.activation(blocks(wv[0]), ps_set[0], ACT.Square, scale=1.0 / GW).then_inc(act_steps, mark("g_mean_sq"))
            act.wait_ge(dve_steps, step("g_var"))
            act.activation(wv[1], wv[1], ACT.Sqrt, bias=eps[:, 0:1]).then_inc(act_steps, mark("g_std"))
            for k in range(4):
                act.wait_ge(sem("g_shift"), 1 + k + 1)
                act.activation(gv[:, k], gv[:, k], ACT.Identity, bias=col("gmlp_ln_b", k), scale=col("gmlp_ln_g", k)).then_inc(sem("v_ready"), 1)
            act.wait_ge(pe_steps, step("v_rowT"))
            act.copy(v_row, ps[0:DECB, 7, :]).then_inc(act_steps, mark("v_row_ready"))
            act.wait_ge(act_steps, step("v_row_ready"))
            act.dma_start(O["gmlp_v_sample"][0, :, 0, :], v_row).then_inc(sem("v_row_stored"), 16)
            for i in range(NT):
                act.wait_ge(sem("v_turned"), i + 1)
                if i >= 2:
                    act.wait_ge(sem("sg_ready"), i - 1)
                act.copy(acc[:, i % 2, 0:GW], ps[:, i % 2, :]).then_inc(sem("v_nat"), 1)

        def dve_gmlp(dve):
            then = chain(dve, "dve_")
            dve.wait_ge(act_steps, step("g_mean_sq"))
            dve.scalar_tensor_tensor(out=blocks(wv[1]), in0=ps_set[1], scalar=1.0 / GW, in1=blocks(wv[0]),
                                     op0=ALU.mult, op1=ALU.subtract).then_inc(dve_steps, mark("g_var"))
            dve.wait_ge(act_steps, step("g_std"))
            then(dve.reciprocal(wv[1], wv[1]))
            dve.scalar_tensor_tensor(out=blocks(wv[2]), in0=ps_set[0], scalar=-1.0 / GW, in1=blocks(wv[1]),
                                     op0=ALU.mult, op1=ALU.mult).then_inc(sem("g_shift"), 1)
            for k in range(4):
                then(dve.tensor_tensor(gv[:, k], gv[:, k], wv[1], ALU.mult))
                dve.wait_ge(sem("g_shift"), 1 + k)
                dve.tensor_tensor(gv[:, k], gv[:, k], wv[2], ALU.add).then_inc(sem("g_shift"), 1)
            dve.wait_ge(pe_steps, step("wmT_turned"))
            dve.tensor_tensor(wmT, ps[:, 6, :].rearrange("p (g n) -> p g n", g=4),
                              causal[:].unsqueeze(1).to_broadcast([P, 4, P]), ALU.mult).then_inc(dve_steps, mark("wmT_ready"))
            dve.wait_ge(sem("v_ready"), 4)
            dve.wait_ge(sem("gmlp_in"), 80)
            then(dve.tensor_tensor(s_tmp, gv[:, :, SEQ:TOK], first_w.unsqueeze(2).to_broadcast([P, 4, DECB]), ALU.mult))
            then(dve.tensor_tensor(s_tmp, s_tmp, first_b.unsqueeze(2).to_broadcast([P, 4, DECB]), ALU.add))
            dve.tensor_tensor(gu[:, :, SEQ:TOK], gu[:, :, SEQ:TOK], s_tmp, ALU.mult).then_inc(sem("yd_ready"), 1)
            for i in range(NT):
                dve.wait_ge(sem("sg_ready"), i + 1)
                tmp = acc[:, i % 2, GW:2 * GW].rearrange("p (g n) -> p g n", g=4)
                then(dve.tensor_tensor(tmp, ps[:, 4 + i % 2, :].rearrange("p (g n) -> p g n", g=4), b_sp, ALU.add))
                dve.sem_inc(sem("sg_used"), 1)
                b = slice(P * i, P * (i + 1))
                dve.tensor_tensor(gu[:, :, b], gu[:, :, b], tmp, ALU.mult).then_inc(sem("yd_ready"), 1)

        def act_sample_state(act):
            act.wait_ge(sem("yd_ready"), NT + 1)
            for k in range(4):
                act.copy(yd_hi[:, k], gu[:, k]).then_inc(sem("yd_hi"), 1)
            act.wait_ge(sem("bcb_in"), 16)
            act.wait_ge(dve_steps, step("xdt_s"))
            act.wait_ge(sem("sg_ready"), NT)
            for b in range(DECB):
                g = G0["cd_out_d"] + b // 2
                split_hi(act, 1 - b % 2, g + b % 2)
                if b >= 2:
                    act.wait_ge(sem("sst_done"), b - 1)
                for c in range(DC):
                    ins = act.activation(acc[:, b % 2, SN * c:SN * (c + 1)], bcb[:, b, SN * (c // 4):SN * (c // 4 + 1)], ACT.Copy,
                                         scale=sdt[:, 0, c, b:b + 1])
                ins.then_inc(sem("outer_ready"), 1)

        def dve_sample_state(dve):
            then = chain(dve, "dve_")
            dve.wait_ge(sem("sdt_in"), 64)
            dve.tensor_tensor(sdt[:, 0], sdt[:, 0], xbc[:, 0:DC, SEQ:TOK], ALU.mult).then_inc(dve_steps, mark("xdt_s"))
            dve.wait_ge(sem("v_row_stored"), 16)
            for k in range(4):
                dve.wait_ge(sem("yd_hi"), k + 1)
                dve.tensor_tensor(yd_lo[:, k], gu[:, k], yd_hi[:, k].bitcast(F32), ALU.subtract).then_inc(sem("yd_lo"), 1)
            dve.wait_ge(sem("sst_in"), 16)
            residual = dve_residual(True, True)
            for b in range(DECB):
                g = G0["cd_out_d"] + b // 2
                split_lo(dve, 1 - b % 2, g + b % 2)
                if b:
                    residual(1 - b % 2, (b - 1) // 2, G0["cd_out_d"] + (b - 1) // 2)
                dve.wait_ge(sem("outer_ready"), b + 1)
                for c in range(DC):
                    ins = dve.scalar_tensor_tensor(out=sst[:, b, c], in0=sst[:, b, c], scalar=sdt[:, 1, c, b:b + 1],
                                                   in1=acc[:, b % 2, SN * c:SN * (c + 1)], op0=ALU.mult, op1=ALU.add)
                then(ins)
                for c in range(DC):
                    ins = dve.tensor_tensor_reduce(acc[:, b % 2, SN * c:SN * (c + 1)], sst[:, b, c],
                                                   bcb[:, b, SN * (2 + c // 4):SN * (3 + c // 4)], 1.0, 0.0, ALU.mult, ALU.add,
                                                   ys[:, c, b:b + 1])
                ins.then_inc(sem("sst_done"), 1)
            residual(1, DECB // 2 - 1, G0["cd_out_d"] + DECB // 2 - 1)
            dve.wait_ge(sem("sst_done"), DECB)
            y = xbc[:, 0:DC, SEQ:TOK]
            then(dve.tensor_tensor(y, y, dskip[:].unsqueeze(2).to_broadcast([P, DC, DECB]), ALU.mult))
            then(dve.tensor_tensor(y, y, ys[:], ALU.add))

        def dve_gate(dve):
            for c in range(DC):
                dve.wait_ge(sem(f"row_loaded{c % 2}"), 16 * ((FH + SH) // 2 + c // 2 + 1))
                dve.tensor_tensor(xbc[:, c], xbc[:, c], acc[:, c % 2], ALU.mult).then_inc(sem("y_gated"), 1)
            then = chain(dve, "dve_")
            dve.wait_ge(act_steps, step("rms_rstd"))
            for c in range(DC + 1):
                if c < DC:
                    dve.scalar_tensor_tensor(out=xbc[:, c], in0=xbc[:, c], scalar=col("ssm_norm_w", c), in1=wv[2],
                                             op0=ALU.mult, op1=ALU.mult).then_inc(sem("y_scaled"), 1)
                if c:
                    split_act_lo(dve, c - 1, xbc[:, c - 1], 3 * DC + c)

        def act_gate(act):
            act.wait_ge(sem("sst_done"), DECB)
            for c in range(DC):
                act.wait_ge(sem("y_gated"), c + 1)
                if c >= 2:
                    act.wait_ge(sem("rms_used"), c - 1)
                act.activation(wv[c % 2], xbc[:, c], ACT.Square).then_inc(sem("rms_sq"), 1)
            act.wait_ge(sem("rms_used"), DC)
            chain(act, "act_")(act.activation(blocks(wv[2]), ps_set[0], ACT.Ln, bias=eps[:, 0:1], scale=1.0 / SI))
            act.activation(wv[2], wv[2], ACT.Exp, scale=-0.5).then_inc(act_steps, mark("rms_rstd"))
            act.wait_ge(sem("sst_stored"), 16)
            act.wait_ge(tile_done, 2 * G1["cd_out_d"])
            for k in range(DC):
                act.wait_ge(sem("y_scaled"), k + 1)
                act.copy(xs[:, 0, k], xbc[:, k]).then_inc(sem("xs_hi"), 1)

        def pe_gate(pe):
            pe.wait_ge(set_free[0], G1["cd_out_d"])
            for c in range(DC):
                pe.wait_ge(sem("rms_sq"), c + 1)
                for t in range(NB):
                    mm = pe.matmul(ps_set[0][:, t], ones[:], wv[c % 2][:, TB * t:TB * (t + 1)], start=(c == 0), stop=(c == DC - 1))
                mm.then_inc(sem("rms_used"), 1)
            pe.wait_ge(act_steps, step("rms_rstd"))

        N_STORED_CD = 13 + 3

        block = ctx.enter_context(nc.Block())

        @block.sync
        def _(sp):
            sp_setup(sp)
            sp_ab_in(sp)
            sp_naturals(sp)
            wo = square(A["w_out_ab"][0])
            load_pair(sp, G0["ab_out"], *wo(0))
            sp_attention(sp)
            for L in range(DEPTH):
                if L == 0:
                    sp_memory(sp, 0)
                    sp_stream(sp, "ab_out", wo, skip=1)
                else:
                    load_pair(sp, G0["cd_z"], *cd_src("cd_z")(0))
                    sp_cd_in(sp)
                    load_pair(sp, G0["cd_out_d"], *w_out_d(0), nk=4)
                    sp_cd_prep(sp)
                    sp_heads(sp)
                    sp_gmlp(sp)
                    sp_memory(sp, 1)
                    sp_stream(sp, "cd_out_y", w_out_y, skip=1)
                sp_mem_weights(sp, L)
                wq = square(A["w_xq"][L])
                load_pair(sp, G0[f"xq{L}"], *wq(0))
                sp_memory_out(sp, L)
                sp_stream(sp, f"xq{L}", wq, skip=1)
                wo = square(A["w_xo"][L])
                load_pair(sp, G0[f"xo{L}"], *wo(0))
                sp_cross(sp, L)
                sp_stream(sp, f"xo{L}", wo, skip=1)
                sp_ff(sp, L)
            sp_output(sp)
            sp.wait_ge(sem("stored"), 16 * N_STORED_CD)
            sp.wait_ge(sem("mem_k_prompt_stored"), 16 * DEPTH)
            sp.wait_ge(sem("mem_v_prompt_stored"), 16 * DEPTH)

        @block.gpsimd
        def _(pool):
            pool_setup(pool)
            pool_gates(pool)
            pool_attention(pool)
            for L in range(DEPTH):
                if L == 1:
                    pool_states(pool)
                    pool_heads(pool)
                pool_sums(pool, ("ab_out", "cd_out_y")[L], 3 * L)
                pool_memory(pool, L, 3 * L)
                pool_cross(pool, L)
                pool_sums(pool, f"xo{L}", 3 * L + 1)
                pool_norm(pool, 3 * L + 1)
                pool_sums(pool, f"down{L}_2", 3 * L + 2)
                pool_norm(pool, 3 * L + 2)

        @block.tensor
        def _(pe):
            pe_setup(pe)
            pe_ab_in(pe)
            pe_naturals(pe)
            pe_pool(pe)
            pe_attention(pe)
            for L in range(DEPTH):
                if L == 0:
                    pe_stream(pe, "ab_out", xs, split=(sem("xs_lo"), DC))
                else:
                    pe_cd_in(pe)
                    pe_cd_prep(pe)
                    pe_states(pe)
                    pe_heads(pe)
                    pe_gmlp(pe)
                    pe.wait_ge(sem("v_nat"), NT)
                    pe.wait_ge(sem("yd_ready"), NT + 1)
                    pe_stream(pe, "cd_out_d", (yd_hi, yd_lo), nk=4, split=(sem("yd_lo"), 0))
                    pe_gate(pe)
                    pe_stream(pe, "cd_out_y", xs, split=(sem("xs_lo"), 3 * DC))
                pe_memory_turn(pe, L)
                pe_norm(pe, 3 * L, G1[("ab_out", "cd_out_y")[L]])
                pe_memory(pe, L, 3 * L)
                pe.wait_ge(sem("ln_lo"), DC * (3 * L + 1))
                pe_stream(pe, f"xq{L}", xs)
                pe_cross(pe, L)
                pe_stream(pe, f"xo{L}", xs, split=(sem("xs_lo"), XS_LO_MIXER[L]))
                pe_norm(pe, 3 * L + 1, G1[f"xo{L}"])
                pe_ff(pe, L)
                pe_norm(pe, 3 * L + 2, G1[f"down{L}_2"])
            pe_output(pe)

        @block.scalar
        def _(act):
            act_setup(act)
            act_ab_in(act)
            act_naturals(act)
            act.wait_ge(dve_steps, step("new_scores"))
            act.dma_start(ks_d, tiny[0:DECB, 8:8 + FH]).then_inc(sem("q_stored"), 16)
            act.wait_ge(sem("lf_stored"), 48)
            act_load_c(act, 0)
            act_load_c(act, 1)
            act_pool(act)
            act_attention(act)
            for L in range(DEPTH):
                if L == 0:
                    act_stream(act, "ab_out", act_square(0))
                else:
                    act_cd_in(act)
                    act_cd_prep(act)
                    act_states(act)
                    act_heads(act)
                    act_gmlp(act)
                    act_sample_state(act)
                    act_gate(act)
                    act_stream(act, "cd_out_y", act_square(3))
                act_memory_turn(act, L)
                act_norm_stats(act, 3 * L)
                act_memory(act, L, 3 * L)
                act_xq(act, L)
                act_cross(act, L)
                act_stream(act, f"xo{L}", act_square(3 * L + 1))
                act_norm(act, 3 * L + 1)
                act_ff(act, L)
                if L + 1 < DEPTH:
                    act_norm(act, 3 * L + 2)
            act_last_norm(act)

        @block.vector
        def _(dve):
            dve_setup(dve)
            dve_ab_in(dve)
            dve_state_sums(dve)
            dve_naturals(dve)
            dve_new_scores(dve)
            dve_pool(dve)
            dve_attention(dve)
            for L in range(DEPTH):
                if L == 0:
                    dve_stream(dve, "ab_out", dve_residual(True, True))
                else:
                    dve_cd_in(dve)
                    dve_cd_prep(dve)
                    dve_states(dve)
                    dve_heads(dve)
                    dve_gmlp(dve)
                    dve_sample_state(dve)
                    dve_gate(dve)
                    dve_stream(dve, "cd_out_y", dve_residual(False, False))
                dve_memory_turn(dve, L)
                dve_norm_stats(dve, 3 * L)
                dve_memory(dve, L, 3 * L)
                dve_stream(dve, f"xq{L}")
                dve_cross(dve, L, XS_LO_MIXER[L])
                dve_stream(dve, f"xo{L}", dve_residual(False, True))
                dve_norm(dve, 3 * L + 1)
                dve_ff(dve, L)
                if L + 1 < DEPTH:
                    dve_norm(dve, 3 * L + 2)
            dve_output(dve)


_INPUTS = ("x_prompt", "x_sample", "cache_fox_k", "cache_fox_v", "cache_fox_logf", "state_pool", "state_conv",
           "state_ssm", "cache_mem_k", "cache_mem_v", "page_table", "mem_prompt", "w_in_ab", "b_forget", "w_pool",
           "pool_scale", "w_out_ab", "w_in_cd", "conv_w", "conv_b", "dt_bias", "a_log", "d_skip", "ssm_norm_w",
           "gmlp_ln_g", "gmlp_ln_b", "w_spatial", "b_spatial", "w_out_cd", "ln_mix_g", "ln_mix_b", "w_xq", "w_xk",
           "w_xv", "w_xo", "ln_x_g", "ln_x_b", "w_gate", "w_up", "w_down", "ln_ff_g", "ln_ff_b")
_OUTPUTS = (("y_prompt", (1, SEQ, D)), ("y_sample", (DECB, 1, D)),
            ("fox_k_prompt", (1, 1, SEQ, FH, FD)), ("fox_v_prompt", (1, 1, SEQ, FH, FD)),
            ("fox_logf_prompt", (1, 1, SEQ, FH)),
            ("fox_k_sample", (1, DECB, 1, FH, FD)), ("fox_v_sample", (1, DECB, 1, FH, FD)),
            ("fox_logf_sample", (1, DECB, 1, FH)),
            ("pool_state_prompt", (1, 1, PBUF, FW)), ("pool_state_sample", (1, DECB, PBUF, FW)),
            ("conv_state_prompt", (1, 1, CONVW - 1, CCH)), ("conv_state_sample", (1, DECB, CONVW - 1, CCH)),
            ("ssm_state_prompt", (1, 1, SH, SD, SN)), ("ssm_state_sample", (1, DECB, SH, SD, SN)),
            ("gmlp_v_sample", (1, DECB, 1, GW)),
            ("mem_k_prompt", (DEPTH, 1, NMEM, MH, MD)), ("mem_v_prompt", (DEPTH, 1, NMEM, MH, MD)))


def kernel(**inputs):
    import numpy as np
    import concourse.bacc as bacc
    from concourse.bass_utils import run_bass_kernel_spmd

    nc = bacc.Bacc("TRN2", target_bir_lowering=False, num_devices=1)
    arrays, a, o = {}, {}, {}
    for name in _INPUTS:
        arrays["in_" + name] = np.ascontiguousarray(inputs[name])
        a[name] = nc.dram_tensor("in_" + name, arrays["in_" + name].shape,
                                 mybir.dt.from_np(arrays["in_" + name].dtype), kind="ExternalInput").ap()
    for name, shape in _OUTPUTS:
        o[name] = nc.dram_tensor("out_" + name, shape, F32, kind="ExternalOutput").ap()
    hybrid_step(nc, a, o)
    r = run_bass_kernel_spmd(nc, [arrays], core_ids=[0])
    return tuple(r.results[0]["out_" + name] for name, _ in _OUTPUTS)
```
